# Optimizing a Trainium2 kernel written in Bass

```python
import jax
import jax.numpy as jnp
from jax import lax
import numpy as np
import math

D_MODEL = 1024
BATCH = 1
SEQ = 512
DEPTH = 2

GRID_W = 64
CTX_LEN = 256
N_MIXERS = 2
N_ATTN_LAYERS = (DEPTH + N_MIXERS - 1) // N_MIXERS
N_RET_LAYERS = DEPTH // N_MIXERS

HEAD_DIM = 64
N_HEADS = D_MODEL // HEAD_DIM
N_KV_HEADS = N_HEADS // 4
GQA_GROUP = N_HEADS // N_KV_HEADS
WINDOW = 128
ATTN_BLOCK = 128
ATTN_PROJ = (N_HEADS + 2 * N_KV_HEADS) * HEAD_DIM

RET_HEADS = D_MODEL // 256
RET_QK_DIM = D_MODEL // RET_HEADS
RET_V_DIM = 2 * D_MODEL // RET_HEADS
RET_VWIDTH = 2 * D_MODEL
RET_CHUNK = 128
RET_PROJ = 2 * D_MODEL + 2 * RET_VWIDTH

D_FF = -(-8 * D_MODEL // (3 * 256)) * 256

ROPE_BASE = 10000.0
EPS = 1e-6
NEG_INF = -1e30


def rms_norm(x, g):
    xf = x.astype(jnp.float32)
    y = xf * lax.rsqrt(jnp.mean(xf * xf, axis=-1, keepdims=True) + EPS)
    return (y * g.astype(jnp.float32)).astype(x.dtype)

def modulate(h, shift, scale):
    return h * (1 + scale) + shift

def grid_positions(n):
    rows = n // GRID_W
    row = jnp.broadcast_to(jnp.arange(rows, dtype=jnp.int32)[:, None], (rows, GRID_W)).reshape(n)
    col = jnp.broadcast_to(jnp.arange(GRID_W, dtype=jnp.int32)[None, :], (rows, GRID_W)).reshape(n)
    return row, col

def rope_tables(n, head_dim):
    row, col = grid_positions(n)
    axis_dim = head_dim // 2
    inv = ROPE_BASE ** (-jnp.arange(0, axis_dim, 2, dtype=jnp.float32) / axis_dim)
    ang_r = row.astype(jnp.float32)[:, None] * inv
    ang_c = col.astype(jnp.float32)[:, None] * inv
    return jnp.cos(ang_r), jnp.sin(ang_r), jnp.cos(ang_c), jnp.sin(ang_c)

def rotate_axis(x, cos, sin):
    x1, x2 = jnp.split(x, 2, axis=-1)
    cos = cos[:, None, :]
    sin = sin[:, None, :]
    return jnp.concatenate([x1 * cos - x2 * sin, x1 * sin + x2 * cos], axis=-1)

def rope_2d(x, tables):
    cos_r, sin_r, cos_c, sin_c = tables
    xr, xc = jnp.split(x.astype(jnp.float32), 2, axis=-1)
    out = jnp.concatenate([rotate_axis(xr, cos_r, sin_r), rotate_axis(xc, cos_c, sin_c)], axis=-1)
    return out.astype(x.dtype)

def swiglu(h, w_in, w_out):
    gate, up = jnp.split(h @ w_in, 2, axis=-1)
    return (jax.nn.silu(gate) * up) @ w_out

def windowed_gqa_sink(h_x, h_c, w_qkv, q_gain, k_gain, sink, w_o, need_ctx_out):
    B, S, _ = h_x.shape
    L = h_c.shape[1]
    nb = S // ATTN_BLOCK
    band = ATTN_BLOCK + 2 * WINDOW
    scale = HEAD_DIM ** -0.5
    qd = N_HEADS * HEAD_DIM
    kvd = N_KV_HEADS * HEAD_DIM
    tables = rope_tables(S, HEAD_DIM)
    sink_g = sink.astype(jnp.float32).reshape(N_KV_HEADS, GQA_GROUP)[None, :, :, None, None]

    q_x, k_x, v_x = jnp.split(h_x @ w_qkv, [qd, qd + kvd], axis=-1)
    q_x = rope_2d(rms_norm(q_x.reshape(B, S, N_HEADS, HEAD_DIM), q_gain), tables)
    q_x = q_x.reshape(B, S, N_KV_HEADS, GQA_GROUP, HEAD_DIM)
    k_x = rope_2d(rms_norm(k_x.reshape(B, S, N_KV_HEADS, HEAD_DIM), k_gain), tables)
    v_x = v_x.reshape(B, S, N_KV_HEADS, HEAD_DIM)
    k_c, v_c = jnp.split(h_c @ w_qkv[:, qd:], 2, axis=-1)
    k_c = rms_norm(k_c.reshape(B, L, N_KV_HEADS, HEAD_DIM), k_gain)
    v_c = v_c.reshape(B, L, N_KV_HEADS, HEAD_DIM)

    pad = ((0, 0), (WINDOW, WINDOW), (0, 0), (0, 0))
    k_pad = jnp.pad(k_x, pad)
    v_pad = jnp.pad(v_x, pad)
    r_idx = jnp.arange(ATTN_BLOCK, dtype=jnp.int32)[:, None]
    n_idx = jnp.arange(band, dtype=jnp.int32)[None, :]
    in_window = (n_idx >= r_idx) & (n_idx - r_idx <= 2 * WINDOW)

    def block(b):
        start = b * ATTN_BLOCK
        qb = lax.dynamic_slice_in_dim(q_x, start, ATTN_BLOCK, axis=1)
        kb = lax.dynamic_slice_in_dim(k_pad, start, band, axis=1)
        vb = lax.dynamic_slice_in_dim(v_pad, start, band, axis=1)
        key_pos = start - WINDOW + n_idx
        valid = in_window & (key_pos >= 0) & (key_pos < S)
        s_ctx = jnp.einsum('bqkgd,bnkd->bkgqn', qb, k_c, preferred_element_type=jnp.float32) * scale
        s_loc = jnp.einsum('bqkgd,bnkd->bkgqn', qb, kb, preferred_element_type=jnp.float32) * scale
        s_loc = jnp.where(valid, s_loc, NEG_INF)
        sink_col = jnp.broadcast_to(sink_g, s_ctx.shape[:-1] + (1,))
        p = jax.nn.softmax(jnp.concatenate([s_ctx, s_loc, sink_col], axis=-1), axis=-1).astype(vb.dtype)
        return (jnp.einsum('bkgqn,bnkd->bqkgd', p[..., :L], v_c)
                + jnp.einsum('bkgqn,bnkd->bqkgd', p[..., L:L + band], vb))

    o_x = jnp.moveaxis(lax.map(block, jnp.arange(nb, dtype=jnp.int32)), 0, 1).reshape(B, S, qd)
    out_x = o_x @ w_o

    out_c = None
    if need_ctx_out:
        q_c = rms_norm((h_c @ w_qkv[:, :qd]).reshape(B, L, N_HEADS, HEAD_DIM), q_gain)
        q_c = q_c.reshape(B, L, N_KV_HEADS, GQA_GROUP, HEAD_DIM)
        s_c = jnp.einsum('bqkgd,bnkd->bkgqn', q_c, k_c, preferred_element_type=jnp.float32) * scale
        sink_col = jnp.broadcast_to(sink_g, s_c.shape[:-1] + (1,))
        p_c = jax.nn.softmax(jnp.concatenate([s_c, sink_col], axis=-1), axis=-1).astype(v_c.dtype)
        o_c = jnp.einsum('bkgqn,bnkd->bqkgd', p_c[..., :L], v_c)
        out_c = o_c.reshape(B, L, qd) @ w_o
    return out_c, out_x

def retention_chunked(q, k, v, log_gamma, state0):
    B, T, H, _ = q.shape
    nc = T // RET_CHUNK
    pos = jnp.arange(RET_CHUNK, dtype=jnp.float32)
    diff = pos[:, None] - pos[None, :]
    intra = jnp.where(diff >= 0, jnp.exp(log_gamma[:, None, None] * jnp.maximum(diff, 0.0)), 0.0)
    q_decay = jnp.exp(log_gamma[None, :] * (pos + 1.0)[:, None])[None, :, :, None]
    k_decay = jnp.exp(log_gamma[None, :] * (RET_CHUNK - 1.0 - pos)[:, None])[None, :, :, None]
    chunk_decay = jnp.exp(log_gamma * RET_CHUNK)[None, :, None, None]

    def to_chunks(a):
        return jnp.moveaxis(a.reshape(B, nc, RET_CHUNK, H, a.shape[-1]), 1, 0)

    def step(state, inp):
        qc, kc, vc = inp
        scores = jnp.einsum('bnhd,bmhd->bhnm', qc, kc) * intra
        inner = jnp.einsum('bhnm,bmhe->bnhe', scores, vc)
        cross = jnp.einsum('bnhd,bhde->bnhe', qc, state) * q_decay
        new_state = state * chunk_decay + jnp.einsum('bmhd,bmhe->bhde', kc * k_decay, vc)
        return new_state, inner + cross

    state, out = lax.scan(step, state0, (to_chunks(q), to_chunks(k), to_chunks(v)))
    return jnp.moveaxis(out, 0, 1).reshape(B, T, H, v.shape[-1]), state

def retention_final_state(k, v, log_gamma):
    T = k.shape[1]
    pos = jnp.arange(T, dtype=jnp.float32)
    decay = jnp.exp(log_gamma[None, :] * (T - 1.0 - pos)[:, None])[None, :, :, None]
    return jnp.einsum('bthd,bthe->bhde', k * decay, v)

def bidir_retention(h_x, h_c, w_qkvg, decay_logit, gn_gain, w_o, need_ctx_out):
    B, S, _ = h_x.shape
    L = h_c.shape[1]
    qk = RET_HEADS * RET_QK_DIM
    f32 = jnp.float32
    tables = rope_tables(S, RET_QK_DIM)
    log_g = jax.nn.log_sigmoid(decay_logit.astype(f32))
    k_scale = RET_QK_DIM ** -0.5

    q_x, k_x, v_x, g_x = jnp.split(h_x @ w_qkvg, [qk, 2 * qk, 2 * qk + RET_VWIDTH], axis=-1)
    q_x = rope_2d(q_x.reshape(B, S, RET_HEADS, RET_QK_DIM), tables).astype(f32)
    k_x = rope_2d(k_x.reshape(B, S, RET_HEADS, RET_QK_DIM), tables).astype(f32) * k_scale
    v_x = v_x.reshape(B, S, RET_HEADS, RET_V_DIM).astype(f32)
    k_c, v_c = jnp.split(h_c @ w_qkvg[:, qk:2 * qk + RET_VWIDTH], [qk], axis=-1)
    k_c = k_c.reshape(B, L, RET_HEADS, RET_QK_DIM).astype(f32) * k_scale
    v_c = v_c.reshape(B, L, RET_HEADS, RET_V_DIM).astype(f32)

    def flip(a):
        return jnp.flip(a, axis=1)

    def gated_out(o, g):
        mu = jnp.mean(o, axis=-1, keepdims=True)
        var = jnp.mean(jnp.square(o - mu), axis=-1, keepdims=True)
        y = ((o - mu) * lax.rsqrt(var + EPS)).reshape(o.shape[0], o.shape[1], RET_VWIDTH) * gn_gain.astype(f32)
        return (jax.nn.silu(g) * y.astype(g.dtype)) @ w_o

    out_c = None
    if need_ctx_out:
        q_c = (h_c @ w_qkvg[:, :qk]).reshape(B, L, RET_HEADS, RET_QK_DIM).astype(f32)
        g_c = h_c @ w_qkvg[:, 2 * qk + RET_VWIDTH:]
        zero_state = jnp.zeros((B, RET_HEADS, RET_QK_DIM, RET_V_DIM), f32)
        oc_f, state_f = retention_chunked(q_c, k_c, v_c, log_g[0], zero_state)
        oc_b, state_b = retention_chunked(flip(q_c), flip(k_c), flip(v_c), log_g[1], zero_state)
        out_c = gated_out(oc_f + flip(oc_b), g_c)
    else:
        state_f = retention_final_state(k_c, v_c, log_g[0])
        state_b = retention_final_state(flip(k_c), flip(v_c), log_g[1])

    ox_f, _ = retention_chunked(q_x, k_x, v_x, log_g[0], state_f)
    ox_b, _ = retention_chunked(flip(q_x), flip(k_x), flip(v_x), log_g[1], state_b)
    out_x = gated_out(ox_f + flip(ox_b), g_x)
    return out_c, out_x

def first_inputs(seed: int = 0) -> dict:
    key = jax.random.key(seed)
    ks = jax.random.split(key, 19)
    f32 = jnp.float32

    def nrm(k, shape, scale):
        return jax.random.normal(k, shape, f32) * scale

    gamma = 1.0 - 2.0 ** (-5.0 - np.arange(RET_HEADS))
    decay_init = jnp.asarray(np.log(gamma / (1.0 - gamma)), dtype=f32)
    return {
        'x': nrm(ks[0], (BATCH, SEQ, D_MODEL), 1.0),
        'c': nrm(ks[1], (BATCH, D_MODEL), 1.0),
        'ctx': nrm(ks[2], (BATCH, CTX_LEN, D_MODEL), 1.0),
        'c_ctx': nrm(ks[3], (D_MODEL,), 1.0),
        'ada_w': nrm(ks[4], (DEPTH, D_MODEL, 6 * D_MODEL), 0.5 * D_MODEL ** -0.5),
        'ada_b': nrm(ks[5], (DEPTH, 6 * D_MODEL), 0.02),
        'norm1_g': 1.0 + nrm(ks[6], (DEPTH, D_MODEL), 0.02),
        'norm2_g': 1.0 + nrm(ks[7], (DEPTH, D_MODEL), 0.02),
        'ffn_w_in': nrm(ks[8], (DEPTH, D_MODEL, 2 * D_FF), D_MODEL ** -0.5),
        'ffn_w_out': nrm(ks[9], (DEPTH, D_FF, D_MODEL), D_FF ** -0.5),
        'attn_w_qkv': nrm(ks[10], (N_ATTN_LAYERS, D_MODEL, ATTN_PROJ), D_MODEL ** -0.5),
        'attn_q_norm': 1.0 + nrm(ks[11], (N_ATTN_LAYERS, HEAD_DIM), 0.02),
        'attn_k_norm': 1.0 + nrm(ks[12], (N_ATTN_LAYERS, HEAD_DIM), 0.02),
        'attn_sink': nrm(ks[13], (N_ATTN_LAYERS, N_HEADS), 0.5),
        'attn_w_o': nrm(ks[14], (N_ATTN_LAYERS, N_HEADS * HEAD_DIM, D_MODEL), (N_HEADS * HEAD_DIM) ** -0.5),
        'ret_w_qkvg': nrm(ks[15], (N_RET_LAYERS, D_MODEL, RET_PROJ), D_MODEL ** -0.5),
        'ret_decay_logit': decay_init[None, None, :] + nrm(ks[16], (N_RET_LAYERS, 2, RET_HEADS), 0.01),
        'ret_gn_g': 1.0 + nrm(ks[17], (N_RET_LAYERS, RET_VWIDTH), 0.02),
        'ret_w_o': nrm(ks[18], (N_RET_LAYERS, RET_VWIDTH, D_MODEL), RET_VWIDTH ** -0.5),
    }

def first_block(x, c, ctx, c_ctx, ada_w, ada_b, norm1_g, norm2_g, ffn_w_in, ffn_w_out,
              attn_w_qkv, attn_q_norm, attn_k_norm, attn_sink, attn_w_o,
              ret_w_qkvg, ret_decay_logit, ret_gn_g, ret_w_o):
    c_act = jax.nn.silu(c)[:, None, :]
    cc_act = jax.nn.silu(c_ctx)[None, None, :]
    y_ctx = ctx
    for i in range(DEPTH):
        need_ctx_out = i < DEPTH - 1
        mx = jnp.split(c_act @ ada_w[i] + ada_b[i], 6, axis=-1)
        mc = jnp.split(cc_act @ ada_w[i] + ada_b[i], 6, axis=-1)
        h_x = modulate(rms_norm(x, norm1_g[i]), mx[0], mx[1])
        h_c = modulate(rms_norm(y_ctx, norm1_g[i]), mc[0], mc[1])
        j = i // N_MIXERS
        if i % N_MIXERS == 0:
            out_c, out_x = windowed_gqa_sink(h_x, h_c, attn_w_qkv[j], attn_q_norm[j], attn_k_norm[j],
                                             attn_sink[j], attn_w_o[j], need_ctx_out)
        else:
            out_c, out_x = bidir_retention(h_x, h_c, ret_w_qkvg[j], ret_decay_logit[j], ret_gn_g[j],
                                           ret_w_o[j], need_ctx_out)
        x = x + mx[2] * out_x
        x = x + mx[5] * swiglu(modulate(rms_norm(x, norm2_g[i]), mx[3], mx[4]), ffn_w_in[i], ffn_w_out[i])
        if need_ctx_out:
            y_ctx = y_ctx + mc[2] * out_c
            y_ctx = y_ctx + mc[5] * swiglu(modulate(rms_norm(y_ctx, norm2_g[i]), mc[3], mc[4]),
                                           ffn_w_in[i], ffn_w_out[i])
    return x


HY_WIDTH = D_MODEL // 4
HY_GROUPS = 4
ATT_WIDTH = D_MODEL // 2
ATT_HEADS = 4
ATT_HEAD_DIM = ATT_WIDTH // (2 * ATT_HEADS)
POOL_WINDOWS = (2, 4, 8, 16)
POOL_WIDTH = D_MODEL - HY_WIDTH - ATT_WIDTH
POOL_GROUP = POOL_WIDTH // len(POOL_WINDOWS)
IN_WIDTH = 3 * HY_WIDTH + 3 * ATT_WIDTH + POOL_WIDTH
ROPE_THETA = 500000.0
ROPE_DIM = ATT_HEAD_DIM // 4
Q_BLOCK = 128
HY_EMB = 33
HY_BANDS = (HY_EMB - 1) // 2
HY_FILTER_HIDDEN = 64
HY_DECAY_TARGET = 1e-2
HY_FAST_DECAY = 0.3
HY_SLOW_DECAY = 1.5
HY_SHIFT = 0.0
N_GROUPS = 4
EXPERTS_PER_GROUP = 4
N_EXPERTS = N_GROUPS * EXPERTS_PER_GROUP
TOP_K_IN_GROUP = 2
D_EXPERT = 256
PLE_DIM = 256
LN_EPS = 1e-5
RMS_EPS = 1e-5
DN_ALPHA = (2 * DEPTH) ** 0.25
DN_BETA = (8 * DEPTH) ** -0.25


def layer_norm(x, g, b):
    xf = x.astype(jnp.float32)
    mu = jnp.mean(xf, axis=-1, keepdims=True)
    var = jnp.mean(jnp.square(xf - mu), axis=-1, keepdims=True)
    y = (xf - mu) * lax.rsqrt(var + LN_EPS) * g.astype(jnp.float32) + b.astype(jnp.float32)
    return y.astype(x.dtype)

def rms_norm_2(x, g):
    xf = x.astype(jnp.float32)
    y = xf * lax.rsqrt(jnp.mean(jnp.square(xf), axis=-1, keepdims=True) + RMS_EPS) * g.astype(jnp.float32)
    return y.astype(x.dtype)

def rope_tables_2(seq_len):
    pos = jnp.arange(seq_len, dtype=jnp.float32)
    inv_freq = jnp.power(ROPE_THETA, -jnp.arange(0, ROPE_DIM, 2, dtype=jnp.float32) / ROPE_DIM)
    ang = pos[:, None] * inv_freq[None, :]
    ang = jnp.concatenate([ang, ang], axis=-1)
    return jnp.cos(ang), jnp.sin(ang)

def apply_partial_rope(x, cos, sin):
    xf = x.astype(jnp.float32)
    xr, xp = xf[..., :ROPE_DIM], xf[..., ROPE_DIM:]
    half = ROPE_DIM // 2
    rot = jnp.concatenate([-xr[..., half:], xr[..., :half]], axis=-1)
    c = cos[None, :, None, None, :]
    s = sin[None, :, None, None, :]
    return jnp.concatenate([xr * c + rot * s, xp], axis=-1).astype(x.dtype)

def short_conv_centred(u, w, b):
    up = jnp.pad(u, ((0, 0), (1, 1), (0, 0)))
    return up[:, :-2] * w[0] + up[:, 1:-1] * w[1] + up[:, 2:] * w[2] + b

def hyena_filters(seq_len, fw1, fb1, freq1, fw2, fb2, freq2, fw3):
    f32 = jnp.float32
    t = jnp.linspace(0.0, 1.0, seq_len, dtype=f32)[:, None]
    wpos = 2.0 * math.pi * jnp.arange(seq_len, dtype=f32)[:, None] / seq_len
    bands = jnp.linspace(1e-4, HY_BANDS - 1, HY_BANDS, dtype=f32)[None, :]
    z = jnp.concatenate([t, jnp.cos(wpos * bands), -jnp.sin(wpos * bands)], axis=-1)
    hdn = jnp.sin(freq1.astype(f32) * (z @ fw1.astype(f32) + fb1.astype(f32)))
    hdn = jnp.sin(freq2.astype(f32) * (hdn @ fw2.astype(f32) + fb2.astype(f32)))
    filt = hdn @ fw3.astype(f32)
    max_decay = math.log(HY_DECAY_TARGET) / HY_FAST_DECAY
    min_decay = math.log(HY_DECAY_TARGET) / HY_SLOW_DECAY
    deltas = jnp.linspace(min_decay, max_decay, HY_WIDTH, dtype=f32)[None, :]
    window = jnp.exp(-t * jnp.abs(deltas)) + HY_SHIFT
    h_fwd = filt[:, :HY_WIDTH] * window
    h_bwd = filt[:, HY_WIDTH:] * window
    k = jnp.concatenate([h_fwd, jnp.zeros((1, HY_WIDTH), f32), h_bwd[:0:-1]], axis=0)
    return k * lax.rsqrt(jnp.sum(jnp.square(k), axis=0, keepdims=True) + 1e-6)

def hyena_mixer(u, conv_w, conv_b, fw1, fb1, freq1, fw2, fb2, freq2, fw3, bias_d):
    B, L, _ = u.shape
    uc = short_conv_centred(u, conv_w, conv_b)
    x0, x1, v = jnp.split(uc, 3, axis=-1)
    v = (v * x1).astype(jnp.float32)
    k = hyena_filters(L, fw1, fb1, freq1, fw2, fb2, freq2, fw3)
    vf = jnp.fft.rfft(v, n=2 * L, axis=1)
    kf = jnp.fft.rfft(k, axis=0)
    y = jnp.fft.irfft(vf * kf[None], n=2 * L, axis=1)[:, :L]
    y = y + v * bias_d.astype(jnp.float32)
    return (y * x0.astype(jnp.float32)).astype(u.dtype)

def diff_attention(q, k, v, lq1, lk1, lq2, lk2, subln_g, lam_init, cos, sin):
    B, S, _ = q.shape
    q = q.reshape(B, S, ATT_HEADS, 2, ATT_HEAD_DIM)
    k = k.reshape(B, S, ATT_HEADS, 2, ATT_HEAD_DIM)
    v = v.reshape(B, S, ATT_HEADS, 2 * ATT_HEAD_DIM)
    q = apply_partial_rope(q, cos, sin) * (ATT_HEAD_DIM ** -0.5)
    k = apply_partial_rope(k, cos, sin)
    f32 = jnp.float32
    lam = (jnp.exp(jnp.sum(lq1.astype(f32) * lk1.astype(f32)))
           - jnp.exp(jnp.sum(lq2.astype(f32) * lk2.astype(f32))) + lam_init)
    nb = S // Q_BLOCK
    qb = q.reshape(B, nb, Q_BLOCK, ATT_HEADS, 2, ATT_HEAD_DIM).transpose(1, 0, 2, 3, 4, 5)

    def one_block(qblk):
        s = jnp.einsum('bqhcd,bkhcd->bhcqk', qblk, k, preferred_element_type=f32)
        pr = jax.nn.softmax(s, axis=-1)
        a = pr[:, :, 0] - lam * pr[:, :, 1]
        return jnp.einsum('bhqk,bkhe->bqhe', a.astype(v.dtype), v)

    o = lax.map(one_block, qb)
    o = o.transpose(1, 0, 2, 3, 4).reshape(B, S, ATT_HEADS, 2 * ATT_HEAD_DIM)
    o = rms_norm_2(o, subln_g) * (1.0 - lam_init)
    return o.reshape(B, S, ATT_HEADS * 2 * ATT_HEAD_DIM)

def pool_mixer(u, w, b, scale):
    B, S, _ = u.shape
    G = len(POOL_WINDOWS)
    f32 = jnp.float32
    uf = u.astype(f32).reshape(B, S, G, POOL_GROUP)
    csum = jnp.concatenate([jnp.zeros((B, 1, G, POOL_GROUP), f32), jnp.cumsum(uf, axis=1)], axis=1)
    pos = jnp.arange(S)
    pooled = []
    for g, win in enumerate(POOL_WINDOWS):
        lo = jnp.clip(pos - win // 2, 0, S - 1)
        hi = jnp.clip(pos + win // 2 - 1, 0, S - 1)
        cg = csum[:, :, g]
        cnt = (hi - lo + 1).astype(f32)[None, :, None]
        pooled.append((cg[:, hi + 1] - cg[:, lo]) / cnt)
    y = jnp.stack(pooled, axis=2) - uf
    y = jnp.einsum('bsgc,gcd->bsgd', y, w.astype(f32)) + b.astype(f32)
    return (y.reshape(B, S, POOL_WIDTH) * scale.astype(f32)).astype(u.dtype)

def hier_moe(h, wgc, bgc, wgf, bgf, w1, w3, w2):
    B, S, D = h.shape
    f32 = jnp.float32
    t = h.reshape(B * S, D)
    T = t.shape[0]
    pg = jax.nn.softmax(jnp.dot(t, wgc, preferred_element_type=f32) + bgc.astype(f32), axis=-1)
    gw, gi = lax.top_k(pg, 1)
    fl = (jnp.dot(t, wgf, preferred_element_type=f32) + bgf.astype(f32)).reshape(T, N_GROUPS, EXPERTS_PER_GROUP)
    idx = jnp.broadcast_to(gi[:, :, None], (T, 1, EXPERTS_PER_GROUP))
    fs = jnp.take_along_axis(fl, idx, axis=1)[:, 0]
    tv, ti = lax.top_k(jax.nn.softmax(fs, axis=-1), TOP_K_IN_GROUP)
    tv = tv / jnp.sum(tv, axis=-1, keepdims=True)
    eid = gi * EXPERTS_PER_GROUP + ti
    wts = gw * tv
    gates = jnp.sum(jax.nn.one_hot(eid, N_EXPERTS, dtype=f32) * wts[..., None], axis=1)
    a = jnp.einsum('td,edf->tef', t, w1)
    c = jnp.einsum('td,edf->tef', t, w3)
    act = jax.nn.silu(a) * c * gates[:, :, None].astype(t.dtype)
    y = jnp.einsum('tef,efd->td', act, w2)
    return y.reshape(B, S, D)

def second_inputs(seed: int = 0) -> dict:
    key = jax.random.key(seed)
    ks = iter(jax.random.split(key, 48))
    f32 = jnp.float32

    def nrm(shape, scale):
        return scale * jax.random.normal(next(ks), shape, f32)

    def gain(shape):
        return 1.0 + 0.05 * jax.random.normal(next(ks), shape, f32)

    L = DEPTH
    return {
        'x': nrm((BATCH, SEQ, D_MODEL), 1.0),
        'p': nrm((DEPTH, BATCH, SEQ, PLE_DIM), 1.0),
        'ln0_g': gain((D_MODEL,)),
        'ln0_b': nrm((D_MODEL,), 0.02),
        'w_in': nrm((L, D_MODEL, IN_WIDTH), D_MODEL ** -0.5),
        'hy_conv_w': nrm((L, 3, 3 * HY_WIDTH), 3 ** -0.5),
        'hy_conv_b': nrm((L, 3 * HY_WIDTH), 0.02),
        'hy_fw1': nrm((L, HY_EMB, HY_FILTER_HIDDEN), HY_EMB ** -0.5),
        'hy_fb1': nrm((L, HY_FILTER_HIDDEN), 0.02),
        'hy_freq1': gain((L, HY_FILTER_HIDDEN)),
        'hy_fw2': nrm((L, HY_FILTER_HIDDEN, HY_FILTER_HIDDEN), HY_FILTER_HIDDEN ** -0.5),
        'hy_fb2': nrm((L, HY_FILTER_HIDDEN), 0.02),
        'hy_freq2': gain((L, HY_FILTER_HIDDEN)),
        'hy_fw3': nrm((L, HY_FILTER_HIDDEN, 2 * HY_WIDTH), HY_FILTER_HIDDEN ** -0.5),
        'hy_bias': nrm((L, HY_WIDTH), 1.0),
        'att_lq1': nrm((L, ATT_HEAD_DIM), 0.1),
        'att_lk1': nrm((L, ATT_HEAD_DIM), 0.1),
        'att_lq2': nrm((L, ATT_HEAD_DIM), 0.1),
        'att_lk2': nrm((L, ATT_HEAD_DIM), 0.1),
        'att_subln_g': gain((L, 2 * ATT_HEAD_DIM)),
        'pool_w': nrm((L, len(POOL_WINDOWS), POOL_GROUP, POOL_GROUP), POOL_GROUP ** -0.5),
        'pool_b': nrm((L, len(POOL_WINDOWS), POOL_GROUP), 0.02),
        'pool_scale': gain((L, POOL_WIDTH)),
        'w_out': nrm((L, D_MODEL, D_MODEL), DN_BETA * D_MODEL ** -0.5),
        'ln1_g': gain((L, D_MODEL)),
        'ln1_b': nrm((L, D_MODEL), 0.02),
        'moe_wgc': nrm((L, D_MODEL, N_GROUPS), D_MODEL ** -0.5),
        'moe_bgc': nrm((L, N_GROUPS), 0.01),
        'moe_wgf': nrm((L, D_MODEL, N_EXPERTS), D_MODEL ** -0.5),
        'moe_bgf': nrm((L, N_EXPERTS), 0.01),
        'moe_w1': nrm((L, N_EXPERTS, D_MODEL, D_EXPERT), D_MODEL ** -0.5),
        'moe_w3': nrm((L, N_EXPERTS, D_MODEL, D_EXPERT), D_MODEL ** -0.5),
        'moe_w2': nrm((L, N_EXPERTS, D_EXPERT, D_MODEL), DN_BETA * D_EXPERT ** -0.5),
        'ple_wg': nrm((L, D_MODEL, D_MODEL), D_MODEL ** -0.5),
        'ple_bg': nrm((L, D_MODEL), 0.02),
        'ple_wp': nrm((L, PLE_DIM, D_MODEL), DN_BETA * PLE_DIM ** -0.5),
        'ln2_g': gain((L, D_MODEL)),
        'ln2_b': nrm((L, D_MODEL), 0.02),
    }

def second_block(x, p, ln0_g, ln0_b, w_in, hy_conv_w, hy_conv_b, hy_fw1, hy_fb1, hy_freq1,
              hy_fw2, hy_fb2, hy_freq2, hy_fw3, hy_bias, att_lq1, att_lk1, att_lq2, att_lk2,
              att_subln_g, pool_w, pool_b, pool_scale, w_out, ln1_g, ln1_b, moe_wgc, moe_bgc,
              moe_wgf, moe_bgf, moe_w1, moe_w3, moe_w2, ple_wg, ple_bg, ple_wp, ln2_g, ln2_b):
    S = x.shape[1]
    h = layer_norm(x, ln0_g, ln0_b)
    cos, sin = rope_tables_2(S)
    o_q = 3 * HY_WIDTH
    o_k = o_q + ATT_WIDTH
    o_v = o_k + ATT_WIDTH
    o_p = o_v + ATT_WIDTH
    for i in range(DEPTH):
        lam_init = 0.8 - 0.6 * math.exp(-0.3 * i)
        u = h @ w_in[i]
        y_hy = hyena_mixer(u[..., :o_q], hy_conv_w[i], hy_conv_b[i], hy_fw1[i], hy_fb1[i],
                           hy_freq1[i], hy_fw2[i], hy_fb2[i], hy_freq2[i], hy_fw3[i], hy_bias[i])
        y_att = diff_attention(u[..., o_q:o_k], u[..., o_k:o_v], u[..., o_v:o_p],
                               att_lq1[i], att_lk1[i], att_lq2[i], att_lk2[i], att_subln_g[i],
                               lam_init, cos, sin)
        y_pool = pool_mixer(u[..., o_p:], pool_w[i], pool_b[i], pool_scale[i])
        mix = jnp.concatenate([y_hy, y_att, y_pool], axis=-1) @ w_out[i]
        h = layer_norm(DN_ALPHA * h + mix, ln1_g[i], ln1_b[i])
        y_moe = hier_moe(h, moe_wgc[i], moe_bgc[i], moe_wgf[i], moe_bgf[i],
                         moe_w1[i], moe_w3[i], moe_w2[i])
        y_ple = jax.nn.sigmoid(h @ ple_wg[i] + ple_bg[i]) * (p[i] @ ple_wp[i])
        h = layer_norm(DN_ALPHA * h + y_moe + y_ple, ln2_g[i], ln2_b[i])
    return h


def setup_inputs(seed=0):
    out = dict(first_inputs(seed))
    for name, value in second_inputs(seed + 1).items():
        if name != "x":
            out[name + "_2"] = value
    return out


def reference(
    x, c, ctx, c_ctx, ada_w, ada_b, norm1_g, norm2_g, ffn_w_in, ffn_w_out, attn_w_qkv,
    attn_q_norm, attn_k_norm, attn_sink, attn_w_o, ret_w_qkvg, ret_decay_logit, ret_gn_g,
    ret_w_o, p_2, ln0_g_2, ln0_b_2, w_in_2, hy_conv_w_2, hy_conv_b_2, hy_fw1_2, hy_fb1_2,
    hy_freq1_2, hy_fw2_2, hy_fb2_2, hy_freq2_2, hy_fw3_2, hy_bias_2, att_lq1_2, att_lk1_2,
    att_lq2_2, att_lk2_2, att_subln_g_2, pool_w_2, pool_b_2, pool_scale_2, w_out_2, ln1_g_2,
    ln1_b_2, moe_wgc_2, moe_bgc_2, moe_wgf_2, moe_bgf_2, moe_w1_2, moe_w3_2, moe_w2_2, ple_wg_2,
    ple_bg_2, ple_wp_2, ln2_g_2, ln2_b_2,
):
    x = first_block(
        x, c, ctx, c_ctx, ada_w, ada_b, norm1_g, norm2_g, ffn_w_in, ffn_w_out, attn_w_qkv,
        attn_q_norm, attn_k_norm, attn_sink, attn_w_o, ret_w_qkvg, ret_decay_logit, ret_gn_g,
        ret_w_o,
    )
    return second_block(
        x, p_2, ln0_g_2, ln0_b_2, w_in_2, hy_conv_w_2, hy_conv_b_2, hy_fw1_2, hy_fb1_2,
        hy_freq1_2, hy_fw2_2, hy_fb2_2, hy_freq2_2, hy_fw3_2, hy_bias_2, att_lq1_2, att_lk1_2,
        att_lq2_2, att_lk2_2, att_subln_g_2, pool_w_2, pool_b_2, pool_scale_2, w_out_2, ln1_g_2,
        ln1_b_2, moe_wgc_2, moe_bgc_2, moe_wgf_2, moe_bgf_2, moe_w1_2, moe_w3_2, moe_w2_2,
        ple_wg_2, ple_bg_2, ple_wp_2, ln2_g_2, ln2_b_2,
    )


_drawn_inputs = setup_inputs


def setup_inputs(seed=0):
    import zlib

    import numpy as np

    out = dict(_drawn_inputs(seed))
    spreads = {}
    factors = {'norm1_g': 4.291,
     'norm2_g': 4.164,
     'attn_q_norm': 8.0,
     'attn_k_norm': 8.0,
     'attn_sink': 8.0,
     'ret_gn_g': 6.874,
     'hy_conv_b_2': 3.981,
     'hy_fb1_2': 5.807,
     'hy_freq1_2': 5.002,
     'hy_fb2_2': 4.341,
     'hy_freq2_2': 5.056,
     'att_lq1_2': 8.0,
     'att_lk1_2': 4.78,
     'att_lk2_2': 9.41,
     'att_subln_g_2': 3.531,
     'pool_b_2': 7.455,
     'pool_scale_2': 3.926,
     'moe_bgc_2': 5.582,
     'moe_bgf_2': 28.236,
     'ple_bg_2': 27.55,
     'att_lq2_2': 3.278}
    for name, (base, spread) in spreads.items():
        noise = np.random.default_rng([zlib.crc32(name.encode()), seed]).standard_normal(out[name].shape)
        drawn = base * np.exp(spread * noise) if base else spread * noise
        out[name] = jnp.asarray(drawn.astype(out[name].dtype))
    for name, factor in factors.items():
        out[name] = (out[name] * factor).astype(out[name].dtype)
    return out
```

```python
import math
from contextlib import ExitStack

import numpy as np

import concourse.bass as bass
from concourse import mybir
from concourse.alu_op_type import AluOpType as ALU

F32 = mybir.dt.float32
ACT = mybir.ActivationFunctionType
AX = mybir.AxisListType
P = 128
D = 1024
S = 512
L = 256
T = S + L
DFF = 2816
NF = DFF // P
UB = 8
F32R = mybir.dt.float32r
CHUNKS = (4, 4, 4, 4, 3, 3)
ALPHA = (2 * 2) ** 0.25
MAGIC = 12582912.0
PI = 3.1415925
NX = 6144
NB = 13056
NR = 18432

PCOLS = {}
_at = 0


def _col(name, n):
    global _at
    PCOLS[name] = (_at, n)
    _at += n


_col("cc", 16)
_col("ada_b", 96)
_col("n1", 16)
_col("n2", 16)
_col("qn", 1)
_col("kn", 1)
_col("sink", 16)
_col("dl", 8)
_col("gn", 16)
_col("ln0g", 8)
_col("ln0b", 8)
_col("ln1g", 16)
_col("ln1b", 16)
_col("ln2g", 16)
_col("ln2b", 16)
_col("cw", 36)
_col("cb", 12)
_col("hb", 4)
_col("fr1", 2)
_col("fb1", 2)
_col("fr2", 2)
_col("fb2", 2)
_col("sub", 2)
_col("pb", 4)
_col("psc", 4)
_col("pleb", 16)
_col("mb", 40)
NPRM = _at


def _plan():
    plan = [("att", 20, False),
            ("ff0", 66, False), ("ret", 64, False), ("ff1", 66, False)]
    for i in range(2):
        plan += [(f"win{i}", 20, False), ("dft", 4, True), ("idft", 4, True), (f"wout{i}", 8, False),
                 (f"ple{i}", 10, False), (f"moe{i}", 96, False)]
    return plan


PLAN = _plan()


class Queue:

    def __init__(self, sem):
        self.sem, self.n, self.ops, self.seen = sem, 0, [], {}

    def wait(self, *toks):
        for t in toks:
            if t is None:
                continue
            sem, val = t
            if self.seen.get(sem.name, 0) < val:
                self.seen[sem.name] = val
                self.ops.append((None, sem, val))

    def do(self, fn, inc=True):
        if not inc:
            self.ops.append((fn, None, 0))
            return None
        self.n += 1
        self.ops.append((fn, self.sem, 1))
        return (self.sem, self.n)

    def now(self):
        return (self.sem, self.n)

    def play(self, eng):
        for fn, sem, val in self.ops:
            if fn is None:
                eng.wait_ge(sem, val)
            elif sem is None:
                fn(eng)
            else:
                fn(eng).then_inc(sem, val)


class Slots:

    def __init__(self, aps):
        self.aps, self.free, self.i, self.held = aps, [() for _ in aps], 0, set()

    def take(self, *writers):
        assert len(self.held) < len(self.aps)
        while self.i % len(self.aps) in self.held:
            self.i += 1
        i = self.i % len(self.aps)
        self.i += 1
        self.held.add(i)
        for w in writers:
            w.wait(*self.free[i])
        return i

    def ap(self, i):
        return self.aps[i]

    def give(self, i, *toks):
        self.free[i] = toks
        self.held.discard(i)


def build(nc, io, out):
    ctx = ExitStack()
    with ctx:
        def sb(name, shape, dt=F32):
            return ctx.enter_context(nc.sbuf_tensor(name, shape, dt))

        def sem(name):
            return ctx.enter_context(nc.semaphore(name))

        XF = sb("XF", [P, NX])
        RT = sb("RT", [P, NR], F32R)
        RTF = RT[:, :].bitcast(F32)
        BF = sb("BF", [P, NB])
        RAW = sb("RAW", [P, 2, UB * P])
        WH = sb("WH", [P, 3, UB * P], F32R)
        WL = sb("WL", [P, 3, UB * P], F32R)
        PRM = sb("PRM", [P, NPRM])
        IDT = sb("IDT", [P, P])
        MEAN = {n: sb(f"MEAN{n}", [P, P]) for n in (128, 512, 1024)}
        BD64 = sb("BD64", [P, P])
        SM = sb("SM", [P, 1100])
        SCR = sb("SCR", [P, 9, 512])
        PS = ctx.enter_context(nc.psum_tensor("PS", [P, 8, 512], F32))
        PSF = PS[:, :, :].rearrange("p a b -> p (a b)")
        XS = [XF[:, 0:4096].rearrange("p (k t) -> p k t", k=8), XF[:, 4096:6144].rearrange("p (k t) -> p k t", k=8)]

        class Pair:

            def __init__(self, at, tiles, n):
                def view(t, a):
                    return t[:, a:a + tiles * n].rearrange("p (k t) -> p k t", k=tiles)

                self.hi, self.lo = view(RT, at), view(RT, at + tiles * n)
                self.hf, self.lf = view(RTF, at), view(RTF, at + tiles * n)

        HS = [Pair(0, 8, S), Pair(8192, 8, L)]

        pe, act, dve, pool, sp = (Queue(sem("s_" + n)) for n in ("pe", "act", "dve", "pool", "sp"))
        sp2 = act
        engines = (pe, act, dve, pool)

        def everyone():
            return [q.now() for q in engines]

        def mm(o, w, x, start, stop, inc):
            return pe.do(lambda e: e.matmul(o, w, x, start=start, stop=stop), inc)

        def tr(o, x, n=P, inc=True):
            return pe.do(lambda e: e.transpose(o, x, IDT[0:n, 0:n]), inc)

        def fn(o, x, f, bias=0.0, scale=1.0, acc=None):
            if acc is None:
                return act.do(lambda e: e.activation(o, x, f, bias=bias, scale=scale))
            return act.do(lambda e: e.activation(o, x, f, bias=bias, scale=scale, accum_out=acc))

        def cp(q, o, x):
            if q is act:
                return fn(o, x, ACT.Copy)
            return q.do(lambda e: e.tensor_copy(o, x))

        def tt(q, o, a, b, op):
            return q.do(lambda e: e.tensor_tensor(o, a, b, op))

        def ts(q, o, a, s1, s2, o1, o2=None):
            if o2 is None:
                return q.do(lambda e: e.tensor_scalar(o, a, s1, None, o1))
            return q.do(lambda e: e.tensor_scalar(o, a, s1, s2, o1, o2))

        def stt(o, a, s, b, o1, o2):
            return dve.do(lambda e: e.scalar_tensor_tensor(o, a, s, b, o1, o2))

        def rsq(o, x, eps, t):
            act.wait(t)
            a = fn(o, x, ACT.Sqrt, bias=eps)
            dve.wait(a)
            return a, rcp(o, o)

        def rcp(o, x):
            return dve.do(lambda e: e.reciprocal(o, x))

        def rmax(o, x):
            return dve.do(lambda e: e.reduce_max(o, x, AX.X))

        def rsum(o, x):
            return dve.do(lambda e: e.reduce_sum(o, x, AX.X))

        def ms(q, o, v):
            return q.do(lambda e: e.memset(o, v))

        def dot(o, a, b, acc):
            return dve.do(lambda e: e.tensor_tensor_reduce(o, a, b, 1.0, 0.0, ALU.mult, ALU.add, acc))

        def shuf(o, x, mask):
            return dve.do(lambda e: e.stream_shuffle(o, x, mask))

        def own(q):
            q.wait(q.now())

        class Load:

            def __init__(self, name):
                self.sem, self.n = sem(name), 0

            def start(self, q, o, i):
                self.n += 16
                q.ops.append((lambda e: e.dma_start(o, i), self.sem, 16))
                return (self.sem, self.n)

        bank = Slots([PS[:, i, :] for i in range(8)])
        scr = Slots([SCR[:, i, :] for i in range(9)])

        small = [0]

        def sm(n):
            a = small[0]
            small[0] += n
            assert small[0] <= 488
            return SM[:, a:a + n]

        EPS6, EPS5, ONE = sm(1), sm(1), sm(1)

        def finish(src):
            l_out = Load("l_out")
            for k in range(8):
                t = l_out.start(act, out[:, k, :], src[:, k, 0:S])
            act.wait(t)
            block = ctx.enter_context(nc.Block())
            block.sync(lambda e: sp.play(e))
            block.scalar(lambda e: act.play(e))
            block.tensor(lambda e: pe.play(e))
            block.vector(lambda e: dve.play(e))
            block.gpsimd(lambda e: pool.play(e))

        l_prm = Load("l_prm")
        prm = None
        for o, i in ((PRM[:, :], io["prm"]), (IDT[:, :], io["ident"])):
            prm = l_prm.start(act, o, i)
        xin = Load("l_x").start(act, XF[:, :], io["xt"])
        ms(dve, EPS6, 1e-6)
        ms(dve, EPS5, 1e-5)
        ms(dve, ONE, 1.0)
        for n in MEAN:
            ms(dve, MEAN[n][:, :], 1.0 / n)
        ms(dve, BD64[:, :], 0.0)
        own(dve)
        ms(dve, BD64[0:64, 0:64], 1.0 / 64)
        ready = ms(dve, BD64[64:128, 64:128], 1.0 / 64)
        for q in engines:
            q.wait(prm, ready)

        def pc(name, a=0, n=1):
            c = PCOLS[name][0] + a
            return PRM[:, c:c + n]

        l_cst = Load("l_cst")

        def constants(name, at, after):
            src = io[name]
            act.wait(*after)
            return l_cst.start(act, BF[:, at:at + src.shape[1]], src)

        class Stream:

            def __init__(self):
                self.units = [(n, i, raw) for n, k, raw in PLAN for i in range(k)]
                self.raw = Slots([RAW[:, i, :] for i in range(2)])
                self.load = [Load(f"l_w{i}") for i in range(2)]
                self.part = Slots([(WH[:, i, :], WL[:, i, :], WH[:, i, :].bitcast(F32)) for i in range(3)])
                self.made, self.at, self.b, self.live = [], 0, UB, []
                for _ in range(2):
                    self.fetch()

            def fetch(self):
                if len(self.made) == len(self.units):
                    return
                name, i, raw = self.units[len(self.made)]
                r = self.raw.take(sp)
                src, dst = io[name][i], self.raw.aps[r]
                t = self.load[r].start(sp, dst, src)
                if raw:
                    self.made.append((None, r, (t,)))
                    return
                p = self.part.take(act, pool)
                hi, lo, hf = self.part.aps[p]
                act.wait(t)
                ta = fn(hi, dst, ACT.Copy)
                pool.wait(ta)
                tl = tt(pool, lo, dst, hf, ALU.subtract)
                self.raw.give(r, tl)
                self.made.append((p, r, (ta, tl)))

            def unit(self):
                name, i, raw = self.units[self.at]
                while len(self.made) <= self.at:
                    self.fetch()
                p, r, toks = self.made[self.at]
                pe.wait(*toks)
                self.live.append(self.at)
                self.at += 1
                if raw:
                    return self.raw.aps[r]
                return self.part.aps[p][0:2]

            def release(self, tok):
                p, r, _ = self.made[self.live.pop(0)]
                if p is None:
                    self.raw.give(r, tok)
                else:
                    self.part.give(p, tok)
                self.b = UB
                self.ahead()

            def ahead(self):
                while len(self.made) < len(self.units):
                    nxt = self.units[len(self.made)]
                    busy = len(self.made) - (self.live[0] if self.live else self.at)
                    if busy >= (2 if nxt[2] or self.units[len(self.made) - 2][2] else 3):
                        return
                    self.fetch()

            def next(self):
                if self.b == UB:
                    self.cur = self.unit()
                    self.b = 0
                a = [x[:, self.b * P:(self.b + 1) * P] for x in self.cur]
                self.b += 1
                return a

            def full(self):
                return self.b == UB

        RING = Slots([BF[:, i * 1024:i * 1024 + 1024] for i in range(12)])
        l_ring = [Load(f"l_a{i}") for i in range(12)]
        W = Stream()

        def split_mm(o, w, x, first, last, inc):
            mm(o, w[0], x[0], first, False, False)
            mm(o, w[0], x[1], False, False, False)
            return mm(o, w[1], x[0], False, last, inc)

        def project_steps(kt, parts, ready=None, banks=None):
            banks = banks or bank
            bs = [banks.take(pe) for _ in parts]
            toks = [None] * len(parts)
            for k in range(kt):
                w = W.next()
                for i in range(len(parts)):
                    if ready is not None:
                        pe.wait(*ready(k, i))
                xs = [x(k) for _, x in parts]
                os_ = [banks.ap(b)[:, 0:n] for b, (n, _) in zip(bs, parts)]
                last = k == kt - 1
                for o, x in zip(os_, xs):
                    mm(o, w[0], x[0], k == 0, False, False)
                    mm(o, w[0], x[1], False, False, False)
                for i, (o, x) in enumerate(zip(os_, xs)):
                    end = W.full() and i == len(parts) - 1
                    t = mm(o, w[1], x[0], False, last, end or last)
                    toks[i] = t
                if W.full():
                    W.release(t)
                yield None
            yield [(banks, b, t) for b, t in zip(bs, toks)]

        def project(kt, parts, ready=None, banks=None):
            for r in project_steps(kt, parts, ready, banks):
                pass
            return [(b, t) for _, b, t in r]

        XP = [(0, 0, S), (1, S, L)]

        def of(pair, k):
            return pair.hi[:, k, :], pair.lo[:, k, :]

        def hparts(parts):
            return [(n, (lambda k, j=j: of(HS[j], k))) for j, _, n in parts]

        def hready(tk, parts):
            return lambda k, i: tk[(k, parts[i][0])]

        def split(src, hi, hf, lo, need):
            act.wait(need)
            ta = fn(hi, src, ACT.Copy)
            pool.wait(ta)
            return ta, tt(pool, lo, src, hf, ALU.subtract)

        def tokens_by_weights(tl, us, b):
            j, c = (0, tl * P) if tl < 4 else (1, (tl - 4) * P)
            for k in range(8):
                w = [x.rearrange("p (k c) -> p k c", k=4)[:, k % 4, :] for x in us[k // 4]]
                t = split_mm(bank.aps[b][:, 0:256], [x[:, c:c + P] for x in of(HS[j], k)], w,
                             k == 0, k == 7, k == 7)
            return t

        class Sums:

            def __init__(self, n, square):
                self.n, self.square, self.acc, self.prev = n, square, None, None

            def flush(self):
                if self.prev is None:
                    return
                s, x, t = self.prev
                a = scr.aps[self.acc][:, 0:self.n]
                dve.wait(t, self.tok)
                self.tok = tt(dve, a, self.first if self.first is not None else a, x, ALU.add)
                self.first = None
                if s is not None:
                    scr.give(s, self.tok)
                self.prev = None

            def feed(self, x, t):
                if not self.square:
                    if self.acc is None:
                        self.acc, self.first, self.tok = scr.take(dve), x, t
                        return
                    self.prev = (None, x, t)
                    self.flush()
                    return
                s = scr.take(act, dve) if self.acc is None else scr.take(act)
                act.wait(t)
                v = scr.aps[s][:, 0:self.n]
                t = fn(v, x, ACT.Square)
                if self.acc is None:
                    self.acc, self.first, self.tok = s, None, t
                    return
                self.flush()
                self.prev = (s, v, t)

            def mean(self):
                self.flush()
                b = bank.take(pe)
                pe.wait(self.tok)
                t = mm(bank.aps[b][:, 0:self.n], MEAN[1024][:, :], scr.aps[self.acc][:, 0:self.n], True, True, True)
                scr.give(self.acc, t)
                return b, t

        sums = {}

        def gather(parts, square):
            for j, c0, n in parts:
                sums[j] = Sums(n, square)

        def root(b, t, n, eps):
            s = scr.take(act)
            a, r = rsq(scr.aps[s][:, 0:n], bank.aps[b][:, 0:n], eps, t)
            bank.give(b, a)
            return s, r

        def mean_square(over, tiles, n, eps, need):
            b = bank.take(pe)
            last = len(tiles) - 1
            for k, x in enumerate(tiles):
                s = scr.take(act)
                act.wait(need[k])
                t = fn(scr.aps[s][:, 0:n], x, ACT.Square)
                pe.wait(t)
                t = mm(bank.aps[b][:, 0:n], MEAN[over][:, :], scr.aps[s][:, 0:n], k == 0, k == last, True)
                scr.give(s, t)
            return root(b, t, n, eps)

        def apply_norm(j, n, xt, s, r, A, B, hfree):
            for q in (dve, act, pool):
                q.wait(r, *hfree)
            H = HS[j]
            tk = {}
            for k in range(8):
                dve.wait(xt[(k, j)])
                q = scr.take(dve, act)
                h = scr.aps[q][:, 0:n]
                t = stt(h, XS[j][:, k, :], A[:, k:k + 1], scr.aps[s][:, 0:n], ALU.mult, ALU.mult)
                act.wait(t)
                ta = fn(H.hi[:, k, :], h, ACT.Identity, bias=B[:, k:k + 1])
                if k % 2:
                    own(act)
                    tb = fn(h, h, ACT.Identity, bias=B[:, k:k + 1])
                    pool.wait(tb)
                    td = tt(pool, H.lo[:, k, :], h, H.hf[:, k, :], ALU.subtract)
                else:
                    dve.wait(t, ta)
                    td = stt(H.lo[:, k, :], h, B[:, k:k + 1], H.hf[:, k, :], ALU.add, ALU.subtract)
                scr.give(q, td)
                tk[(k, j)] = (ta, td)
            scr.give(s, t)
            return tk

        def rms_modulate(xt, A, B, parts, hfree):
            rs_ = [(j, n, root(*sums.pop(j).mean(), n, EPS6)) for j, c0, n in parts]
            tk = {}
            for j, n, (s, r) in rs_:
                tk.update(apply_norm(j, n, xt, s, r, A[:, 8 * j:8 * j + 8], B[:, 8 * j:8 * j + 8], hfree))
            return tk

        def layer_norm(xt, g, b, hfree):
            X = XS[0]
            bk, t = sums.pop(0).mean()
            dve.wait(t)
            ct = {}
            for k in range(8):
                dve.wait(xt[(k, 0)])
                ct[(k, 0)] = tt(dve, X[:, k, :], X[:, k, :], bank.aps[bk], ALU.subtract)
            bank.give(bk, ct[(7, 0)])
            s, r = mean_square(1024, [X[:, k, :] for k in range(8)], S, EPS5, [ct[(k, 0)] for k in range(8)])
            return apply_norm(0, S, ct, s, r, g, b, hfree)

        gather(XP, True)
        for k in range(8):
            for j in range(2):
                sums[j].feed(XS[j][:, k, :], xin)
        cact = sm(16)
        own(act)
        ct = fn(cact, pc("cc", 0, 16), ACT.Silu)
        mods = []
        for i in range(2):
            mod = sm(96).rearrange("p (j m) -> p j m", j=2)
            pe.wait(ct)
            prev = None

            def turned(c, s, t, mod=mod, i=i):
                b = bank.take(pe)
                pe.wait(t)
                for q in range(4):
                    t = tr(bank.aps[b][:, 2 * q:2 * q + 2], scr.aps[s][0:2, q * P:q * P + P], 2)
                scr.give(s, t)
                dve.wait(t)
                for j in range(2):
                    v = bank.aps[b][:, 0:8].rearrange("p (m j) -> p j m", j=2)[:, j, :]
                    t = tt(dve, mod[:, j, 4 * c:4 * c + 4], v, pc("ada_b", 48 * i + 4 * c, 4), ALU.add)
                bank.give(b, t)

            for c in range(12):
                b = bank.take(pe)
                for q in range(4):
                    r = RING.take(sp)
                    tu = l_ring[r].start(sp, RING.aps[r], io[f"ada{i}"][4 * c + q])
                    pe.wait(tu)
                    u = RING.aps[r].rearrange("p (k c) -> p k c", k=2)
                    for z in range(2):
                        k = 2 * q + z
                        t = mm(bank.aps[b][0:2, :], cact[:, 2 * k:2 * k + 2], u[:, z, :], k == 0, k == 7, z == 1)
                    RING.give(r, t)
                s = scr.take(act)
                act.wait(t)
                t = cp(act, scr.aps[s][0:2, :], bank.aps[b][0:2, :])
                bank.give(b, t)
                if prev:
                    turned(*prev)
                prev = (c, s, t)
            turned(*prev)
            own(dve)
            AB = []
            for q, nm in ((0, "n1"), (3, "n2")):
                A, B = sm(16), sm(16)
                for j in range(2):
                    stt(A[:, 8 * j:8 * j + 8], mod[:, j, 8 * (q + 1):8 * (q + 2)], 1.0, pc(nm, 8 * i, 8),
                        ALU.add, ALU.mult)
                    t = cp(dve, B[:, 8 * j:8 * j + 8], mod[:, j, 8 * q:8 * q + 8])
                AB.append((A, B))
            for q in engines:
                q.wait(t)
            mods.append((mod, AB))

        def residual(xt, mod, s, parts, res, k):
            for (j, c0, n), (b, t) in zip(parts, res):
                dve.wait(t, xt[(k, j)])
                x = XS[j][:, k, :]
                t = stt(x, bank.aps[b][:, 0:n], mod[:, j, 8 * s + k:8 * s + k + 1], x, ALU.mult, ALU.add)
                bank.give(b, t)
                xt[(k, j)] = t
                if j in sums:
                    sums[j].feed(x, t)

        def swiglu(i, xt, mod, AB, parts, hfree):
            hk = rms_modulate(xt, AB[1][0], AB[1][1], parts, hfree)
            A = [Pair(12288, 4, S), Pair(16384, 4, L)]
            afree = [pe.now()]
            for c, nf in enumerate(CHUNKS):
                ft = {}
                for f in range(nf):
                    gate = project(8, hparts(parts), hready(hk, parts))
                    up = project(8, hparts(parts))
                    for (j, c0, n), (bg, tg), (bu, tu) in zip(parts, gate, up):
                        s = scr.take(act)
                        act.wait(tg)
                        a = fn(scr.aps[s][:, 0:n], bank.aps[bg][:, 0:n], ACT.Silu)
                        bank.give(bg, a)
                        dve.wait(a, tu)
                        v = scr.aps[s][:, 0:n]
                        t = tt(dve, v, bank.aps[bu][:, 0:n], v, ALU.mult)
                        bank.give(bu, t)
                        act.wait(*afree)
                        pool.wait(*afree)
                        ft[(f, j)] = split(v, A[j].hi[:, f, :], A[j].hf[:, f, :], A[j].lo[:, f, :], t)
                        scr.give(s, ft[(f, j)][1])
                if c == len(CHUNKS) - 1:
                    hf = [pe.now()]
                    gather(parts, i == 0)
                for m in range(8):
                    r = project(nf, [(n, (lambda f, j=j: of(A[j], f))) for j, _, n in parts],
                                lambda f, i_: ft[(f, parts[i_][0])])
                    residual(xt, mod, 5, parts, r, m)
                afree = [pe.now()]
            return hf

        xt = {(k, j): None for k in range(8) for j in range(2)}

        mod, AB = mods[0]
        tok = constants("c_l0", 0, everyone())
        hk = rms_modulate(xt, AB[0][0], AB[0][1], XP, ())
        for q in engines:
            q.wait(tok)
        CS = BF[:, 0:1280]
        COS, SIN = CS[:, 0:512], CS[:, 512:1024]
        MSK = CS[:, 1024:1280].rearrange("p (a b) -> p a b", a=2)
        kD = BF[:, 1280:4352].rearrange("p (a t) -> p a t", a=4)
        vD = BF[:, 4352:5888].rearrange("p (a g d) -> p a g d", a=6, g=4)
        qT = Slots([BF[:, 5888 + 1536 * i:7424 + 1536 * i].rearrange("p (a t) -> p a t", a=2) for i in range(2)])
        PR = Slots([BF[:, 8960 + 640 * i:9600 + 640 * i] for i in range(6)])
        OP = [Pair(12288, 4, S), Pair(16384, 4, L)]
        SW16 = [(i + 16) % 32 for i in range(32)]

        nsink = sm(16)
        tns = ts(dve, nsink, pc("sink", 0, 16), -1.0, None, ALU.mult)
        own(dve)

        def head_norm(banks, b, tok, n, gain, dst, rope, fin):
            sq, q1, rr = scr.take(act), scr.take(dve), scr.take(act)
            act.wait(tok)
            dve.wait(tok)
            ps = banks.aps[b][:, 0:n]
            ta = fn(scr.aps[sq][:, 0:n], ps, ACT.Square)
            dve.wait(ta)
            td = ts(dve, scr.aps[q1][:, 0:n], ps, gain, None, ALU.mult)
            banks.give(b, ta, td)

            def later():
                b2 = banks.take(pe)
                pe.wait(ta)
                t = mm(banks.aps[b2][:, 0:n], BD64[:, :], scr.aps[sq][:, 0:n], True, True, True)
                act.wait(t)
                t2, _ = rsq(scr.aps[rr][:, 0:n], banks.aps[b2][:, 0:n], EPS6, t)
                banks.give(b2, t2)
                own(dve)
                if not rope:
                    t = tt(dve, dst, scr.aps[q1][:, 0:n], scr.aps[rr][:, 0:n], ALU.mult)
                    scr.give(sq, t)
                else:
                    tq = tt(dve, scr.aps[q1][:, 0:n], scr.aps[q1][:, 0:n], scr.aps[rr][:, 0:n], ALU.mult)
                    own(dve)
                    tsw = shuf(scr.aps[sq][:, 0:n], scr.aps[q1][:, 0:n], SW16)
                    pool.wait(tq, tsw)
                    tt(pool, scr.aps[q1][:, 0:n], scr.aps[q1][:, 0:n], COS, ALU.mult)
                    tt(pool, scr.aps[sq][:, 0:n], scr.aps[sq][:, 0:n], SIN, ALU.mult)
                    own(pool)
                    t = tt(pool, dst, scr.aps[q1][:, 0:n], scr.aps[sq][:, 0:n], ALU.add)
                    scr.give(sq, t)
                scr.give(q1, t)
                scr.give(rr, t)
                fin(t)

            return later

        later = []

        def flush():
            for f in later:
                f()
            later.clear()

        kq = {}
        for m in range(2):
            res = project(8, hparts(XP), hready(hk, XP))
            flush()
            for (j, c0, n), (b, t) in zip(XP, res):
                kr = scr.take(dve, pool)

                def fin(t, kr=kr, m=m, j=j, c0=c0, n=n):
                    act.wait(t)
                    for g in range(2):
                        for h2 in range(2):
                            tk = cp(act, kD[64 * h2:64 * h2 + 64, 2 * m + g, c0:c0 + n],
                                    scr.aps[kr][64 * g:64 * g + 64, 0:n])
                        kq[(2 * m + g, j)] = tk
                    scr.give(kr, tk)

                later.append(head_norm(bank, b, t, n, pc("kn"), scr.aps[kr][:, 0:n], j == 0, fin))
        vt = []
        us = [W.unit(), W.unit()]
        for tl in range(6):
            b = bank.take(pe)
            t = tokens_by_weights(tl, us, b)
            if tl == 0:
                flush()
            act.wait(t)
            t2 = cp(act, vD[:, tl, :, :], bank.aps[b][:, 0:256].rearrange("p (g d) -> p g d", g=4))
            vt.append(t2)
            bank.give(b, t2)
        W.release(t)
        W.release(t)
        qt, qslot = {}, {}

        def query_steps(g, banks):
            qs = qslot[g] = qT.take(dve, pool)
            for m in range(2):
                for res in project_steps(8, hparts(XP), hready(hk, XP), banks):
                    if res is None:
                        yield
                todo = []
                for (j, c0, n), (bk, b, t) in zip(XP, res):
                    def fin(t, m=m, j=j):
                        qt[(g, m, j)] = t

                    todo.append(head_norm(bk, b, t, n, pc("qn"), qT.aps[qs][:, m, c0:c0 + n], j == 0, fin))
                yield
                for f in todo:
                    f()
                    yield

        for _ in query_steps(0, bank):
            pass

        mx, nm, ss, es, rs = sm(8), sm(8), sm(8), sm(8), sm(8)
        pairs, single, outs, fbank = Slots([0, 2]), Slots([PS[:, 4, :]]), Slots([PS[:, 5, :]]), Slots(
            [PS[:, 6, :], PS[:, 7, :]])
        for i in range(2):
            pairs.give(i, *bank.free[2 * i], *bank.free[2 * i + 1])
            fbank.give(i, *bank.free[6 + i])
        single.give(0, *bank.free[4])
        outs.give(0, *bank.free[5])
        ot = {}

        def attn_scores(g, blk, hh, it):
            h = 4 * g + hh
            m, hf = h // 2, 64 * (h % 2)
            j = 0 if blk < 4 else 1
            q0 = blk * P
            lo, hi = (max(blk - 1, 0), min(blk + 2, 4)) if j == 0 else (0, 0)
            nl = (hi - lo) * P
            s = pairs.take(pe)
            o = pairs.aps[s] * 512
            pe.wait(qt[(g, hh // 2, j)], kq[(g, 0)], kq[(g, 1)])
            w = qT.aps[qslot[g]][hf:hf + 64, hh // 2, q0:q0 + P]
            t = mm(PSF[:, o + 256:o + 512], w, kD[hf:hf + 64, g, S:T], True, True, True)
            if nl:
                t = mm(PSF[:, o + 512:o + 512 + nl], w, kD[hf:hf + 64, g, lo * P:hi * P], True, True, True)
            sc = PSF[:, o + 256:o + 512 + nl]
            dve.wait(t)
            if nl == 384:
                v = PSF[:, o + 512:o + 896].rearrange("p (a b) -> p a b", a=3)[:, 0:3:2, :]
                tt(dve, v, v, MSK, ALU.add)
                own(dve)
            elif nl:
                a = 1 if lo == blk else 0
                v = PSF[:, o + 512 + a * P:o + 640 + a * P]
                tt(dve, v, v, MSK[:, a, :], ALU.add)
                own(dve)
            c = it % 8
            rmax(mx[:, c:c + 1], sc)
            own(dve)
            t = ts(dve, nm[:, c:c + 1], mx[:, c:c + 1], -0.125, nsink[:, h:h + 1], ALU.mult, ALU.min)
            p = PR.take(act)
            act.wait(t, tns)
            pp = PR.aps[p][:, 0:256 + nl]
            t1 = fn(pp, sc, ACT.Exp, bias=nm[:, c:c + 1], scale=0.125, acc=ss[:, c:c + 1])
            pairs.give(s, t1)
            t2 = fn(es[:, c:c + 1], pc("sink", h), ACT.Exp, bias=nm[:, c:c + 1])
            return p, pp, c, t2

        def attn_norm(p, pp, c, t2):
            dve.wait(t2)
            tt(dve, rs[:, c:c + 1], ss[:, c:c + 1], es[:, c:c + 1], ALU.add)
            own(dve)
            t = rcp(rs[:, c:c + 1], rs[:, c:c + 1])
            pool.wait(t)
            return p, pp, ts(pool, pp, pp, rs[:, c:c + 1], 1.0, ALU.mult, ALU.mult)

        def attn_values(g, blk, ps):
            j = 0 if blk < 4 else 1
            q0 = blk * P
            lo, hi = (max(blk - 1, 0), min(blk + 2, 4)) if j == 0 else (0, 0)
            keys = [4, 5] + list(range(lo, hi))
            ob = outs.take(pe)
            acc = outs.aps[ob][0:64, :]
            prev = None

            def pv(item, last):
                jt, s, t = item
                pe.wait(t, vt[keys[jt]])
                t = mm(acc, vD[:, keys[jt], g, :], scr.aps[s], jt == 0, last, True)
                scr.give(s, t)
                return t

            for jt in range(len(keys)):
                b = single.take(pe)
                tb = single.aps[b]
                for hh in range(4):
                    pe.wait(ps[hh][2])
                    t = tr(tb[:, hh * P:(hh + 1) * P], ps[hh][1][:, jt * P:(jt + 1) * P], inc=hh == 3 )
                e = act if jt % 2 else dve
                s = scr.take(e)
                e.wait(t)
                t2 = cp(e, scr.aps[s], tb)
                single.give(b, t2)
                if prev is not None:
                    pv(prev, False)
                prev = (jt, s, t2)
            for hh in range(4):
                PR.give(ps[hh][0], t)
            t = pv(prev, True)
            av = acc.rearrange("p (a b q) -> p a b q", a=2, b=2)
            s = scr.take(act)
            sv = scr.aps[s][:, 0:256].rearrange("p (a q) -> p a q", a=2)
            act.wait(t)
            cp(act, sv[64:128], av[:, :, 1, :])
            td = cp(act, sv[0:64], av[:, :, 0, :])
            outs.give(ob, td)
            act.wait(*ofree)
            pool.wait(*ofree)
            a, c = 2 * (g % 2), q0 - (0 if j == 0 else S)
            o = OP[j]
            tk = split(sv, o.hi[:, a:a + 2, c:c + P], o.hf[:, a:a + 2, c:c + P], o.lo[:, a:a + 2, c:c + P], td)
            scr.give(s, tk[1])
            ot[(g, blk)] = tk

        filler = []

        def fill(n):
            while n and filler:
                try:
                    next(filler[0])
                    n -= 1
                except StopIteration:
                    filler.pop(0)

        def output_half(g):
            for q in (pe,):
                for g2 in (g - 1, g):
                    for b2 in range(6):
                        q.wait(*ot[(g2, b2)])
            for m in range(8):
                for res in project_steps(4, [(n, (lambda k, j=j: of(OP[j], k))) for j, _, n in XP], None, fbank):
                    if res is None:
                        yield
                for (j, c0, n), (bk, b, t) in zip(XP, res):
                    dve.wait(t, xt[(m, j)])
                    x = XS[j][:, m, :]
                    t2 = stt(x, bk.aps[b][:, 0:n], mods[0][0][:, j, 16 + m:17 + m], x, ALU.mult, ALU.add)
                    bk.give(b, t2)
                    xt[(m, j)] = t2
                    if j in sums:
                        sums[j].feed(x, t2)
                yield

        ofree = ()
        for g in range(4):
            work = [(blk, hh) for blk in range(6) for hh in range(4)]
            if g < 3:
                filler.append(query_steps(g + 1, fbank))
            soft, groups = [], {}
            for it in range(len(work) + 3):
                if it < len(work):
                    blk, hh = work[it]
                    soft.append(attn_scores(g, blk, hh, it))
                    fill(1)
                if 1 <= it <= len(work):
                    blk, hh = work[it - 1]
                    groups.setdefault(blk, []).append(attn_norm(*soft[it - 1]))
                if it >= 2 and (it - 2) % 4 == 3:
                    blk = work[it - 2][0]
                    attn_values(g, blk, groups[blk])
            fill(10**9)
            qT.give(qslot[g], pe.now())
            if g % 2:
                if g == 3:
                    gather(XP, True)
                for _ in output_half(g):
                    pass
                ofree = (pe.now(),)
        for i in range(2):
            bank.give(2 * i, *pairs.free[i])
            bank.give(2 * i + 1, *pairs.free[i])
            bank.give(6 + i, *fbank.free[i])
        bank.give(4, *single.free[0])
        bank.give(5, *outs.free[0])
        hfree = [pe.now()]

        tok = constants("c_l1", 0, everyone())
        hfree = swiglu(0, xt, mod, AB, XP, hfree)

        mod, AB = mods[1]
        hk = rms_modulate(xt, AB[0][0], AB[0][1], XP, hfree)
        for q in engines:
            q.wait(tok)
        CS = BF[:, 0:2944]
        RC = CS[:, 0:1024].rearrange("p (a t) -> p a t", a=2)
        RS = CS[:, 1024:2048].rearrange("p (a t) -> p a t", a=2)
        DIF = CS[:, 2048:2944]
        qR = BF[:, 2944:3968].rearrange("p (a t) -> p a t", a=2)
        kR = BF[:, 3968:5504].rearrange("p (a t) -> p a t", a=2)
        vR = BF[:, 5504:8576].rearrange("p (a t) -> p a t", a=6)
        ST = BF[:, 8576:11648].rearrange("p (a t) -> p a t", a=6)
        M1 = BF[:, 11648:12544]
        CX, CY, MT = XF[:, 4096:4736], XF[:, 4736:5376], XF[:, 5376:5888]
        MT2 = BF[:, 12544:12928]
        YP = Pair(12288, 4, S)
        lg, e1, e2, e3, e4 = (sm(8) for _ in range(5))
        dl = pc("dl", 0, 8)
        ts(dve, e1, dl, -1.0, None, ALU.mult)
        own(dve)
        t = tt(dve, e1, e1, dl, ALU.min)
        act.wait(t)
        t = fn(e2, e1, ACT.Exp)
        dve.wait(t)
        ts(dve, e3, e2, 2.0, None, ALU.add)
        own(dve)
        rcp(e3, e3)
        own(dve)
        tt(dve, e2, e2, e3, ALU.mult)
        own(dve)
        tt(dve, e3, e2, e2, ALU.mult)
        own(dve)
        ms(dve, e4, 1.0 / 19)
        for n in range(17, 0, -2):
            own(dve)
            tt(dve, e4, e4, e3, ALU.mult)
            own(dve)
            ts(dve, e4, e4, 1.0 / n, None, ALU.add)
        own(dve)
        tt(dve, e4, e4, e2, ALU.mult)
        ts(dve, lg, dl, 0.0, None, ALU.min)
        own(dve)
        tlg = stt(lg, e4, -2.0, lg, ALU.mult, ALU.add)
        own(dve)
        lgL, lgS = sm(4), sm(4)
        ts(dve, lgL, lg[:, 0:4], float(L), None, ALU.mult)
        ts(dve, lgS, lg[:, 4:8], float(S), None, ALU.mult)
        nlb = sm(4)
        t = ts(dve, nlb, lg[:, 4:8], -1.0, None, ALU.mult)
        dve.wait(t)
        act.wait(t)

        yt = {}
        done = {"pv": None, "score": None, "score_d": None, "wo": None}
        for h in range(4):
            lf, lb = lg[:, h:h + 1], lg[:, 4 + h:5 + h]
            dve.wait(done["score_d"])
            pool.wait(done["score_d"])
            act.wait(done["score_d"])
            for a, n in ((0, 512), (512, 384)):
                v, w = M1[:, a:a + n], MT[:, 0:n]
                ts(dve, v, DIF[:, a:a + n], 0.0, lf, ALU.max, ALU.mult)
                ts(dve, w, DIF[:, a:a + n], 0.0, nlb[:, h:h + 1], ALU.min, ALU.mult)
                own(dve)
                t = tt(dve, v, v, w, ALU.add)
                own(dve)
            act.wait(t)
            tM1 = fn(M1, M1, ACT.Exp)
            pool.wait(tM1)
            tM1 = tt(pool, M1[:, 384:512], M1[:, 384:512], IDT[:, :], ALU.add)
            fn(CX, DIF[:, 256:896], ACT.Exp, scale=lf, bias=lgL[:, h:h + 1])
            a = fn(CY, DIF[:, 256:896], ACT.Exp, scale=nlb[:, h:h + 1], bias=lgS[:, h:h + 1])
            pool.wait(a)
            tM2 = tt(pool, CX, CX, CY, ALU.add)

            qk = {}
            for isk in range(2):
                parts = XP if isk else XP[:1]
                dst = kR if isk else qR
                for m in range(2):
                    res = project(8, hparts(parts), hready(hk, parts))
                    b, t = res[0]
                    ps = bank.aps[b]
                    s1, s2 = scr.take(dve), scr.take(dve)
                    dve.wait(t, done["score"])
                    pool.wait(done["score"])
                    tt(dve, scr.aps[s1], ps, RC[:, m, :], ALU.mult)
                    tt(dve, scr.aps[s2][0:64, :], ps[64:128, :], RS[64:128, m, :], ALU.mult)
                    t = tt(dve, scr.aps[s2][64:128, :], ps[0:64, :], RS[0:64, m, :], ALU.mult)
                    bank.give(b, t)
                    pool.wait(t)
                    t = tt(pool, dst[:, m, 0:S], scr.aps[s1], scr.aps[s2], ALU.add)
                    scr.give(s1, t)
                    scr.give(s2, t)
                    qk[(isk, m, 0)] = t
                    if isk:
                        b, t = res[1]
                        act.wait(t, done["score"])
                        t = cp(act, dst[:, m, S:T], bank.aps[b][:, 0:L])
                        bank.give(b, t)
                        qk[(isk, m, 1)] = t
            vtk = {}
            for half in range(2):
                us = [W.unit(), W.unit()]
                for tl in range(6):
                    b = bank.take(pe)
                    t = tokens_by_weights(tl, us, b)
                    act.wait(t, done["pv"])
                    vtk[(half, tl)] = cp(act, vR[:, tl, half * 256:half * 256 + 256], bank.aps[b][:, 0:256])
                    bank.give(b, vtk[(half, tl)])
                W.release(t)
                W.release(t)
            st = []
            for j in range(6):
                b = bank.take(pe)
                jj = 0 if j < 4 else 1
                for d in range(2):
                    pe.wait(qk[(0, d, 0)], qk[(1, d, jj)])
                    t = mm(bank.aps[b], kR[:, d, j * P:j * P + P], qR[:, d, :], d == 0, d == 1, d == 1)
                if j < 4:
                    dec = M1[:, 384 - P * j:896 - P * j]
                else:
                    dec = CX[:, 128 - P * (j - 4):640 - P * (j - 4)]
                dve.wait(t, tM1, tM2, done["pv"])
                t2 = stt(ST[:, j, :], bank.aps[b], 0.0625, dec, ALU.mult, ALU.mult)
                bank.give(b, t2)
                st.append(t2)
            done["score"], done["score_d"] = t, st[-1]
            os_ = []
            for e_ in range(4):
                b = bank.take(pe)
                for j in range(6):
                    pe.wait(st[j], vtk[(e_ // 2, j)])
                    t = mm(bank.aps[b], vR[:, j, e_ * P:e_ * P + P], ST[:, j, :], j == 0, j == 5, j == 5)
                done["pv"] = t
                s = scr.take(act)
                act.wait(t)
                t = cp(act, scr.aps[s], bank.aps[b])
                bank.give(b, t)
                os_.append((s, t))
            gt = []
            for m in range(2):
                gt += project(8, hparts(XP[:1]))
            om = bank.take(pe)
            for e_ in range(4):
                pe.wait(os_[e_][1])
                t = mm(bank.aps[om], MEAN[512][:, :], scr.aps[os_[e_][0]], e_ == 0, e_ == 3, e_ == 3)
            dve.wait(t)
            cts = []
            for e_ in range(4):
                dve.wait(os_[e_][1])
                o = scr.aps[os_[e_][0]]
                cts.append(tt(dve, o, o, bank.aps[om], ALU.subtract))
            bank.give(om, cts[-1])
            gt += project(8, hparts(XP[:1]))
            s, r = mean_square(512, [scr.aps[q_] for q_, _ in os_], S, EPS6, cts)
            gt += project(8, hparts(XP[:1]))
            if h == 3:
                hfree = [pe.now()]
            dve.wait(r)
            for e_ in range(4):
                o = scr.aps[os_[e_][0]]
                b, t = gt[e_]
                sg = scr.take(act)
                act.wait(t)
                ta = fn(scr.aps[sg], bank.aps[b], ACT.Silu)
                bank.give(b, ta)
                stt(o, o, pc("gn", 4 * h + e_), scr.aps[s], ALU.mult, ALU.mult)
                dve.wait(ta)
                own(dve)
                t = tt(dve, o, o, scr.aps[sg], ALU.mult)
                scr.give(sg, t)
                act.wait(done["wo"])
                pool.wait(done["wo"])
                yt[e_] = split(o, YP.hi[:, e_, :], YP.hf[:, e_, :], YP.lo[:, e_, :], t)
                scr.give(os_[e_][0], yt[e_][1])
            scr.give(s, t)
            if h == 3:
                gather(XP[:1], True)
            for m in range(8):
                r = project(4, [(S, lambda k: of(YP, k))], lambda k, i: yt[k])
                residual(xt, mod, 2, XP[:1], r, m)
            done["wo"] = pe.now()
        WG = sb("WG", [P, 2, 160], F32R)

        def second_constants(i, after):
            constants(f"c_2{i}", 0, after)
            return constants(f"c_f{i}", 6824, after)

        tok = second_constants(0, everyone())
        hfree = swiglu(1, xt, mod, AB, XP[:1], hfree)

        XO = XP[:1]
        def plus_alpha_h(m, y, b):
            x = XS[0][:, m, :]
            t = stt(x, HS[0].hf[:, m, :], ALPHA, y, ALU.mult, ALU.add)
            if b is not None:
                bank.give(b, t)
            own(dve)
            return stt(x, HS[0].lf[:, m, :], ALPHA, x, ALU.mult, ALU.add)

        hk = layer_norm(xt, pc("ln0g", 0, 8), pc("ln0b", 0, 8), hfree)
        for i in range(2):
            lam_init = 0.8 - 0.6 * math.exp(-0.3 * i)
            for q in engines:
                q.wait(tok)
            CS = BF[:, 0:2728]
            COS, SIN = CS[:, 0:512], CS[:, 512:1024]
            ICN = CS[:, 1024:2048].rearrange("p (a t) -> p a t", a=2)
            ALT = CS[:, 2048:2049]
            pw, lq, wg = CS[:, 2056:2312], CS[:, 2312:2568], CS[:, 2568:2728]
            VK = BF[:, 2728:6824].rearrange("p (a b c) -> p a b c", a=4, b=2)
            qT = BF[:, 6824:8872].rearrange("p (a t) -> p a t", a=4)
            kT = BF[:, 8872:10920].rearrange("p (a t) -> p a t", a=4)
            vv = BF[:, 10920:12968].rearrange("p (a t) -> p a t", a=4)
            WIN = BF[:, 6824:8872].rearrange("p (a t) -> p a t", a=4)
            ZT = BF[0:33, 8872:9384]
            fws = BF[0:33, 9384:9448], BF[0:64, 9448:9512]
            fw3 = BF[0:64, 9512:10024]
            uh = XF[:, 0:3096].rearrange("p (a t) -> p a t", a=6)
            YF = XF[:, 0:2048].rearrange("p (a c) -> p a c", a=8)
            x0 = XF[:, 3096:4120].rearrange("p (a t) -> p a t", a=2)
            vT = XF[:, 4120:5144].rearrange("p (a t) -> p a t", a=2)
            YP = Pair(8192, 8, S)
            yt = {}

            def put(k, s, t, YP=YP, yt=yt):
                yt[k] = split(scr.aps[s], YP.hi[:, k, :], YP.hf[:, k, :], YP.lo[:, k, :], t)
                scr.give(s, yt[k][1])

            for q in (act, pool, dve):
                q.wait(*everyone())
            twg = split(wg, WG[:, 0, :], WG[:, 0, :].bitcast(F32), WG[:, 1, :], None)
            tz = ms(pool, uh[:, :, 0:1], 0.0)
            tz = ms(pool, uh[:, :, 513:514], 0.0)
            rn = SM[:, 488:490]

            def filter_steps():
                rhs, tin, held = ZT, None, []
                for z in range(2):
                    b = bank.take(pe)
                    pe.wait(tin)
                    t = mm(bank.aps[b][0:64, :], fws[z], rhs, True, True, True)
                    for h_ in held:
                        scr.give(h_, t)
                    s1, s2 = scr.take(dve, act), scr.take(dve, act)
                    a_, k_ = scr.aps[s1][0:64, :], scr.aps[s2][0:64, :]
                    dve.wait(t)
                    fb, fr = pc(("fb1", "fb2")[z], i)[0:64, :], pc(("fr1", "fr2")[z], i)[0:64, :]
                    t = ts(dve, a_, bank.aps[b][0:64, :], fb, fr, ALU.add, ALU.mult)
                    bank.give(b, t)
                    own(dve)
                    ts(dve, k_, a_, 1.0 / (2 * math.pi), MAGIC, ALU.mult, ALU.add)
                    own(dve)
                    ts(dve, k_, k_, -MAGIC, None, ALU.add)
                    own(dve)
                    stt(a_, k_, -6.28125, a_, ALU.mult, ALU.add)
                    own(dve)
                    stt(a_, k_, -(2 * math.pi - 6.28125), a_, ALU.mult, ALU.add)
                    own(dve)
                    t = ts(dve, a_, a_, PI, -PI, ALU.min, ALU.max)
                    act.wait(t)
                    tin = fn(k_, a_, ACT.Sin)
                    scr.give(s1, tin)
                    rhs, held = k_, [s2]
                    yield
                bss = bank.take(pe)
                prev = None

                def sums(k, s2, ta):
                    pe.wait(ta)
                    for c in range(2):
                        for fb_ in range(2):
                            col = 16 * c + 4 * fb_ + k
                            t = mm(bank.aps[bss][:, col:col + 1],
                                   scr.aps[s2][:, fb_ * 256 + c * P:fb_ * 256 + c * P + P], ONE, True, True, True)
                    scr.give(s2, t)
                    return t

                for k in range(4):
                    b = bank.take(pe)
                    pe.wait(tin)
                    t = mm(bank.aps[b], rhs[:, k * P:k * P + P], fw3, True, True, True)
                    if k == 3:
                        scr.give(held[0], t)
                    if prev:
                        sums(*prev)
                    s, s2 = scr.take(dve), scr.take(act)
                    dve.wait(t)
                    t = tt(dve, scr.aps[s], bank.aps[b], WIN[:, k, :], ALU.mult)
                    bank.give(b, t)
                    act.wait(t)
                    ta = fn(scr.aps[s2], scr.aps[s], ACT.Square)
                    pool.wait(t)
                    hf_, hb_ = scr.aps[s][:, 0:256], scr.aps[s][:, 256:512]
                    tt(pool, VK[:, k, 0, 256:512], hf_, hb_, ALU.add)
                    tkm = tt(pool, VK[:, k, 1, 256:512], hf_, hb_, ALU.subtract)
                    scr.give(s, ta, tkm)
                    prev = (k, s2, ta)
                    if k < 3:
                        yield
                t = sums(*prev)
                dve.wait(t)
                for c in range(2):
                    t = rsum(rn[:, c:c + 1], bank.aps[bss][:, 16 * c:16 * c + 8])
                bank.give(bss, t)
                act.wait(t)
                t = fn(rn, rn, ACT.Sqrt, bias=EPS6)
                dve.wait(t)
                rcp(rn, rn)
                own(dve)
                made["k"] = tkm

            made = {}
            steps = filter_steps()
            next(steps)
            ut = []
            for m in range(6):
                (b, t), = project(8, hparts(XO), hready(hk, XO))
                act.wait(t)
                t = cp(act, uh[:, m, 1:513], bank.aps[b])
                bank.give(b, t)
                ut.append(t)
                next(steps, None)
            for _ in steps:
                pass
            tkm = made["k"]
            SW8 = [(q + 8) % 16 if q < 16 else q for q in range(32)]
            pool.wait(pe.now(), dve.now())

            def rot(b, t, dst):
                s1, s2 = scr.take(act, pool), scr.take(dve, pool)
                act.wait(t)
                ta = cp(act, scr.aps[s1], bank.aps[b])
                bank.give(b, ta)
                dve.wait(ta)
                td = shuf(scr.aps[s2], scr.aps[s1], SW8)
                pool.wait(td)
                tt(pool, scr.aps[s1], scr.aps[s1], COS, ALU.mult)
                tt(pool, scr.aps[s2], scr.aps[s2], SIN, ALU.mult)
                own(pool)
                tp = tt(pool, dst, scr.aps[s1], scr.aps[s2], ALU.add)
                scr.give(s1, tp)
                scr.give(s2, tp)
                return tp

            qk = {}
            for m in range(8):
                (b, t), = project(8, hparts(XO))
                qk[m] = rot(b, t, (qT if m < 4 else kT)[:, m % 4, :])
            vtk = {}
            for half in range(2):
                us = [W.unit(), W.unit()]
                for tl in range(4):
                    b = bank.take(pe)
                    t = tokens_by_weights(tl, us, b)
                    act.wait(t)
                    vtk[(half, tl)] = cp(act, vv[:, tl, half * 256:half * 256 + 256], bank.aps[b][:, 0:256])
                    bank.give(b, vtk[(half, tl)])
                W.release(t)
                W.release(t)

            dve.wait(tz, *ut)
            for c in range(6):
                w = [pc("cw", 18 * i + 6 * k + c) for k in range(3)]
                s = scr.take(dve) if c >= 2 else None
                dst = x0[:, c, :] if c < 2 else scr.aps[s]
                ts(dve, dst, uh[:, c, 0:512], w[0], pc("cb", 6 * i + c), ALU.mult, ALU.add)
                own(dve)
                stt(dst, uh[:, c, 1:513], w[1], dst, ALU.mult, ALU.add)
                own(dve)
                t = stt(dst, uh[:, c, 2:514], w[2], dst, ALU.mult, ALU.add)
                own(dve)
                if 2 <= c < 4:
                    t = cp(dve, vT[:, c - 2, :], dst)
                    own(dve)
                if c >= 4:
                    t = tt(dve, vT[:, c - 4, :], vT[:, c - 4, :], dst, ALU.mult)
                if s is not None:
                    scr.give(s, t)
            tv = t
            for c in range(2):
                for k in range(4):
                    pe.wait(tv)
                    b = bank.take(pe)
                    t = tr(bank.aps[b][:, 0:P], vT[:, c, k * P:k * P + P])
                    act.wait(t)
                    cp(act, VK[:, k, 0, c * P:c * P + P], bank.aps[b][:, 0:P])
                    t = cp(act, VK[:, k, 1, c * P:c * P + P], bank.aps[b][:, 0:P])
                    bank.give(b, t)
            tvk = t
            pr = project(8, hparts(XO)) + project(8, hparts(XO))
            hfree = [pe.now()]
            for c, (b, t) in enumerate(pr):
                U = uh[:, :, :].rearrange("p a t -> p (a t)")[:, 0:3096]
                A, B = U[:, 0:528], U[:, 528:1056]
                ms(dve, A, 0.0) if c == 0 else None
                if c == 0:
                    ms(dve, B, 0.0)
                own(dve)
                a0 = 8
                s = scr.take(dve)
                s3 = scr.take(dve)
                dve.wait(t)
                cp(dve, A[:, a0:a0 + 512], bank.aps[b])
                t = cp(dve, scr.aps[s], bank.aps[b])
                bank.give(b, t)
                own(dve)
                R = scr.aps[s3]
                tt(dve, B[:, a0:a0 + 513], A[:, a0 - 1:a0 + 512], A[:, a0:a0 + 513], ALU.add)
                own(dve)
                if c == 0:
                    cp(dve, R[0:64, :], B[0:64, a0:a0 + 512])
                    own(dve)
                tt(dve, A[:, a0 - 1:a0 + 514], B[:, a0 - 2:a0 + 513], B[:, a0:a0 + 515], ALU.add)
                own(dve)
                if c == 0:
                    cp(dve, R[64:128, :], A[64:128, a0:a0 + 512])
                else:
                    tt(dve, B[:, a0 - 3:a0 + 516], A[:, a0 - 5:a0 + 514], A[:, a0 - 1:a0 + 518], ALU.add)
                    own(dve)
                    cp(dve, R[0:64, :], B[0:64, a0:a0 + 512])
                    tt(dve, R[64:128, :], B[64:128, a0 - 4:a0 + 508], B[64:128, a0 + 4:a0 + 516], ALU.add)
                own(dve)
                tt(dve, R, R, ICN[:, c, :], ALU.mult)
                own(dve)
                t = tt(dve, R, R, scr.aps[s], ALU.subtract)
                own(dve)
                scr.give(s, t)
                if c == 0:
                    for z in (A, B):
                        ms(dve, z, 0.0)
                    own(dve)
                b = bank.take(pe)
                pe.wait(t)
                t = mm(bank.aps[b], pw[:, c * P:c * P + P], R, True, True, True)
                scr.give(s3, t)
                s = scr.take(dve)
                dve.wait(t)
                t = ts(dve, scr.aps[s], bank.aps[b], pc("pb", 2 * i + c), pc("psc", 2 * i + c), ALU.add, ALU.mult)
                bank.give(b, t)
                put(6 + c, s, t)

            pe.wait(tvk, tkm)
            vn = SM[:, 512:1024]
            b = bank.take(pe)
            for k in range(4):
                t = mm(bank.aps[b][0:1, :], ALT, VK[:, k, 0, :], k == 0, k == 3, k == 3)
            act.wait(t)
            t = cp(act, vn[0:1, :], bank.aps[b][0:1, :])
            bank.give(b, t)
            tvn = t
            ft = []
            for m in range(4):
                bs = []
                u = W.unit()
                for cs in range(2):
                    b = bank.take(pe)
                    for k in range(4):
                        w = u[:, (4 * cs + k) * P:(4 * cs + k + 1) * P]
                        t = mm(bank.aps[b], w, VK[:, k, cs, :], k == 0, k == 3, k == 3)
                    bs.append((b, t))
                W.release(t)
                sv = [scr.take(act), scr.take(act)]
                for cs in range(2):
                    act.wait(bs[cs][1])
                    t = cp(act, scr.aps[sv[cs]][:, 0:256], bank.aps[bs[cs][0]][:, 0:256])
                dve.wait(t, bs[1][1])
                s3 = scr.take(dve)
                kr, ks = bank.aps[bs[0][0]][:, 256:512], bank.aps[bs[1][0]][:, 256:512]
                vr, vs = scr.aps[sv[0]][:, 0:256], scr.aps[sv[1]][:, 0:256]
                t1, t2 = scr.aps[s3][:, 0:256], scr.aps[s3][:, 256:512]
                tt(dve, YF[:, m, :], vr, kr, ALU.mult)
                tt(dve, t1, vs, ks, ALU.mult)
                tt(dve, YF[:, 4 + m, :], vr, ks, ALU.mult)
                t = tt(dve, t2, vs, kr, ALU.mult)
                bank.give(bs[0][0], t)
                bank.give(bs[1][0], t)
                scr.give(sv[0], t)
                scr.give(sv[1], t)
                own(dve)
                tt(dve, YF[:, m, :], YF[:, m, :], t1, ALU.subtract)
                t = tt(dve, YF[:, 4 + m, :], YF[:, 4 + m, :], t2, ALU.add)
                scr.give(s3, t)
                if m == 0:
                    dve.wait(tvn)
                    own(dve)
                    t = tt(dve, YF[0:1, 4, :], vn[0:1, 0:256], vn[0:1, 256:512], ALU.mult)
                ft.append(t)
            hb = [bank.take(pe) for _ in range(2)]
            pe.wait(ft[-1])
            for uu in range(4):
                u = W.unit()
                for q in range(2):
                    m = 2 * uu + q
                    for c in range(2):
                        t = mm(bank.aps[hb[c]], YF[:, m, c * P:c * P + P], u[:, q * 512:q * 512 + 512],
                               m == 0, m == 7, True)
                W.release(t)
            for c in range(2):
                s = scr.take(dve)
                dve.wait(t)
                ty = ts(dve, scr.aps[s], bank.aps[hb[c]], rn[:, c:c + 1], None, ALU.mult)
                bank.give(hb[c], ty)
                own(dve)
                stt(scr.aps[s], vT[:, c, :], pc("hb", 2 * i + c), scr.aps[s], ALU.mult, ALU.add)
                own(dve)
                put(c, s, tt(dve, scr.aps[s], scr.aps[s], x0[:, c, :], ALU.mult))

            la = SM[:, 490:494]
            for z in range(2):
                t = dot(SM[:, 1028:1092], lq[:, 128 * z:128 * z + 64], lq[:, 128 * z + 64:128 * z + 128],
                        la[:, z:z + 1])
                own(dve)
            act.wait(t)
            t = fn(la[:, 0:2], la[:, 0:2], ACT.Exp)
            dve.wait(t)
            stt(la[:, 2:3], la[:, 0:1], -1.0, la[:, 1:2], ALU.mult, ALU.add)
            own(dve)
            nlam = la[:, 3:4]
            ts(dve, nlam, la[:, 2:3], -lam_init, None, ALU.add)
            own(dve)
            subg = SM[:, 494:495]
            ts(dve, subg, pc("sub", i), 1.0 - lam_init, None, ALU.mult)
            own(dve)
            AR = Slots([VK[:, k, c, :] for k in range(4) for c in range(2)])
            PB = Slots([uh.rearrange("p a t -> p (a t)")[:, 512 * k:512 * k + 512] for k in range(6)])
            free = [pe.now(), dve.now(), act.now(), pool.now()]
            for sl in (AR, PB):
                for n in range(len(sl.aps)):
                    sl.give(n, *free)
            mx, nm, ss, rs = (SM[:, 496 + 4 * k:500 + 4 * k] for k in range(4))

            def scores2(h, blk, it):
                res = []
                for c in range(2):
                    b = bank.take(pe)
                    pe.wait(qk[h], qk[4 + h])
                    t = mm(bank.aps[b], qT[64 * c:64 * c + 64, h, blk * P:blk * P + P],
                           kT[64 * c:64 * c + 64, h, :], True, True, True)
                    q = 2 * (it % 2) + c
                    dve.wait(t)
                    rmax(mx[:, q:q + 1], bank.aps[b])
                    own(dve)
                    t = ts(dve, nm[:, q:q + 1], mx[:, q:q + 1], -0.125, None, ALU.mult)
                    p = PB.take(act)
                    act.wait(t)
                    t = fn(PB.aps[p], bank.aps[b], ACT.Exp, bias=nm[:, q:q + 1], scale=0.125, acc=ss[:, q:q + 1])
                    bank.give(b, t)
                    res.append((p, q, t))
                return res

            def mix2(res):
                (p0, q0, t0), (p1, q1, t1) = res
                dve.wait(t0, t1)
                rcp(rs[:, q0:q0 + 2], ss[:, q0:q0 + 2])
                own(dve)
                t = tt(dve, rs[:, q1:q1 + 1], rs[:, q1:q1 + 1], nlam, ALU.mult)
                pool.wait(t)
                t = ts(pool, PB.aps[p1], PB.aps[p1], rs[:, q1:q1 + 1], 1.0, ALU.mult, ALU.mult)
                a = AR.take(dve)
                dve.wait(t)
                t = stt(AR.aps[a], PB.aps[p0], rs[:, q0:q0 + 1], PB.aps[p1], ALU.mult, ALU.add)
                PB.give(p0, t)
                PB.give(p1, t)
                return a, t

            def values2(h, parts_):
                ob = bank.take(pe)
                prev = None
                for j in range(4):
                    b = bank.take(pe)
                    for q in range(4):
                        a, t = parts_[q]
                        pe.wait(t)
                        tx = tr(bank.aps[b][:, q * P:q * P + P], AR.aps[a][:, j * P:j * P + P], inc=q == 3)
                    e = act if j % 2 else dve
                    s = scr.take(e)
                    e.wait(tx)
                    t = cp(e, scr.aps[s], bank.aps[b])
                    bank.give(b, t)
                    if prev is not None:
                        pe.wait(prev[2])
                        t3 = mm(bank.aps[ob], vv[:, prev[0], h * P:h * P + P], scr.aps[prev[1]],
                                prev[0] == 0, False, True)
                        scr.give(prev[1], t3)
                    prev = (j, s, t)
                for a, _ in parts_:
                    AR.give(a, tx)
                pe.wait(prev[2], *[vtk[(h // 2, z)] for z in range(4)])
                t3 = mm(bank.aps[ob], vv[:, 3, h * P:h * P + P], scr.aps[prev[1]], False, True, True)
                scr.give(prev[1], t3)
                s = scr.take(act)
                act.wait(t3)
                t = cp(act, scr.aps[s], bank.aps[ob])
                bank.give(ob, t)
                s2, r = mean_square(128, [scr.aps[s]], S, EPS5, [t])
                dve.wait(r)
                t = stt(scr.aps[s], scr.aps[s], subg, scr.aps[s2], ALU.mult, ALU.mult)
                scr.give(s2, t)
                put(2 + h, s, t)

            work = [(h, b) for h in range(4) for b in range(4)]
            pend, got = [], []
            for it in range(len(work) + 2):
                if it < len(work):
                    pend.append(scores2(*work[it], it))
                if 1 <= it <= len(work):
                    got.append(mix2(pend[it - 1]))
                if it >= 2 and (it - 2) % 4 == 3:
                    h = (it - 2) // 4
                    values2(h, got[4 * h:4 * h + 4])

            xt = {}
            gather(XO, False)
            for m in range(8):
                (b, t), = project(8, [(S, lambda k: of(YP, k))], lambda k, i_: yt[k])
                dve.wait(t, *(everyone() if m == 0 else ()))
                xt[(m, 0)] = plus_alpha_h(m, bank.aps[b], b)
                sums[0].feed(XS[0][:, m, :], xt[(m, 0)])
            hk = layer_norm(xt, pc("ln1g", 8 * i, 8), pc("ln1b", 8 * i, 8), [dve.now(), *hfree])

            b = bank.take(pe)
            pe.wait(*twg)
            for k in range(8):
                pe.wait(*hk[(k, 0)])
                t = split_mm(bank.aps[b][0:20, :], [WG[:, z, 20 * k:20 * k + 20] for z in range(2)],
                             of(HS[0], k), k == 0, k == 7, k == 7)
            s = scr.take(act)
            act.wait(t)
            t = cp(act, scr.aps[s][0:20, :], bank.aps[b][0:20, :])
            bank.give(b, t)
            b2 = bank.take(pe)
            pe.wait(t)
            for tl in range(4):
                t = tr(bank.aps[b2][:, 20 * tl:20 * tl + 20], scr.aps[s][0:20, tl * P:tl * P + P], 20)
            scr.give(s, t)
            LGT = SM[:, 512:592].rearrange("p (a c) -> p a c", a=4)
            dve.wait(t)
            lgp = bank.aps[b2][:, 0:80].rearrange("p (a c) -> p a c", a=4)
            for tl in range(4):
                t = tt(dve, LGT[:, tl, :], lgp[:, tl, :], pc("mb", 20 * i, 20), ALU.add)
            bank.give(b2, t)
            own(dve)

            def region(a, n):
                return SM[:, a + 128:a + 128 + n]

            gmx, oh, gw = region(464, 4), region(468, 16), region(484, 4)
            fs, e16, tmp = region(488, 16), region(504, 16), region(520, 64)
            m1, m2, a1, a2 = region(584, 4), region(588, 4), region(592, 16), region(608, 16)
            GT, w1_, w2_ = region(624, 64), region(688, 4), region(692, 4)
            nf = region(696, 4)
            v4 = lambda z: z.rearrange("p (a c) -> p a c", a=4)

            def first_max(dst, src, mxv):
                rmax(mxv, src)
                own(dve)
                tt(dve, v4(dst), src, mxv.unsqueeze(2).to_broadcast([P, 4, 4]), ALU.is_equal)
                own(dve)
                ts(dve, nf, v4(dst)[:, :, 0], -1.0, 1.0, ALU.mult, ALU.add)
                own(dve)
                for c in range(1, 4):
                    tt(dve, v4(dst)[:, :, c], v4(dst)[:, :, c], nf, ALU.mult)
                    own(dve)
                    if c < 3:
                        tt(dve, nf, nf, v4(dst)[:, :, c], ALU.subtract)
                        own(dve)

            first_max(oh, LGT[:, :, 0:4], gmx)
            tt(dve, v4(e16), LGT[:, :, 0:4], gmx.unsqueeze(2).to_broadcast([P, 4, 4]), ALU.subtract)
            own(dve)
            act.wait(dve.now())
            t = fn(e16, e16, ACT.Exp)
            dve.wait(t)
            rsum(gw, v4(e16))
            own(dve)
            rcp(gw, gw)
            own(dve)
            for g in range(4):
                sel = v4(oh)[:, :, g].unsqueeze(2).to_broadcast([P, 4, 4])
                dst = fs if g == 0 else e16
                tt(dve, v4(dst), LGT[:, :, 4 + 4 * g:8 + 4 * g], sel, ALU.mult)
                own(dve)
                if g:
                    tt(dve, fs, fs, e16, ALU.add)
                    own(dve)
            first_max(a1, v4(fs), m1)
            stt(fs, a1, -1e30, fs, ALU.mult, ALU.add)
            own(dve)
            first_max(a2, v4(fs), m2)
            tt(dve, w2_, m2, m1, ALU.subtract)
            own(dve)
            act.wait(dve.now())
            t = fn(w2_, w2_, ACT.Exp)
            dve.wait(t)
            ts(dve, w1_, w2_, 1.0, None, ALU.add)
            own(dve)
            rcp(w1_, w1_)
            own(dve)
            tt(dve, w1_, w1_, gw, ALU.mult)
            own(dve)
            tt(dve, w2_, w2_, w1_, ALU.mult)
            own(dve)
            tt(dve, v4(a1), v4(a1), w1_.unsqueeze(2).to_broadcast([P, 4, 4]), ALU.mult)
            tt(dve, v4(a2), v4(a2), w2_.unsqueeze(2).to_broadcast([P, 4, 4]), ALU.mult)
            own(dve)
            tt(dve, a1, a1, a2, ALU.add)
            own(dve)
            G16 = GT.rearrange("p (a g c) -> p a g c", a=4, g=4)
            for g in range(4):
                sel = v4(oh)[:, :, g].unsqueeze(2).to_broadcast([P, 4, 4])
                t = tt(dve, G16[:, :, g, :], v4(a1), sel, ALU.mult)
            b = bank.take(pe)
            pe.wait(t)
            for tl in range(4):
                t = tr(bank.aps[b][0:16, tl * P:tl * P + P], GT[:, 16 * tl:16 * tl + 16])
            gts = SM[0:16, 512:1024]
            act.wait(t)
            dve.wait(t)
            tg = cp(act, gts, bank.aps[b][0:16, :])
            bank.give(b, tg)

            PT = Pair(16384, 2, S)
            ptk = []
            for z in range(2):
                s = scr.take(sp2)
                tp = l_cst.start(sp2, scr.aps[s], io[f"pt{i}"][:, z, :])
                ptk.append(split(scr.aps[s], PT.hi[:, z, :], PT.hf[:, z, :], PT.lo[:, z, :], tp))
                scr.give(s, ptk[-1][1])
            for m in range(8):
                (b, t), = project(8, hparts(XO), hready(hk, XO))
                sg = scr.take(act)
                act.wait(t)
                ta = fn(scr.aps[sg], bank.aps[b], ACT.Sigmoid, bias=pc("pleb", 8 * i + m))
                bank.give(b, ta)
                (b, t), = project(2, [(S, lambda k: of(PT, k))], lambda k, i_: ptk[k])
                dve.wait(t, ta)
                t = tt(dve, scr.aps[sg], bank.aps[b], scr.aps[sg], ALU.mult)
                bank.give(b, t)
                own(dve)
                dve.wait(*hk[(m, 0)])
                xt[(m, 0)] = plus_alpha_h(m, scr.aps[sg], None)
                scr.give(sg, xt[(m, 0)])

            A = Pair(8192, 8, S)
            afree = everyone()
            if i == 0:
                tok = second_constants(1, afree)
            for q4 in range(4):
                at = {}
                for ex in range(4):
                    gb = bank.take(pe)
                    pe.wait(tg)
                    t = mm(bank.aps[gb], IDT[0:16, 4 * q4 + ex:4 * q4 + ex + 1].to_broadcast([16, P]), gts,
                           True, True, True)
                    sg = scr.take(act)
                    act.wait(t)
                    tgb = cp(act, scr.aps[sg], bank.aps[gb])
                    bank.give(gb, tgb)
                    for f in range(2):
                        (ba, ta), = project(8, hparts(XO), hready(hk, XO))
                        (bc, tc), = project(8, hparts(XO))
                        s = scr.take(act)
                        v = scr.aps[s]
                        act.wait(ta)
                        t = fn(v, bank.aps[ba], ACT.Silu)
                        bank.give(ba, t)
                        dve.wait(t, tc, tgb)
                        t = tt(dve, v, bank.aps[bc], v, ALU.mult)
                        bank.give(bc, t)
                        own(dve)
                        t = tt(dve, v, v, scr.aps[sg], ALU.mult)
                        act.wait(*afree)
                        pool.wait(*afree)
                        n = 2 * ex + f
                        at[n] = split(v, A.hi[:, n, :], A.hf[:, n, :], A.lo[:, n, :], t)
                        scr.give(s, at[n][1])
                    scr.give(sg, t)
                if q4 == 3:
                    hfree = [pe.now()]
                    gather(XO, False)
                for m in range(8):
                    (b, t), = project(8, [(S, lambda k: of(A, k))], lambda k, i_: at[k])
                    dve.wait(t, xt[(m, 0)])
                    x = XS[0][:, m, :]
                    xt[(m, 0)] = tt(dve, x, bank.aps[b], x, ALU.add)
                    bank.give(b, xt[(m, 0)])
                    if q4 == 3:
                        sums[0].feed(x, xt[(m, 0)])
                afree = [pe.now()]
            hk = layer_norm(xt, pc("ln2g", 8 * i, 8), pc("ln2b", 8 * i, 8), [dve.now(), *hfree])

        for k in range(8):
            dve.wait(*hk[(k, 0)])
            t = tt(dve, XS[0][:, k, :], HS[0].hf[:, k, :], HS[0].lf[:, k, :], ALU.add)
        act.wait(t)
        finish(XS[0])


def shape_constants():
    f = np.float32
    p = np.arange(P)
    t = np.arange(S)
    c = {"ident": np.eye(P, dtype=f)}
    pos = (t // 64, t % 64)

    def inv(n):
        return (f(10000.0) ** (-np.arange(0, n, 2, dtype=f) / f(n))).astype(f)

    r = p % 64
    i32 = inv(32)
    ang = np.where((r // 32 == 0)[:, None], pos[0][None].astype(f), pos[1][None].astype(f)) * i32[r % 16][:, None]
    sgn = np.where(r % 32 < 16, -1, 1)[:, None]
    q, n = p[:, None], p[None, :]
    left = np.where(n >= q, 0.0, -1e30)
    right = np.where(n <= q, 0.0, -1e30)
    c["c_l0"] = np.concatenate([np.cos(ang), np.sin(ang) * sgn, left, right], 1).astype(f)
    i128 = inv(128)
    a = [pos[m][None].astype(f) * i128[p % 64][:, None] for m in range(2)]
    sg = np.where(p < 64, 1, -1)[:, None]
    w = np.arange(896)[None] - 384 - p[:, None]
    c["c_l1"] = np.concatenate(
        [np.cos(a[0]), np.cos(a[1]), np.sin(a[0]) * sg, np.sin(a[1]) * sg,
         w], 1).astype(f)
    j = r
    iv = np.power(f(500000.0), -np.arange(0, 16, 2, dtype=f) / f(16)).astype(f)
    ang = t[None].astype(f) * np.where(j < 16, iv[j % 8], 0)[:, None].astype(f)
    sgn = np.where(j < 8, -1, 1)[:, None]
    cos = np.where((j < 16)[:, None], np.cos(ang), 1.0)
    sin = np.where((j < 16)[:, None], np.sin(ang) * sgn, 0.0)
    tl = np.linspace(0.0, 1.0, S, dtype=f)[:, None]
    dmax, dmin = math.log(1e-2) / 0.3, math.log(1e-2) / 1.5
    deltas = np.linspace(dmin, dmax, 256, dtype=f)[None]
    win = np.exp(-tl * np.abs(deltas))
    wb = win.copy()
    wb[0] = 0.0
    win2 = np.concatenate([win, wb], 1).reshape(4, P, 512).transpose(1, 0, 2).reshape(P, 2048)
    icn = []
    for m in range(2):
        rows = []
        for g in range(2):
            wn = (2, 4, 8, 16)[2 * m + g]
            lo = np.clip(t - wn // 2, 0, S - 1)
            hi = np.clip(t + wn // 2 - 1, 0, S - 1)
            rows.append(np.repeat((1.0 / (hi - lo + 1))[None], 64, 0))
        icn.append(np.concatenate(rows, 0))
    wpos = (f(2.0 * math.pi) * t[:, None].astype(f) / f(S)).astype(f)
    bands = np.linspace(1e-4, 15, 16, dtype=f)[None]
    z = np.zeros((P, S))
    z[0:33] = np.concatenate([tl, np.cos(wpos * bands), -np.sin(wpos * bands)], 1).T
    alt = np.where(p % 2 == 0, 1.0, -1.0)[:, None]
    c["c_2"] = np.concatenate([cos, sin, *icn, alt, np.zeros((P, 7))], 1).astype(f)
    c["c_f"] = np.concatenate([win2, z], 1).astype(f)
    th = 2 * np.pi * ((np.arange(S)[:, None] * t[None]) % 1024) / 1024
    C, Sn = np.cos(th), np.sin(th)
    blocks = []
    for m in range(4):
        for M in (C, Sn):
            for k in range(4):
                blocks.append(M[k * P:(k + 1) * P, m * P:(m + 1) * P])
    c["dft"] = np.stack(blocks).reshape(4, 8, P, P).transpose(0, 2, 1, 3).reshape(4, P, 1024).astype(f)
    IC, IS = C * (2 / 1024), Sn * (2 / 1024)
    IC[0] = 1 / 1024
    IS[0] = np.where(t % 2 == 0, 1, -1) / 1024
    c["idft"] = np.stack([IC, IS]).reshape(4, 2, P, S).transpose(0, 2, 1, 3).reshape(4, P, 1024).astype(f)
    return {k: np.ascontiguousarray(x) for k, x in c.items()}


def _units(blocks):
    return blocks.reshape(-1, UB, P, P).transpose(0, 2, 1, 3).reshape(-1, P, UB * P)


def _mk(w):
    k, m = w.shape
    return w.reshape(k // P, P, m // P, P).transpose(2, 0, 1, 3).reshape(-1, P, P)


def _km(w):
    k, m = w.shape
    return w.reshape(k // P, P, m // 256, 2, P).transpose(2, 0, 3, 1, 4).reshape(-1, P, P)


def _cols(v):
    return v.reshape(-1, P).T


def _rows(v):
    return np.broadcast_to(v.reshape(1, -1), (P, v.size))


def _top(v):
    o = np.zeros((P, v.shape[1]), v.dtype)
    o[:v.shape[0]] = v
    return o


def layouts(a):
    g = {}
    cat = np.concatenate
    g["xt"] = cat([a[n][0].T.reshape(8, P, -1).transpose(1, 0, 2).reshape(P, -1) for n in ("x", "ctx")], 1)
    cols = {
        "cc": np.stack([_cols(a["c"][0]), _cols(a["c_ctx"])], 2).reshape(P, 16),
        "ada_b": cat([_cols(a["ada_b"][i]) for i in range(2)], 1),
        "n1": _cols(a["norm1_g"]), "n2": _cols(a["norm2_g"]),
        "qn": np.tile(a["attn_q_norm"][0], 2)[:, None], "kn": np.tile(a["attn_k_norm"][0], 2)[:, None],
        "sink": _rows(a["attn_sink"][0]), "dl": _rows(a["ret_decay_logit"][0]),
        "gn": _cols(a["ret_gn_g"][0]),
        "ln0g": _cols(a["ln0_g_2"]), "ln0b": _cols(a["ln0_b_2"]),
        "ln1g": _cols(a["ln1_g_2"]), "ln1b": _cols(a["ln1_b_2"]),
        "ln2g": _cols(a["ln2_g_2"]), "ln2b": _cols(a["ln2_b_2"]),
        "cw": _cols(a["hy_conv_w_2"]), "cb": _cols(a["hy_conv_b_2"]), "hb": _cols(a["hy_bias_2"]),
        "fr1": _top(a["hy_freq1_2"].T), "fb1": _top(a["hy_fb1_2"].T),
        "fr2": _top(a["hy_freq2_2"].T), "fb2": _top(a["hy_fb2_2"].T),
        "sub": a["att_subln_g_2"].T,
        "pb": _cols(a["pool_b_2"]), "psc": _cols(a["pool_scale_2"]), "pleb": _cols(a["ple_bg_2"]),
        "mb": cat([_rows(a[n][i]) for i in range(2) for n in ("moe_bgc_2", "moe_bgf_2")], 1),
    }
    prm = np.zeros((P, NPRM), np.float32)
    for n, (at, w) in PCOLS.items():
        prm[:, at:at + w] = cols[n]
    g["prm"] = prm
    qkv = a["attn_w_qkv"][0]
    wo = a["attn_w_o"][0]
    g["att"] = _units(cat([_mk(qkv[:, 1024:1280]), _km(qkv[:, 1280:1536]), _mk(qkv[:, 0:768]), _mk(wo[0:512]),
                           _mk(qkv[:, 768:1024]), _mk(wo[512:1024])], 0))
    r, wo = a["ret_w_qkvg"][0], a["ret_w_o"][0]
    g["ret"] = _units(cat([b for h in range(4) for b in (
        _mk(r[:, 256 * h:256 * h + 256]), _mk(r[:, 1024 + 256 * h:1280 + 256 * h]),
        _km(r[:, 2048 + 512 * h:2560 + 512 * h]), _mk(r[:, 4096 + 512 * h:4608 + 512 * h]),
        _mk(wo[512 * h:512 * h + 512]))], 0))
    wgs = [cat([a["moe_wgc_2"][i], a["moe_wgf_2"][i]], 1).reshape(8, P, 20) for i in range(2)]
    pws = np.zeros((2, 2, 2, 64, 2, 64), np.float32)
    for h in range(2):
        pws[:, :, h, :, h, :] = a["pool_w_2"].reshape(2, 2, 2, 64, 64)[:, :, h]
    c2 = shape_constants()
    for i in range(2):
        g[f"ada{i}"] = a["ada_w"][i].reshape(4, 2, P, 12, 512).transpose(3, 0, 2, 1, 4).reshape(48, P, 1024)
        w = a["ffn_w_in"][i].reshape(D, 2, NF, P).transpose(0, 2, 1, 3).reshape(D, 2 * DFF)
        f0, blocks = 0, []
        for nf in CHUNKS:
            blocks += [_mk(w[:, 2 * P * f0:2 * P * (f0 + nf)]), _mk(a["ffn_w_out"][i][P * f0:P * (f0 + nf)])]
            f0 += nf
        g[f"ff{i}"] = _units(cat(blocks, 0))
        w = a["w_in_2"][i]
        g[f"win{i}"] = _units(cat([_mk(w[:, 0:1792]), _km(w[:, 1792:2304]), _mk(w[:, 2304:2560])], 0))
        g[f"wout{i}"] = _units(_mk(a["w_out_2"][i]))
        wg_, wp = _mk(a["ple_wg_2"][i]).reshape(8, 8, P, P), _mk(a["ple_wp_2"][i]).reshape(8, 2, P, P)
        g[f"ple{i}"] = _units(cat([wg_, wp], 1).reshape(-1, P, P))
        w = np.stack([a["moe_w1_2"][i], a["moe_w3_2"][i]], 0).reshape(2, 16, 8, P, 2, P)
        w = w.transpose(1, 4, 0, 2, 3, 5).reshape(4, -1, P, P)
        g[f"moe{i}"] = _units(cat([cat([w[q], _mk(a["moe_w2_2"][i][4 * q:4 * q + 4].reshape(1024, D))], 0)
                                   for q in range(4)], 0))
        g[f"pt{i}"] = a["p_2"][i, 0].T.reshape(2, P, S).transpose(1, 0, 2)
        g[f"c_2{i}"] = cat([c2["c_2"], pws[i].reshape(2, P, P).transpose(1, 0, 2).reshape(P, 256),
                            *[_rows(a[n][i]) for n in ("att_lq1_2", "att_lk1_2", "att_lq2_2", "att_lk2_2")],
                            wgs[i].transpose(1, 0, 2).reshape(P, 160)], 1)
        g[f"c_f{i}"] = cat([c2["c_f"], _top(a["hy_fw1_2"][i]), _top(a["hy_fw2_2"][i]), _top(a["hy_fw3_2"][i])], 1)
    g.update({k: v for k, v in c2.items() if k not in ("c_2", "c_f")})
    return {k: np.ascontiguousarray(v) for k, v in g.items()}


def kernel(**inputs):
    import numpy as _np
    import concourse.bacc as _bacc
    from concourse.bass_utils import run_bass_kernel_spmd as _run

    a = {k: _np.asarray(v) for k, v in inputs.items()}
    nc = _bacc.Bacc("TRN2", target_bir_lowering=False, num_devices=1)
    arrays, io = {}, {}
    for name, v in layouts(a).items():
        arrays[f"in_{name}"] = v
        io[name] = nc.dram_tensor(f"in_{name}", v.shape, mybir.dt.from_np(v.dtype), kind="ExternalInput").ap()
    out = nc.dram_tensor("out_0", (P, 8, S), F32, kind="ExternalOutput").ap()
    build(nc, io, out)
    r = _run(nc, [arrays], core_ids=[0])
    got = r.results[0]["out_0"]
    return got.transpose(2, 1, 0).reshape(1, S, D)
```

```python
import math
from contextlib import ExitStack

import numpy as np

import concourse.bass as bass
from concourse import mybir
from concourse.alu_op_type import AluOpType as ALU

F32 = mybir.dt.float32
ACT = mybir.ActivationFunctionType
AX = mybir.AxisListType
P = 128
D = 1024
S = 512
L = 256
T = S + L
DFF = 2816
NF = DFF // P
UB = 8
F32R = mybir.dt.float32r
CHUNKS = (4, 4, 4, 4, 3, 3)
NBLK = (2 * S + 16 * (P - 1)) // P
EU = 6
OUT_ORDER = (0, 1, 6, 7, 2, 3, 4, 5)
ALPHA = (2 * 2) ** 0.25
MAGIC = 12582912.0
PI = 3.1415925
NX = 6144
NB = 13056
NR = 18432

PCOLS = {}
_at = 0


def _col(name, n):
    global _at
    PCOLS[name] = (_at, n)
    _at += n


_col("cc", 16)
_col("ada_b", 96)
_col("n1", 16)
_col("n2", 16)
_col("qn", 1)
_col("kn", 1)
_col("sink", 16)
_col("dl", 8)
_col("gn", 16)
_col("ln0g", 8)
_col("ln0b", 8)
_col("ln1g", 16)
_col("ln1b", 16)
_col("ln2g", 16)
_col("ln2b", 16)
_col("cw", 36)
_col("cb", 12)
_col("hb", 4)
_col("fr1", 2)
_col("fb1", 2)
_col("fr2", 2)
_col("fb2", 2)
_col("sub", 2)
_col("pb", 4)
_col("psc", 4)
_col("pleb", 16)
_col("mb", 40)
NPRM = _at


def _plan():
    plan = [("att", 20, False),
            ("ff0", 66, False), ("ret", 64, False), ("ff1", 66, False)]
    for i in range(2):
        plan += [(f"win{i}", 14, False), ("dft", 4, True), ("idft", 4, True), (f"wqk{i}", 6, False),
                 (f"wout{i}", 8, False),
                 (f"ple{i}", 10, False), (f"moe{i}", EU * NBLK, False)]
    return plan


PLAN = _plan()


def _expert_units():
    order = [(0, u) for u in range(4)]
    for b in range(NBLK):
        if b + 1 < NBLK:
            order += [(b + 1, u) for u in range(4)]
        order += [(b, 4), (b, 5)]
    return order


EXPERT_UNITS = _expert_units()


class Queue:

    def __init__(self, sem):
        self.sem, self.n, self.ops, self.seen = sem, 0, [], {}

    def wait(self, *toks):
        for t in toks:
            if t is None:
                continue
            sem, val = t
            if self.seen.get(sem.name, 0) < val:
                self.seen[sem.name] = val
                self.ops.append((None, sem, val))

    def do(self, fn, inc=True):
        if not inc:
            self.ops.append((fn, None, 0))
            return None
        self.n += 1
        self.ops.append((fn, self.sem, 1))
        return (self.sem, self.n)

    def now(self):
        return (self.sem, self.n)

    def play(self, eng):
        for fn, sem, val in self.ops:
            if fn is None:
                eng.wait_ge(sem, val)
            elif sem is None:
                fn(eng)
            else:
                fn(eng).then_inc(sem, val)


class Slots:

    def __init__(self, aps):
        self.aps, self.free, self.i, self.held = aps, [() for _ in aps], 0, set()

    def take(self, *writers):
        assert len(self.held) < len(self.aps)
        while self.i % len(self.aps) in self.held:
            self.i += 1
        i = self.i % len(self.aps)
        self.i += 1
        self.held.add(i)
        for w in writers:
            w.wait(*self.free[i])
        return i

    def ap(self, i):
        return self.aps[i]

    def give(self, i, *toks):
        self.free[i] = toks
        self.held.discard(i)


def build(nc, io, out):
    ctx = ExitStack()
    with ctx:
        def sb(name, shape, dt=F32):
            return ctx.enter_context(nc.sbuf_tensor(name, shape, dt))

        def sem(name):
            return ctx.enter_context(nc.semaphore(name))

        XF = sb("XF", [P, NX])
        RT = sb("RT", [P, NR], F32R)
        RTF = RT[:, :].bitcast(F32)
        BF = sb("BF", [P, NB])
        RAW = sb("RAW", [P, 2, UB * P])
        WH = sb("WH", [P, 3, UB * P], F32R)
        WL = sb("WL", [P, 3, UB * P], F32R)
        PRM = sb("PRM", [P, NPRM])
        IDT = sb("IDT", [P, P])
        MEAN = {n: sb(f"MEAN{n}", [P, P]) for n in (128, 512, 1024)}
        BD64 = sb("BD64", [P, P])
        SM = sb("SM", [P, 1100])
        SCR = sb("SCR", [P, 9, 512])
        IDR = sb("IDR", [P, P], F32R)
        PLACE = sb("PLACE", [P, 8], mybir.dt.uint32)
        EXI = sb("EXI", [1, NBLK], mybir.dt.int32)
        HD = nc.dram_tensor("placed_in", (NBLK * P, D), F32, kind="Internal").ap()
        OD = nc.dram_tensor("placed_out", (NBLK * P, D), F32, kind="Internal").ap()
        PS = ctx.enter_context(nc.psum_tensor("PS", [P, 8, 512], F32))
        PSF = PS[:, :, :].rearrange("p a b -> p (a b)")
        XS = [XF[:, 0:4096].rearrange("p (k t) -> p k t", k=8), XF[:, 4096:6144].rearrange("p (k t) -> p k t", k=8)]

        class Pair:

            def __init__(self, at, tiles, n):
                def view(t, a):
                    return t[:, a:a + tiles * n].rearrange("p (k t) -> p k t", k=tiles)

                self.hi, self.lo = view(RT, at), view(RT, at + tiles * n)
                self.hf, self.lf = view(RTF, at), view(RTF, at + tiles * n)

        HS = [Pair(0, 8, S), Pair(8192, 8, L)]

        pe, act, dve, pool, sp = (Queue(sem("s_" + n)) for n in ("pe", "act", "dve", "pool", "sp"))
        engines = (pe, act, dve, pool)

        def everyone():
            return [q.now() for q in engines]

        def mm(o, w, x, start, stop, inc):
            return pe.do(lambda e: e.matmul(o, w, x, start=start, stop=stop), inc)

        def tr(o, x, n=P, inc=True):
            return pe.do(lambda e: e.transpose(o, x, IDT[0:n, 0:n]), inc)

        def fn(o, x, f, bias=0.0, scale=1.0, acc=None):
            if acc is None:
                return act.do(lambda e: e.activation(o, x, f, bias=bias, scale=scale))
            return act.do(lambda e: e.activation(o, x, f, bias=bias, scale=scale, accum_out=acc))

        def cp(q, o, x):
            if q is act:
                return fn(o, x, ACT.Copy)
            return q.do(lambda e: e.tensor_copy(o, x))

        def tt(q, o, a, b, op):
            return q.do(lambda e: e.tensor_tensor(o, a, b, op))

        def ts(q, o, a, s1, s2, o1, o2=None):
            if o2 is None:
                return q.do(lambda e: e.tensor_scalar(o, a, s1, None, o1))
            return q.do(lambda e: e.tensor_scalar(o, a, s1, s2, o1, o2))

        def stt(o, a, s, b, o1, o2):
            return dve.do(lambda e: e.scalar_tensor_tensor(o, a, s, b, o1, o2))

        def rsq(o, x, eps, t):
            act.wait(t)
            a = fn(o, x, ACT.Sqrt, bias=eps)
            dve.wait(a)
            return a, rcp(o, o)

        def rcp(o, x):
            return dve.do(lambda e: e.reciprocal(o, x))

        def rmax(o, x):
            return dve.do(lambda e: e.reduce_max(o, x, AX.X))

        def rsum(o, x):
            return dve.do(lambda e: e.reduce_sum(o, x, AX.X))

        def ms(q, o, v):
            return q.do(lambda e: e.memset(o, v))

        def dot(o, a, b, acc):
            return dve.do(lambda e: e.tensor_tensor_reduce(o, a, b, 1.0, 0.0, ALU.mult, ALU.add, acc))

        def shuf(o, x, mask):
            return dve.do(lambda e: e.stream_shuffle(o, x, mask))

        def own(q):
            q.wait(q.now())

        class Load:

            def __init__(self, name):
                self.sem, self.n = sem(name), 0

            def start(self, q, o, i):
                self.n += 16
                q.ops.append((lambda e: e.dma_start(o, i), self.sem, 16))
                return (self.sem, self.n)

        bank = Slots([PS[:, i, :] for i in range(8)])
        scr = Slots([SCR[:, i, :] for i in range(9)])

        small = [0]

        def sm(n):
            a = small[0]
            small[0] += n
            assert small[0] <= 488
            return SM[:, a:a + n]

        EPS6, EPS5, ONE = sm(1), sm(1), sm(1)

        def finish(src):
            l_out = Load("l_out")
            for k in range(8):
                t = l_out.start(act, out[:, k, :], src[:, k, 0:S])
            act.wait(t)
            block = ctx.enter_context(nc.Block())
            block.sync(lambda e: sp.play(e))
            block.scalar(lambda e: act.play(e))
            block.tensor(lambda e: pe.play(e))
            block.vector(lambda e: dve.play(e))
            block.gpsimd(lambda e: pool.play(e))

        l_prm = Load("l_prm")
        prm = None
        for o, i in ((PRM[:, :], io["prm"]), (IDT[:, :], io["ident"])):
            prm = l_prm.start(act, o, i)
        xin = Load("l_x").start(act, XF[:, :], io["xt"])
        ms(dve, EPS6, 1e-6)
        ms(dve, EPS5, 1e-5)
        ms(dve, ONE, 1.0)
        for n in MEAN:
            ms(dve, MEAN[n][:, :], 1.0 / n)
        ms(dve, BD64[:, :], 0.0)
        own(dve)
        ms(dve, BD64[0:64, 0:64], 1.0 / 64)
        ready = ms(dve, BD64[64:128, 64:128], 1.0 / 64)
        for q in engines:
            q.wait(prm, ready)

        def pc(name, a=0, n=1):
            c = PCOLS[name][0] + a
            return PRM[:, c:c + n]

        l_cst = Load("l_cst")

        def constants(name, at, after):
            src = io[name]
            act.wait(*after)
            return l_cst.start(act, BF[:, at:at + src.shape[1]], src)

        class Stream:

            def __init__(self):
                self.units = [(n, i, raw) for n, k, raw in PLAN for i in range(k)]

                def part(hi, lo):
                    return hi, lo, hi.bitcast(F32)

                self.raw = [Slots([RAW[:, i, :] for i in range(2)]),
                            Slots([BF[:, 6824 + 1024 * i:7848 + 1024 * i] for i in range(3)])]
                self.load = [[Load(f"l_w{i}") for i in range(2)], [Load(f"l_v{i}") for i in range(3)]]
                self.part = [Slots([part(WH[:, i, :], WL[:, i, :]) for i in range(3)]),
                             Slots([part(RT[:, 13312:14336], RT[:, 14336:15360])])]
                self.loaded, self.made, self.at, self.b, self.live = [], [], 0, UB, []
                self.route, self.base = {}, {}
                self.ahead()

            def prefetch(self):
                while len(self.loaded) < len(self.units):
                    name, i, raw = self.units[len(self.loaded)]
                    moe = name.startswith("moe")
                    if moe and name not in self.route:
                        return
                    z = 1 if moe and i % 5 > 1 else 0
                    slots = self.raw[z]
                    if len(slots.held) == len(slots.aps):
                        return
                    r = slots.take(sp)
                    if moe:
                        t = self.routed(name, i, self.load[z][r], slots.aps[r])
                    else:
                        t = self.load[z][r].start(sp, slots.aps[r], io[name][i])
                    self.loaded.append((z, r, t))

            def ahead(self):
                self.prefetch()
                while len(self.made) < len(self.loaded):
                    name, i, raw = self.units[len(self.made)]
                    z, r, t = self.loaded[len(self.made)]
                    if raw:
                        self.made.append((None, 0, (t,)))
                        continue
                    moe = name.startswith("moe")
                    y = 1 if moe and i % 4 == 3 else 0
                    slots = self.part[y]
                    if len(slots.held) == len(slots.aps):
                        return
                    low = dve if moe and i % 3 == 1 else pool
                    p = slots.take(act, low)
                    hi, lo, hf = slots.aps[p]
                    src = self.raw[z].aps[r]
                    act.wait(t)
                    ta = fn(hi, src, ACT.Copy)
                    low.wait(ta)
                    tl = tt(low, lo, src, hf, ALU.subtract)
                    self.raw[z].give(r, tl)
                    self.made.append((p, y, (ta, tl)))
                    self.prefetch()

            def routing(self, name, tok):
                for slots in (self.raw[1], self.part[1]):
                    for i in range(len(slots.aps)):
                        slots.give(i, *everyone())
                self.route[name] = tok
                self.ahead()

            def routed(self, name, i, ld, dst):
                blk, u = EXPERT_UNITS[i]
                tok, first, base = self.route[name], u == 0, self.base
                sp.wait(tok)

                def load(e):
                    if first:
                        base[blk] = e.value_load(EXI[0:1, blk:blk + 1], min_val=0, max_val=15 * EU)
                    src = io[name][bass.ds(base[blk] + u, 1), :, :].rearrange("a p f -> (a p) f")
                    return e.dma_start(dst, src)

                ld.n += 16
                sp.ops.append((load, ld.sem, 16))
                return (ld.sem, ld.n)

            def unit(self):
                assert self.at < len(self.made)
                p, y, toks = self.made[self.at]
                pe.wait(*toks)
                self.live.append(self.at)
                self.at += 1
                if p is None:
                    z, r, _ = self.loaded[self.at - 1]
                    return self.raw[z].aps[r]
                return self.part[y].aps[p][0:2]

            def release(self, tok):
                n = self.live.pop(0)
                p, y, _ = self.made[n]
                if p is None:
                    z, r, _ = self.loaded[n]
                    self.raw[z].give(r, tok)
                else:
                    self.part[y].give(p, tok)
                self.b = UB
                self.ahead()

            def next(self):
                if self.b == UB:
                    self.cur = self.unit()
                    self.b = 0
                a = [x[:, self.b * P:(self.b + 1) * P] for x in self.cur]
                self.b += 1
                return a

            def full(self):
                return self.b == UB

        RING = Slots([BF[:, i * 1024:i * 1024 + 1024] for i in range(12)])
        l_ring = [Load(f"l_a{i}") for i in range(12)]
        W = Stream()

        def split_mm(o, w, x, first, last, inc):
            mm(o, w[0], x[0], first, False, False)
            mm(o, w[0], x[1], False, False, False)
            return mm(o, w[1], x[0], False, last, inc)

        def project_steps(kt, parts, ready=None, banks=None):
            banks = banks or bank
            bs = [banks.take(pe) for _ in parts]
            toks = [None] * len(parts)
            for k in range(kt):
                w = W.next()
                for i in range(len(parts)):
                    if ready is not None:
                        pe.wait(*ready(k, i))
                xs = [x(k) for _, x in parts]
                os_ = [banks.ap(b)[:, 0:n] for b, (n, _) in zip(bs, parts)]
                last = k == kt - 1
                for o, x in zip(os_, xs):
                    mm(o, w[0], x[0], k == 0, False, False)
                    mm(o, w[0], x[1], False, False, False)
                for i, (o, x) in enumerate(zip(os_, xs)):
                    end = W.full() and i == len(parts) - 1
                    t = mm(o, w[1], x[0], False, last, end or last)
                    toks[i] = t
                if W.full():
                    W.release(t)
                yield None
            yield [(banks, b, t) for b, t in zip(bs, toks)]

        def project(kt, parts, ready=None, banks=None):
            for r in project_steps(kt, parts, ready, banks):
                pass
            return [(b, t) for _, b, t in r]

        def outputs(kt, parts, ready, order=None):
            order = order or range(kt)
            steps = [(m, k) for m in range(2) for k in range(kt - 1)] + [(0, kt - 1), (1, kt - 1)]
            bs = [[bank.take(pe) for _ in parts] for _ in range(2)]
            res = [None, None]
            for m, k in steps:
                w = W.next()
                pe.wait(*[t for i in range(len(parts)) for t in ready(order[k], i)])
                os_ = [bank.ap(b)[:, 0:n] for b, (n, _) in zip(bs[m], parts)]
                xs = [x(order[k]) for _, x in parts]
                for o, x in zip(os_, xs):
                    mm(o, w[0], x[0], k == 0, False, False)
                    mm(o, w[0], x[1], False, False, False)
                toks = []
                for i, (o, x) in enumerate(zip(os_, xs)):
                    end = k == kt - 1 or (W.full() and i == len(parts) - 1)
                    toks.append(mm(o, w[1], x[0], False, k == kt - 1, end))
                if W.full():
                    W.release(toks[-1])
                res[m] = list(zip(bs[m], toks))
            yield res[0]
            yield res[1]
            for m in range(2, 8):
                yield project(kt, [(n, (lambda k, x=x: x(order[k]))) for n, x in parts])

        XP = [(0, 0, S), (1, S, L)]

        def of(pair, k):
            return pair.hi[:, k, :], pair.lo[:, k, :]

        def hparts(parts):
            return [(n, (lambda k, j=j: of(HS[j], k))) for j, _, n in parts]

        def hready(tk, parts):
            return lambda k, i: tk[(k, parts[i][0])]

        def split(src, hi, hf, lo, need):
            act.wait(need)
            ta = fn(hi, src, ACT.Copy)
            pool.wait(ta)
            return ta, tt(pool, lo, src, hf, ALU.subtract)

        def tokens_by_weights(tl, us, b):
            j, c = (0, tl * P) if tl < 4 else (1, (tl - 4) * P)
            for k in range(8):
                w = [x.rearrange("p (k c) -> p k c", k=4)[:, k % 4, :] for x in us[k // 4]]
                t = split_mm(bank.aps[b][:, 0:256], [x[:, c:c + P] for x in of(HS[j], k)], w,
                             k == 0, k == 7, k == 7)
            return t

        class Sums:

            def __init__(self, n, square):
                self.n, self.square, self.acc, self.prev = n, square, None, None

            def flush(self):
                if self.prev is None:
                    return
                s, x, t = self.prev
                a = scr.aps[self.acc][:, 0:self.n]
                dve.wait(t, self.tok)
                self.tok = tt(dve, a, self.first if self.first is not None else a, x, ALU.add)
                self.first = None
                if s is not None:
                    scr.give(s, self.tok)
                self.prev = None

            def feed(self, x, t):
                if not self.square:
                    if self.acc is None:
                        self.acc, self.first, self.tok = scr.take(dve), x, t
                        return
                    self.prev = (None, x, t)
                    self.flush()
                    return
                s = scr.take(act, dve) if self.acc is None else scr.take(act)
                act.wait(t)
                v = scr.aps[s][:, 0:self.n]
                t = fn(v, x, ACT.Square)
                if self.acc is None:
                    self.acc, self.first, self.tok = s, None, t
                    return
                self.flush()
                self.prev = (s, v, t)

            def mean(self):
                self.flush()
                b = bank.take(pe)
                pe.wait(self.tok)
                t = mm(bank.aps[b][:, 0:self.n], MEAN[1024][:, :], scr.aps[self.acc][:, 0:self.n], True, True, True)
                scr.give(self.acc, t)
                return b, t

        sums = {}

        def gather(parts, square):
            for j, c0, n in parts:
                sums[j] = Sums(n, square)

        def root(b, t, n, eps):
            s = scr.take(act)
            a, r = rsq(scr.aps[s][:, 0:n], bank.aps[b][:, 0:n], eps, t)
            bank.give(b, a)
            return s, r

        def mean_square(over, tiles, n, eps, need):
            b = bank.take(pe)
            last = len(tiles) - 1
            for k, x in enumerate(tiles):
                s = scr.take(act)
                act.wait(need[k])
                t = fn(scr.aps[s][:, 0:n], x, ACT.Square)
                pe.wait(t)
                t = mm(bank.aps[b][:, 0:n], MEAN[over][:, :], scr.aps[s][:, 0:n], k == 0, k == last, True)
                scr.give(s, t)
            return root(b, t, n, eps)

        def apply_norm(j, n, xt, s, r, A, B, hfree):
            for q in (dve, act, pool):
                q.wait(r, *hfree)
            H = HS[j]
            tk = {}
            for k in range(8):
                yield tk
                dve.wait(xt[(k, j)])
                q = scr.take(dve, act)
                h = scr.aps[q][:, 0:n]
                t = stt(h, XS[j][:, k, :], A[:, k:k + 1], scr.aps[s][:, 0:n], ALU.mult, ALU.mult)
                act.wait(t)
                ta = fn(H.hi[:, k, :], h, ACT.Identity, bias=B[:, k:k + 1])
                if k % 2:
                    own(act)
                    tb = fn(h, h, ACT.Identity, bias=B[:, k:k + 1])
                    pool.wait(tb)
                    td = tt(pool, H.lo[:, k, :], h, H.hf[:, k, :], ALU.subtract)
                else:
                    dve.wait(t, ta)
                    td = stt(H.lo[:, k, :], h, B[:, k:k + 1], H.hf[:, k, :], ALU.add, ALU.subtract)
                scr.give(q, td)
                tk[(k, j)] = (ta, td)
            scr.give(s, t)
            yield tk

        def rms_steps(xt, A, B, parts, hfree):
            rs_ = [(j, n, root(*sums.pop(j).mean(), n, EPS6)) for j, c0, n in parts]
            tk = {}
            for j, n, (s, r) in rs_:
                for done in apply_norm(j, n, xt, s, r, A[:, 8 * j:8 * j + 8], B[:, 8 * j:8 * j + 8], hfree):
                    yield tk
                tk.update(done)
            yield tk

        def last(steps):
            for r in steps:
                pass
            return r

        def rms_modulate(xt, A, B, parts, hfree):
            return last(rms_steps(xt, A, B, parts, hfree))

        def layer_norm(xt, g, b, hfree):
            X = XS[0]
            bk, t = sums.pop(0).mean()
            dve.wait(t)
            ct = {}
            for k in range(8):
                dve.wait(xt[(k, 0)])
                ct[(k, 0)] = tt(dve, X[:, k, :], X[:, k, :], bank.aps[bk], ALU.subtract)
            bank.give(bk, ct[(7, 0)])
            s, r = mean_square(1024, [X[:, k, :] for k in range(8)], S, EPS5, [ct[(k, 0)] for k in range(8)])
            return last(apply_norm(0, S, ct, s, r, g, b, hfree))

        cact = sm(16)
        own(act)
        ct = fn(cact, pc("cc", 0, 16), ACT.Silu)
        gather(XP, True)
        for k in range(8):
            for j in range(2):
                sums[j].feed(XS[j][:, k, :], xin)
        xt = {(k, j): xin for k in range(8) for j in range(2)}
        mods = []
        for i in range(2):
            mod = sm(96).rearrange("p (j m) -> p j m", j=2)
            pe.wait(ct)
            prev = None

            def turned(c, s, t, mod=mod, i=i):
                b = bank.take(pe)
                pe.wait(t)
                for q in range(4):
                    t = tr(bank.aps[b][:, 2 * q:2 * q + 2], scr.aps[s][0:2, q * P:q * P + P], 2)
                scr.give(s, t)
                dve.wait(t)
                for j in range(2):
                    v = bank.aps[b][:, 0:8].rearrange("p (m j) -> p j m", j=2)[:, j, :]
                    t = tt(dve, mod[:, j, 4 * c:4 * c + 4], v, pc("ada_b", 48 * i + 4 * c, 4), ALU.add)
                bank.give(b, t)

            for c in range(12):
                b = bank.take(pe)
                for q in range(4):
                    r = RING.take(sp)
                    tu = l_ring[r].start(sp, RING.aps[r], io[f"ada{i}"][4 * c + q])
                    pe.wait(tu)
                    u = RING.aps[r].rearrange("p (k c) -> p k c", k=2)
                    for z in range(2):
                        k = 2 * q + z
                        t = mm(bank.aps[b][0:2, :], cact[:, 2 * k:2 * k + 2], u[:, z, :], k == 0, k == 7, z == 1)
                    RING.give(r, t)
                s = scr.take(act)
                act.wait(t)
                t = cp(act, scr.aps[s][0:2, :], bank.aps[b][0:2, :])
                bank.give(b, t)
                if prev:
                    turned(*prev)
                prev = (c, s, t)
                if i == 1:
                    next(steps)
                    if c % 3 == 2:
                        next(steps)
            turned(*prev)
            own(dve)
            AB = []
            for q, nm in ((0, "n1"), (3, "n2")):
                A, B = sm(16), sm(16)
                for j in range(2):
                    stt(A[:, 8 * j:8 * j + 8], mod[:, j, 8 * (q + 1):8 * (q + 2)], 1.0, pc(nm, 8 * i, 8),
                        ALU.add, ALU.mult)
                    t = cp(dve, B[:, 8 * j:8 * j + 8], mod[:, j, 8 * q:8 * q + 8])
                AB.append((A, B))
            for q in engines:
                q.wait(t)
            mods.append((mod, AB))
            if i == 0:
                steps = rms_steps(xt, AB[0][0], AB[0][1], XP, ())
        hk = last(steps)

        def residual(xt, mod, s, parts, res, k):
            for (j, c0, n), (b, t) in zip(parts, res):
                dve.wait(t, xt[(k, j)])
                x = XS[j][:, k, :]
                t = stt(x, bank.aps[b][:, 0:n], mod[:, j, 8 * s + k:8 * s + k + 1], x, ALU.mult, ALU.add)
                bank.give(b, t)
                xt[(k, j)] = t
                if j in sums:
                    sums[j].feed(x, t)

        def swiglu(i, xt, mod, AB, parts, hfree):
            hk = rms_modulate(xt, AB[1][0], AB[1][1], parts, hfree)
            A = [Pair(12288, 4, S), Pair(16384, 4, L)]
            afree = [pe.now()]
            for c, nf in enumerate(CHUNKS):
                ft = {}
                for f in range(nf):
                    for _ in range(2):
                        if errands:
                            errands.pop()()
                    gate = project(8, hparts(parts), hready(hk, parts))
                    up = project(8, hparts(parts))
                    for (j, c0, n), (bg, tg), (bu, tu) in zip(parts, gate, up):
                        s = scr.take(act)
                        act.wait(tg)
                        a = fn(scr.aps[s][:, 0:n], bank.aps[bg][:, 0:n], ACT.Silu)
                        bank.give(bg, a)
                        dve.wait(a, tu)
                        v = scr.aps[s][:, 0:n]
                        t = tt(dve, v, bank.aps[bu][:, 0:n], v, ALU.mult)
                        bank.give(bu, t)
                        act.wait(*afree)
                        pool.wait(*afree)
                        ft[(f, j)] = split(v, A[j].hi[:, f, :], A[j].hf[:, f, :], A[j].lo[:, f, :], t)
                        scr.give(s, ft[(f, j)][1])
                if c == len(CHUNKS) - 1:
                    hf = [pe.now()]
                    gather(parts, i == 0)
                for m, r in enumerate(outputs(nf, [(n, (lambda f, j=j: of(A[j], f))) for j, _, n in parts],
                                              lambda f, i_: ft[(f, parts[i_][0])])):
                    residual(xt, mod, 5, parts, r, m)
                afree = [pe.now()]
            return hf


        mod, AB = mods[0]
        tok = constants("c_l0", 0, everyone())
        for q in (dve, pool):
            q.wait(tok)
        CS = BF[:, 0:1280]
        COS, SIN = CS[:, 0:512], CS[:, 512:1024]
        MSK = CS[:, 1024:1280].rearrange("p (a b) -> p a b", a=2)
        kD = BF[:, 1280:4352].rearrange("p (a t) -> p a t", a=4)
        vD = BF[:, 4352:5888].rearrange("p (a g d) -> p a g d", a=6, g=4)
        qT = Slots([BF[:, 5888 + 1536 * i:7424 + 1536 * i].rearrange("p (a t) -> p a t", a=2) for i in range(2)])
        PR = Slots([BF[:, 8960 + 640 * i:9600 + 640 * i] for i in range(6)])
        OP = [Pair(12288, 4, S), Pair(16384, 4, L)]
        SW16 = [(i + 16) % 32 for i in range(32)]

        nsink = sm(16)
        tns = ts(dve, nsink, pc("sink", 0, 16), -1.0, None, ALU.mult)
        own(dve)

        def head_norm(banks, b, tok, n, gain, dst, rope, fin):
            sq, q1, rr = scr.take(act), scr.take(dve), scr.take(act)
            act.wait(tok)
            dve.wait(tok)
            ps = banks.aps[b][:, 0:n]
            ta = fn(scr.aps[sq][:, 0:n], ps, ACT.Square)
            dve.wait(ta)
            td = ts(dve, scr.aps[q1][:, 0:n], ps, gain, None, ALU.mult)
            banks.give(b, ta, td)

            def later():
                b2 = banks.take(pe)
                pe.wait(ta)
                t = mm(banks.aps[b2][:, 0:n], BD64[:, :], scr.aps[sq][:, 0:n], True, True, True)
                act.wait(t)
                t2, _ = rsq(scr.aps[rr][:, 0:n], banks.aps[b2][:, 0:n], EPS6, t)
                banks.give(b2, t2)
                own(dve)
                if not rope:
                    t = tt(dve, dst, scr.aps[q1][:, 0:n], scr.aps[rr][:, 0:n], ALU.mult)
                    scr.give(sq, t)
                else:
                    tq = tt(dve, scr.aps[q1][:, 0:n], scr.aps[q1][:, 0:n], scr.aps[rr][:, 0:n], ALU.mult)
                    own(dve)
                    tsw = shuf(scr.aps[sq][:, 0:n], scr.aps[q1][:, 0:n], SW16)
                    pool.wait(tq, tsw)
                    tt(pool, scr.aps[q1][:, 0:n], scr.aps[q1][:, 0:n], COS, ALU.mult)
                    tt(pool, scr.aps[sq][:, 0:n], scr.aps[sq][:, 0:n], SIN, ALU.mult)
                    own(pool)
                    t = tt(pool, dst, scr.aps[q1][:, 0:n], scr.aps[sq][:, 0:n], ALU.add)
                    scr.give(sq, t)
                scr.give(q1, t)
                scr.give(rr, t)
                fin(t)

            return later

        later = []

        def flush():
            for f in later:
                f()
            later.clear()

        kq = {}
        for m in range(2):
            res = project(8, hparts(XP), hready(hk, XP))
            flush()
            for (j, c0, n), (b, t) in zip(XP, res):
                kr = scr.take(dve, pool)

                def fin(t, kr=kr, m=m, j=j, c0=c0, n=n):
                    act.wait(t)
                    for g in range(2):
                        for h2 in range(2):
                            tk = cp(act, kD[64 * h2:64 * h2 + 64, 2 * m + g, c0:c0 + n],
                                    scr.aps[kr][64 * g:64 * g + 64, 0:n])
                        kq[(2 * m + g, j)] = tk
                    scr.give(kr, tk)

                later.append(head_norm(bank, b, t, n, pc("kn"), scr.aps[kr][:, 0:n], j == 0, fin))
        vt = []
        us = [W.unit(), W.unit()]
        for tl in range(6):
            b = bank.take(pe)
            t = tokens_by_weights(tl, us, b)
            if tl == 0:
                flush()
            act.wait(t)
            t2 = cp(act, vD[:, tl, :, :], bank.aps[b][:, 0:256].rearrange("p (g d) -> p g d", g=4))
            vt.append(t2)
            bank.give(b, t2)
        W.release(t)
        W.release(t)
        qt, qslot = {}, {}

        def query_steps(g, banks):
            qs = qslot[g] = qT.take(dve, pool)
            for m in range(2):
                for res in project_steps(8, hparts(XP), hready(hk, XP), banks):
                    if res is None:
                        yield
                todo = []
                for (j, c0, n), (bk, b, t) in zip(XP, res):
                    def fin(t, m=m, j=j):
                        qt[(g, m, j)] = t

                    todo.append(head_norm(bk, b, t, n, pc("qn"), qT.aps[qs][:, m, c0:c0 + n], j == 0, fin))
                yield
                for f in todo:
                    f()
                    yield

        for _ in query_steps(0, bank):
            pass

        mx, nm, ss, es, rs = sm(8), sm(8), sm(8), sm(8), sm(8)
        pairs, single, outs, fbank = Slots([0, 2]), Slots([PS[:, 4, :]]), Slots([PS[:, 5, :]]), Slots(
            [PS[:, 6, :], PS[:, 7, :]])
        for i in range(2):
            pairs.give(i, *bank.free[2 * i], *bank.free[2 * i + 1])
            fbank.give(i, *bank.free[6 + i])
        single.give(0, *bank.free[4])
        outs.give(0, *bank.free[5])
        ot = {}

        def attn_scores(g, blk, hh, it):
            h = 4 * g + hh
            m, hf = h // 2, 64 * (h % 2)
            j = 0 if blk < 4 else 1
            q0 = blk * P
            lo, hi = (max(blk - 1, 0), min(blk + 2, 4)) if j == 0 else (0, 0)
            nl = (hi - lo) * P
            s = pairs.take(pe)
            o = pairs.aps[s] * 512
            pe.wait(qt[(g, hh // 2, j)], kq[(g, 0)], kq[(g, 1)])
            w = qT.aps[qslot[g]][hf:hf + 64, hh // 2, q0:q0 + P]
            t = mm(PSF[:, o + 256:o + 512], w, kD[hf:hf + 64, g, S:T], True, True, True)
            if nl:
                t = mm(PSF[:, o + 512:o + 512 + nl], w, kD[hf:hf + 64, g, lo * P:hi * P], True, True, True)
            sc = PSF[:, o + 256:o + 512 + nl]
            dve.wait(t)
            if nl == 384:
                v = PSF[:, o + 512:o + 896].rearrange("p (a b) -> p a b", a=3)[:, 0:3:2, :]
                tt(dve, v, v, MSK, ALU.add)
                own(dve)
            elif nl:
                a = 1 if lo == blk else 0
                v = PSF[:, o + 512 + a * P:o + 640 + a * P]
                tt(dve, v, v, MSK[:, a, :], ALU.add)
                own(dve)
            c = it % 8
            rmax(mx[:, c:c + 1], sc)
            own(dve)
            t = ts(dve, nm[:, c:c + 1], mx[:, c:c + 1], -0.125, nsink[:, h:h + 1], ALU.mult, ALU.min)
            p = PR.take(act)
            act.wait(t, tns)
            pp = PR.aps[p][:, 0:256 + nl]
            t1 = fn(pp, sc, ACT.Exp, bias=nm[:, c:c + 1], scale=0.125, acc=ss[:, c:c + 1])
            pairs.give(s, t1)
            t2 = fn(es[:, c:c + 1], pc("sink", h), ACT.Exp, bias=nm[:, c:c + 1])
            return p, pp, c, t2

        def attn_norm(p, pp, c, t2):
            dve.wait(t2)
            tt(dve, rs[:, c:c + 1], ss[:, c:c + 1], es[:, c:c + 1], ALU.add)
            own(dve)
            t = rcp(rs[:, c:c + 1], rs[:, c:c + 1])
            pool.wait(t)
            return p, pp, ts(pool, pp, pp, rs[:, c:c + 1], 1.0, ALU.mult, ALU.mult)

        def attn_values(g, blk, ps):
            j = 0 if blk < 4 else 1
            q0 = blk * P
            lo, hi = (max(blk - 1, 0), min(blk + 2, 4)) if j == 0 else (0, 0)
            keys = [4, 5] + list(range(lo, hi))
            ob = outs.take(pe)
            acc = outs.aps[ob][0:64, :]
            prev = None

            def pv(item, last):
                jt, s, t = item
                pe.wait(t, vt[keys[jt]])
                t = mm(acc, vD[:, keys[jt], g, :], scr.aps[s], jt == 0, last, True)
                scr.give(s, t)
                return t

            for jt in range(len(keys)):
                b = single.take(pe)
                tb = single.aps[b]
                for hh in range(4):
                    pe.wait(ps[hh][2])
                    t = tr(tb[:, hh * P:(hh + 1) * P], ps[hh][1][:, jt * P:(jt + 1) * P], inc=hh == 3 )
                e = act if jt % 2 else dve
                s = scr.take(e)
                e.wait(t)
                t2 = cp(e, scr.aps[s], tb)
                single.give(b, t2)
                fill(VFILL[g])
                if prev is not None:
                    pv(prev, False)
                prev = (jt, s, t2)
            for hh in range(4):
                PR.give(ps[hh][0], t)
            t = pv(prev, True)
            av = acc.rearrange("p (a b q) -> p a b q", a=2, b=2)
            s = scr.take(act)
            sv = scr.aps[s][:, 0:256].rearrange("p (a q) -> p a q", a=2)
            act.wait(t)
            cp(act, sv[64:128], av[:, :, 1, :])
            td = cp(act, sv[0:64], av[:, :, 0, :])
            outs.give(ob, td)
            act.wait(ofree.get(g % 2))
            pool.wait(ofree.get(g % 2))
            a, c = 2 * (g % 2), q0 - (0 if j == 0 else S)
            o = OP[j]
            tk = split(sv, o.hi[:, a:a + 2, c:c + P], o.hf[:, a:a + 2, c:c + P], o.lo[:, a:a + 2, c:c + P], td)
            scr.give(s, tk[1])
            ot[(g, blk)] = tk

        VFILL = (1, 1, 1, 1)
        filler = []

        def fill(n):
            while n and filler:
                try:
                    next(filler[0])
                    n -= 1
                except StopIteration:
                    filler.pop(0)

        def output(g):
            a = 2 * (g % 2)
            for b2 in range(6):
                pe.wait(*ot[(g, b2)])
            for m in range(8):
                for res in project_steps(2, [(n, (lambda k, j=j: of(OP[j], a + k))) for j, _, n in XP], None, fbank):
                    if res is None:
                        yield
                for (j, c0, n), (bk, b, t) in zip(XP, res):
                    dve.wait(t, xt[(m, j)])
                    x = XS[j][:, m, :]
                    t2 = stt(x, bk.aps[b][:, 0:n], mods[0][0][:, j, 16 + m:17 + m], x, ALU.mult, ALU.add)
                    bk.give(b, t2)
                    xt[(m, j)] = t2
                    if j in sums:
                        sums[j].feed(x, t2)
                yield

        ofree = {}
        for g in range(4):
            work = [(blk, hh) for blk in range(6) for hh in range(4)]
            FILL = (0, 1, 1, 0)
            if g < 3:
                filler.append(query_steps(g + 1, fbank))
            if g:
                filler.append(output(g - 1))
            soft, groups = [], {}
            for it in range(len(work) + 3):
                if it < len(work):
                    blk, hh = work[it]
                    soft.append(attn_scores(g, blk, hh, it))
                    fill(FILL[g])
                if 1 <= it <= len(work):
                    blk, hh = work[it - 1]
                    groups.setdefault(blk, []).append(attn_norm(*soft[it - 1]))
                if it >= 2 and (it - 2) % 4 == 3:
                    blk = work[it - 2][0]
                    attn_values(g, blk, groups[blk])
            fill(10**9)
            qT.give(qslot[g], pe.now())
            if g:
                ofree[(g - 1) % 2] = pe.now()
        gather(XP, True)
        for _ in output(3):
            pass
        for i in range(2):
            bank.give(2 * i, *pairs.free[i])
            bank.give(2 * i + 1, *pairs.free[i])
            bank.give(6 + i, *fbank.free[i])
        bank.give(4, *single.free[0])
        bank.give(5, *outs.free[0])
        hfree = [pe.now()]

        zs = scr.take(dve)
        t = ms(dve, scr.aps[zs], 0.0)
        act.wait(t)
        l_zero = Load("l_zero")
        tzero = []

        def write_zeros(n):
            for z in range(2):
                tzero.append(l_zero.start(act, HD[n * P:n * P + P, 512 * z:512 * z + 512], scr.aps[zs]))

        errands = [lambda n=n: write_zeros(n) for n in range(NBLK)]
        own(act)
        fn(IDR[:, :], IDT[:, :], ACT.Copy)
        tok = constants("c_l1", 0, everyone())
        hfree = swiglu(0, xt, mod, AB, XP, hfree)
        tzero = tzero[-1]
        scr.give(zs, tzero)

        mod, AB = mods[1]
        hk = rms_modulate(xt, AB[0][0], AB[0][1], XP, hfree)
        for q in engines:
            q.wait(tok)
        CS = BF[:, 0:2944]
        RC = CS[:, 0:1024].rearrange("p (a t) -> p a t", a=2)
        RS = CS[:, 1024:2048].rearrange("p (a t) -> p a t", a=2)
        DIF = CS[:, 2048:2944]
        qR = BF[:, 2944:3968].rearrange("p (a t) -> p a t", a=2)
        kR = BF[:, 3968:5504].rearrange("p (a t) -> p a t", a=2)
        vR = BF[:, 5504:8576].rearrange("p (a t) -> p a t", a=6)
        ST = BF[:, 8576:11648].rearrange("p (a t) -> p a t", a=6)
        M1 = BF[:, 11648:12544]
        CX, CY, MT = XF[:, 4096:4736], XF[:, 4736:5376], XF[:, 5376:5888]
        YP = Pair(12288, 4, S)
        lg, e1, e2, e3, e4 = (sm(8) for _ in range(5))
        dl = pc("dl", 0, 8)
        ts(dve, e1, dl, -1.0, None, ALU.mult)
        own(dve)
        t = tt(dve, e1, e1, dl, ALU.min)
        act.wait(t)
        t = fn(e2, e1, ACT.Exp)
        dve.wait(t)
        ts(dve, e3, e2, 2.0, None, ALU.add)
        own(dve)
        rcp(e3, e3)
        own(dve)
        tt(dve, e2, e2, e3, ALU.mult)
        own(dve)
        tt(dve, e3, e2, e2, ALU.mult)
        own(dve)
        ms(dve, e4, 1.0 / 19)
        for n in range(17, 0, -2):
            own(dve)
            tt(dve, e4, e4, e3, ALU.mult)
            own(dve)
            ts(dve, e4, e4, 1.0 / n, None, ALU.add)
        own(dve)
        tt(dve, e4, e4, e2, ALU.mult)
        ts(dve, lg, dl, 0.0, None, ALU.min)
        own(dve)
        tlg = stt(lg, e4, -2.0, lg, ALU.mult, ALU.add)
        own(dve)
        lgL, lgS = sm(4), sm(4)
        ts(dve, lgL, lg[:, 0:4], float(L), None, ALU.mult)
        ts(dve, lgS, lg[:, 4:8], float(S), None, ALU.mult)
        nlb = sm(4)
        t = ts(dve, nlb, lg[:, 4:8], -1.0, None, ALU.mult)
        dve.wait(t)
        act.wait(t)

        yt = {}
        done = {"pv": None, "score": None, "score_d": None, "wo": None}
        for h in range(4):
            lf, lb = lg[:, h:h + 1], lg[:, 4 + h:5 + h]
            dve.wait(done["score_d"])
            pool.wait(done["score_d"])
            act.wait(done["score_d"])
            for a, n in ((0, 512), (512, 384)):
                v, w = M1[:, a:a + n], MT[:, 0:n]
                ts(dve, v, DIF[:, a:a + n], 0.0, lf, ALU.max, ALU.mult)
                ts(dve, w, DIF[:, a:a + n], 0.0, nlb[:, h:h + 1], ALU.min, ALU.mult)
                own(dve)
                t = tt(dve, v, v, w, ALU.add)
                own(dve)
            act.wait(t)
            tM1 = fn(M1, M1, ACT.Exp)
            pool.wait(tM1)
            tM1 = tt(pool, M1[:, 384:512], M1[:, 384:512], IDT[:, :], ALU.add)
            fn(CX, DIF[:, 256:896], ACT.Exp, scale=lf, bias=lgL[:, h:h + 1])
            a = fn(CY, DIF[:, 256:896], ACT.Exp, scale=nlb[:, h:h + 1], bias=lgS[:, h:h + 1])
            pool.wait(a)
            tM2 = tt(pool, CX, CX, CY, ALU.add)

            qk = {}
            for isk in range(2):
                parts = XP if isk else XP[:1]
                dst = kR if isk else qR
                for m in range(2):
                    res = project(8, hparts(parts), hready(hk, parts))
                    b, t = res[0]
                    ps = bank.aps[b]
                    s1, s2 = scr.take(dve), scr.take(dve)
                    dve.wait(t, done["score"])
                    pool.wait(done["score"])
                    tt(dve, scr.aps[s1], ps, RC[:, m, :], ALU.mult)
                    tt(dve, scr.aps[s2][0:64, :], ps[64:128, :], RS[64:128, m, :], ALU.mult)
                    t = tt(dve, scr.aps[s2][64:128, :], ps[0:64, :], RS[0:64, m, :], ALU.mult)
                    bank.give(b, t)
                    pool.wait(t)
                    t = tt(pool, dst[:, m, 0:S], scr.aps[s1], scr.aps[s2], ALU.add)
                    scr.give(s1, t)
                    scr.give(s2, t)
                    qk[(isk, m, 0)] = t
                    if isk:
                        b, t = res[1]
                        act.wait(t, done["score"])
                        t = cp(act, dst[:, m, S:T], bank.aps[b][:, 0:L])
                        bank.give(b, t)
                        qk[(isk, m, 1)] = t
            vtk = {}
            for half in range(2):
                us = [W.unit(), W.unit()]
                for tl in range(6):
                    b = bank.take(pe)
                    t = tokens_by_weights(tl, us, b)
                    act.wait(t, done["pv"])
                    vtk[(half, tl)] = cp(act, vR[:, tl, half * 256:half * 256 + 256], bank.aps[b][:, 0:256])
                    bank.give(b, vtk[(half, tl)])
                W.release(t)
                W.release(t)
            st = []
            for j in range(6):
                b = bank.take(pe)
                jj = 0 if j < 4 else 1
                for d in range(2):
                    pe.wait(qk[(0, d, 0)], qk[(1, d, jj)])
                    t = mm(bank.aps[b], kR[:, d, j * P:j * P + P], qR[:, d, :], d == 0, d == 1, d == 1)
                if j < 4:
                    dec = M1[:, 384 - P * j:896 - P * j]
                else:
                    dec = CX[:, 128 - P * (j - 4):640 - P * (j - 4)]
                dve.wait(t, tM1, tM2, done["pv"])
                t2 = stt(ST[:, j, :], bank.aps[b], 0.0625, dec, ALU.mult, ALU.mult)
                bank.give(b, t2)
                st.append(t2)
            done["score"], done["score_d"] = t, st[-1]
            os_ = []
            for e_ in range(4):
                b = bank.take(pe)
                for j in range(6):
                    pe.wait(st[j], vtk[(e_ // 2, j)])
                    t = mm(bank.aps[b], vR[:, j, e_ * P:e_ * P + P], ST[:, j, :], j == 0, j == 5, j == 5)
                done["pv"] = t
                s = scr.take(act)
                act.wait(t)
                t = cp(act, scr.aps[s], bank.aps[b])
                bank.give(b, t)
                os_.append((s, t))
            gt = []
            for m in range(2):
                gt += project(8, hparts(XP[:1]))
            om = bank.take(pe)
            for e_ in range(4):
                pe.wait(os_[e_][1])
                t = mm(bank.aps[om], MEAN[512][:, :], scr.aps[os_[e_][0]], e_ == 0, e_ == 3, e_ == 3)
            dve.wait(t)
            cts = []
            for e_ in range(4):
                dve.wait(os_[e_][1])
                o = scr.aps[os_[e_][0]]
                cts.append(tt(dve, o, o, bank.aps[om], ALU.subtract))
            bank.give(om, cts[-1])
            gt += project(8, hparts(XP[:1]))
            s, r = mean_square(512, [scr.aps[q_] for q_, _ in os_], S, EPS6, cts)
            gt += project(8, hparts(XP[:1]))
            if h == 3:
                hfree = [pe.now()]
            dve.wait(r)
            for e_ in range(4):
                o = scr.aps[os_[e_][0]]
                b, t = gt[e_]
                sg = scr.take(act)
                act.wait(t)
                ta = fn(scr.aps[sg], bank.aps[b], ACT.Silu)
                bank.give(b, ta)
                stt(o, o, pc("gn", 4 * h + e_), scr.aps[s], ALU.mult, ALU.mult)
                dve.wait(ta)
                own(dve)
                t = tt(dve, o, o, scr.aps[sg], ALU.mult)
                scr.give(sg, t)
                act.wait(done["wo"])
                pool.wait(done["wo"])
                yt[e_] = split(o, YP.hi[:, e_, :], YP.hf[:, e_, :], YP.lo[:, e_, :], t)
                scr.give(os_[e_][0], yt[e_][1])
            scr.give(s, t)
            if h == 3:
                gather(XP[:1], True)
            for m, r in enumerate(outputs(4, [(S, lambda k: of(YP, k))], lambda k, i: yt[k])):
                residual(xt, mod, 2, XP[:1], r, m)
            done["wo"] = pe.now()
        WG = sb("WG", [P, 2, 160], F32R)

        l_sc, l_xb, l_ob = Load("l_sc"), [Load(f"l_xb{z}") for z in range(2)], [Load(f"l_ob{z}") for z in range(2)]
        l_g = [Load(f"l_g{z}") for z in range(4)]

        def feature_mean(b, tl, need):
            pe.wait(need)
            for k in range(8):
                t = mm(bank.aps[b][:, tl * P:tl * P + P], MEAN[1024][:, :], XS[0][:, k, tl * P:tl * P + P],
                       k == 0, k == 7, k == 7)
            return t

        class Known:

            def __init__(self, b, t):
                self.b, self.t = b, t

            def mean(self):
                return self.b, self.t

        def scatter(dst, rows, src):
            l_sc.n += 16
            at = bass.IndirectOffsetOnAxis(rows, 0)
            pool.ops.append((lambda e: e.indirect_dma_start(dst, at, src, None), l_sc.sem, 16))
            return (l_sc.sem, l_sc.n)

        def fetch_rows(g, dst, rows):
            l_g[g].n += 16
            at = bass.IndirectOffsetOnAxis(rows, 0)
            pool.ops.append((lambda e: e.indirect_dma_start(dst, None, OD, at), l_g[g].sem, 16))
            return (l_g[g].sem, l_g[g].n)

        tok = [constants("c_20", 0, everyone()), constants("c_f0", 6824, ())]
        hfree = swiglu(1, xt, mod, AB, XP[:1], hfree)

        XO = XP[:1]
        def plus_alpha_h(m, y, b):
            x = XS[0][:, m, :]
            t = stt(x, HS[0].hf[:, m, :], ALPHA, y, ALU.mult, ALU.add)
            if b is not None:
                bank.give(b, t)
            own(dve)
            return stt(x, HS[0].lf[:, m, :], ALPHA, x, ALU.mult, ALU.add)

        hk = layer_norm(xt, pc("ln0g", 0, 8), pc("ln0b", 0, 8), hfree)
        for i in range(2):
            lam_init = 0.8 - 0.6 * math.exp(-0.3 * i)
            for q in engines:
                q.wait(*tok[-1:])
            CS = BF[:, 0:2728]
            COS, SIN = CS[:, 0:512], CS[:, 512:1024]
            ICN = CS[:, 1024:2048].rearrange("p (a t) -> p a t", a=2)
            ALT = CS[:, 2048:2049]
            pw, lq, wg = CS[:, 2056:2312], CS[:, 2312:2568], CS[:, 2568:2728]
            VK = BF[:, 2728:6824].rearrange("p (a b c) -> p a b c", a=4, b=2)
            qT = BF[:, 6824:8872].rearrange("p (a t) -> p a t", a=4)
            kT = BF[:, 8872:10920].rearrange("p (a t) -> p a t", a=4)
            vv = BF[:, 10920:12968].rearrange("p (a t) -> p a t", a=4)
            WIN = BF[:, 6824:8872].rearrange("p (a t) -> p a t", a=4)
            ZT = BF[0:33, 8872:9384]
            fws = BF[0:33, 9384:9448], BF[0:64, 9448:9512]
            fw3 = BF[0:64, 9512:10024]
            uh = XF[:, 0:3096].rearrange("p (a t) -> p a t", a=6)
            YF = XF[:, 0:2048].rearrange("p (a c) -> p a c", a=8)
            x0 = XF[:, 3096:4120].rearrange("p (a t) -> p a t", a=2)
            vT = XF[:, 4120:5144].rearrange("p (a t) -> p a t", a=2)
            YP = Pair(8192, 8, S)
            yt = {}

            def put(k, s, t, YP=YP, yt=yt):
                yt[k] = split(scr.aps[s], YP.hi[:, k, :], YP.hf[:, k, :], YP.lo[:, k, :], t)
                scr.give(s, yt[k][1])

            for q in (act, pool, dve):
                q.wait(*everyone())
            twg = split(wg, WG[:, 0, :], WG[:, 0, :].bitcast(F32), WG[:, 1, :], None)
            tz = ms(pool, uh[:, :, 0:1], 0.0)
            tz = ms(pool, uh[:, :, 513:514], 0.0)
            rn = SM[:, 488:490]

            def filter_steps():
                rhs, tin, held = ZT, None, []
                for z in range(2):
                    b = bank.take(pe)
                    pe.wait(tin)
                    t = mm(bank.aps[b][0:64, :], fws[z], rhs, True, True, True)
                    for h_ in held:
                        scr.give(h_, t)
                    s1, s2 = scr.take(dve, act), scr.take(dve, act)
                    a_, k_ = scr.aps[s1][0:64, :], scr.aps[s2][0:64, :]
                    dve.wait(t)
                    fb, fr = pc(("fb1", "fb2")[z], i)[0:64, :], pc(("fr1", "fr2")[z], i)[0:64, :]
                    t = ts(dve, a_, bank.aps[b][0:64, :], fb, fr, ALU.add, ALU.mult)
                    bank.give(b, t)
                    own(dve)
                    ts(dve, k_, a_, 1.0 / (2 * math.pi), MAGIC, ALU.mult, ALU.add)
                    own(dve)
                    ts(dve, k_, k_, -MAGIC, None, ALU.add)
                    own(dve)
                    stt(a_, k_, -6.28125, a_, ALU.mult, ALU.add)
                    own(dve)
                    stt(a_, k_, -(2 * math.pi - 6.28125), a_, ALU.mult, ALU.add)
                    own(dve)
                    t = ts(dve, a_, a_, PI, -PI, ALU.min, ALU.max)
                    act.wait(t)
                    tin = fn(k_, a_, ACT.Sin)
                    scr.give(s1, tin)
                    rhs, held = k_, [s2]
                    yield
                bss = bank.take(pe)
                prev = None

                def sums(k, s2, ta):
                    pe.wait(ta)
                    for c in range(2):
                        for fb_ in range(2):
                            col = 16 * c + 4 * fb_ + k
                            t = mm(bank.aps[bss][:, col:col + 1],
                                   scr.aps[s2][:, fb_ * 256 + c * P:fb_ * 256 + c * P + P], ONE, True, True, True)
                    scr.give(s2, t)
                    return t

                for k in range(4):
                    b = bank.take(pe)
                    pe.wait(tin)
                    t = mm(bank.aps[b], rhs[:, k * P:k * P + P], fw3, True, True, True)
                    if k == 3:
                        scr.give(held[0], t)
                    if prev:
                        sums(*prev)
                    s, s2 = scr.take(dve), scr.take(act)
                    dve.wait(t)
                    t = tt(dve, scr.aps[s], bank.aps[b], WIN[:, k, :], ALU.mult)
                    bank.give(b, t)
                    act.wait(t)
                    ta = fn(scr.aps[s2], scr.aps[s], ACT.Square)
                    pool.wait(t)
                    hf_, hb_ = scr.aps[s][:, 0:256], scr.aps[s][:, 256:512]
                    tt(pool, VK[:, k, 0, 256:512], hf_, hb_, ALU.add)
                    tkm = tt(pool, VK[:, k, 1, 256:512], hf_, hb_, ALU.subtract)
                    scr.give(s, ta, tkm)
                    prev = (k, s2, ta)
                    if k < 3:
                        yield
                t = sums(*prev)
                dve.wait(t)
                for c in range(2):
                    t = rsum(rn[:, c:c + 1], bank.aps[bss][:, 16 * c:16 * c + 8])
                bank.give(bss, t)
                act.wait(t)
                t = fn(rn, rn, ACT.Sqrt, bias=EPS6)
                dve.wait(t)
                rcp(rn, rn)
                own(dve)
                made["k"] = tkm

            made = {}
            steps = filter_steps()
            next(steps)
            ut = []
            for m in range(6):
                (b, t), = project(8, hparts(XO), hready(hk, XO))
                act.wait(t)
                t = cp(act, uh[:, m, 1:513], bank.aps[b])
                bank.give(b, t)
                ut.append(t)
                next(steps, None)
            for _ in steps:
                pass
            tkm = made["k"]
            SW8 = [(q + 8) % 16 if q < 16 else q for q in range(32)]
            pool.wait(pe.now(), dve.now())

            def rot(b, t, dst):
                s1, s2 = scr.take(act, pool), scr.take(dve, pool)
                act.wait(t)
                ta = cp(act, scr.aps[s1], bank.aps[b])
                bank.give(b, ta)
                dve.wait(ta)
                td = shuf(scr.aps[s2], scr.aps[s1], SW8)
                pool.wait(td)
                tt(pool, scr.aps[s1], scr.aps[s1], COS, ALU.mult)
                tt(pool, scr.aps[s2], scr.aps[s2], SIN, ALU.mult)
                own(pool)
                tp = tt(pool, dst, scr.aps[s1], scr.aps[s2], ALU.add)
                scr.give(s1, tp)
                scr.give(s2, tp)
                return tp

            qk = {}

            def qk_steps(h):
                for m in (h, 4 + h):
                    for r in project_steps(8, hparts(XO)):
                        yield
                    (_, b, t), = r
                    qk[m] = rot(b, t, (qT if m < 4 else kT)[:, m % 4, :])

            for _ in qk_steps(0):
                pass
            vtk = {}
            for half in range(2):
                us = [W.unit(), W.unit()]
                for tl in range(4):
                    b = bank.take(pe)
                    t = tokens_by_weights(tl, us, b)
                    act.wait(t)
                    vtk[(half, tl)] = cp(act, vv[:, tl, half * 256:half * 256 + 256], bank.aps[b][:, 0:256])
                    bank.give(b, vtk[(half, tl)])
                W.release(t)
                W.release(t)

            dve.wait(tz, *ut)
            for c in range(6):
                w = [pc("cw", 18 * i + 6 * k + c) for k in range(3)]
                s = scr.take(dve) if c >= 2 else None
                dst = x0[:, c, :] if c < 2 else scr.aps[s]
                ts(dve, dst, uh[:, c, 0:512], w[0], pc("cb", 6 * i + c), ALU.mult, ALU.add)
                own(dve)
                stt(dst, uh[:, c, 1:513], w[1], dst, ALU.mult, ALU.add)
                own(dve)
                t = stt(dst, uh[:, c, 2:514], w[2], dst, ALU.mult, ALU.add)
                own(dve)
                if 2 <= c < 4:
                    t = cp(dve, vT[:, c - 2, :], dst)
                    own(dve)
                if c >= 4:
                    t = tt(dve, vT[:, c - 4, :], vT[:, c - 4, :], dst, ALU.mult)
                if s is not None:
                    scr.give(s, t)
            tv = t
            for c in range(2):
                for k in range(4):
                    pe.wait(tv)
                    b = bank.take(pe)
                    t = tr(bank.aps[b][:, 0:P], vT[:, c, k * P:k * P + P])
                    act.wait(t)
                    cp(act, VK[:, k, 0, c * P:c * P + P], bank.aps[b][:, 0:P])
                    t = cp(act, VK[:, k, 1, c * P:c * P + P], bank.aps[b][:, 0:P])
                    bank.give(b, t)
            tvk = t
            pr = project(8, hparts(XO)) + project(8, hparts(XO))
            for c, (b, t) in enumerate(pr):
                U = uh[:, :, :].rearrange("p a t -> p (a t)")[:, 0:3096]
                A, B = U[:, 0:528], U[:, 528:1056]
                ms(dve, A, 0.0) if c == 0 else None
                if c == 0:
                    ms(dve, B, 0.0)
                own(dve)
                a0 = 8
                s = scr.take(dve)
                s3 = scr.take(dve)
                dve.wait(t)
                cp(dve, A[:, a0:a0 + 512], bank.aps[b])
                t = cp(dve, scr.aps[s], bank.aps[b])
                bank.give(b, t)
                own(dve)
                R = scr.aps[s3]
                tt(dve, B[:, a0:a0 + 513], A[:, a0 - 1:a0 + 512], A[:, a0:a0 + 513], ALU.add)
                own(dve)
                if c == 0:
                    cp(dve, R[0:64, :], B[0:64, a0:a0 + 512])
                    own(dve)
                tt(dve, A[:, a0 - 1:a0 + 514], B[:, a0 - 2:a0 + 513], B[:, a0:a0 + 515], ALU.add)
                own(dve)
                if c == 0:
                    cp(dve, R[64:128, :], A[64:128, a0:a0 + 512])
                else:
                    tt(dve, B[:, a0 - 3:a0 + 516], A[:, a0 - 5:a0 + 514], A[:, a0 - 1:a0 + 518], ALU.add)
                    own(dve)
                    cp(dve, R[0:64, :], B[0:64, a0:a0 + 512])
                    tt(dve, R[64:128, :], B[64:128, a0 - 4:a0 + 508], B[64:128, a0 + 4:a0 + 516], ALU.add)
                own(dve)
                tt(dve, R, R, ICN[:, c, :], ALU.mult)
                own(dve)
                t = tt(dve, R, R, scr.aps[s], ALU.subtract)
                own(dve)
                scr.give(s, t)
                if c == 0:
                    for z in (A, B):
                        ms(dve, z, 0.0)
                    own(dve)
                b = bank.take(pe)
                pe.wait(t)
                t = mm(bank.aps[b], pw[:, c * P:c * P + P], R, True, True, True)
                scr.give(s3, t)
                s = scr.take(dve)
                dve.wait(t)
                t = ts(dve, scr.aps[s], bank.aps[b], pc("pb", 2 * i + c), pc("psc", 2 * i + c), ALU.add, ALU.mult)
                bank.give(b, t)
                put(6 + c, s, t)

            pe.wait(tvk, tkm)
            vn = SM[:, 512:1024]
            b = bank.take(pe)
            for k in range(4):
                t = mm(bank.aps[b][0:1, :], ALT, VK[:, k, 0, :], k == 0, k == 3, k == 3)
            act.wait(t)
            t = cp(act, vn[0:1, :], bank.aps[b][0:1, :])
            bank.give(b, t)
            tvn = t
            ft = []
            for m in range(4):
                bs = []
                u = W.unit()
                for cs in range(2):
                    b = bank.take(pe)
                    for k in range(4):
                        w = u[:, (4 * cs + k) * P:(4 * cs + k + 1) * P]
                        t = mm(bank.aps[b], w, VK[:, k, cs, :], k == 0, k == 3, k == 3)
                    bs.append((b, t))
                W.release(t)
                sv = [scr.take(act), scr.take(act)]
                for cs in range(2):
                    act.wait(bs[cs][1])
                    t = cp(act, scr.aps[sv[cs]][:, 0:256], bank.aps[bs[cs][0]][:, 0:256])
                dve.wait(t, bs[1][1])
                s3 = scr.take(dve)
                kr, ks = bank.aps[bs[0][0]][:, 256:512], bank.aps[bs[1][0]][:, 256:512]
                vr, vs = scr.aps[sv[0]][:, 0:256], scr.aps[sv[1]][:, 0:256]
                t1, t2 = scr.aps[s3][:, 0:256], scr.aps[s3][:, 256:512]
                tt(dve, YF[:, m, :], vr, kr, ALU.mult)
                tt(dve, t1, vs, ks, ALU.mult)
                tt(dve, YF[:, 4 + m, :], vr, ks, ALU.mult)
                t = tt(dve, t2, vs, kr, ALU.mult)
                bank.give(bs[0][0], t)
                bank.give(bs[1][0], t)
                scr.give(sv[0], t)
                scr.give(sv[1], t)
                own(dve)
                tt(dve, YF[:, m, :], YF[:, m, :], t1, ALU.subtract)
                t = tt(dve, YF[:, 4 + m, :], YF[:, 4 + m, :], t2, ALU.add)
                scr.give(s3, t)
                if m == 0:
                    dve.wait(tvn)
                    own(dve)
                    t = tt(dve, YF[0:1, 4, :], vn[0:1, 0:256], vn[0:1, 256:512], ALU.mult)
                ft.append(t)
            hb = [bank.take(pe) for _ in range(2)]
            pe.wait(ft[-1])
            for uu in range(4):
                u = W.unit()
                for q in range(2):
                    m = 2 * uu + q
                    for c in range(2):
                        t = mm(bank.aps[hb[c]], YF[:, m, c * P:c * P + P], u[:, q * 512:q * 512 + 512],
                               m == 0, m == 7, True)
                W.release(t)
            for c in range(2):
                s = scr.take(dve)
                dve.wait(t)
                ty = ts(dve, scr.aps[s], bank.aps[hb[c]], rn[:, c:c + 1], None, ALU.mult)
                bank.give(hb[c], ty)
                own(dve)
                stt(scr.aps[s], vT[:, c, :], pc("hb", 2 * i + c), scr.aps[s], ALU.mult, ALU.add)
                own(dve)
                put(c, s, tt(dve, scr.aps[s], scr.aps[s], x0[:, c, :], ALU.mult))

            la = SM[:, 490:494]
            for z in range(2):
                t = dot(SM[:, 1028:1092], lq[:, 128 * z:128 * z + 64], lq[:, 128 * z + 64:128 * z + 128],
                        la[:, z:z + 1])
                own(dve)
            act.wait(t)
            t = fn(la[:, 0:2], la[:, 0:2], ACT.Exp)
            dve.wait(t)
            stt(la[:, 2:3], la[:, 0:1], -1.0, la[:, 1:2], ALU.mult, ALU.add)
            own(dve)
            nlam = la[:, 3:4]
            ts(dve, nlam, la[:, 2:3], -lam_init, None, ALU.add)
            own(dve)
            subg = SM[:, 494:495]
            ts(dve, subg, pc("sub", i), 1.0 - lam_init, None, ALU.mult)
            own(dve)
            AR = Slots([VK[:, k, c, :] for k in range(4) for c in range(2)])
            PB = Slots([uh.rearrange("p a t -> p (a t)")[:, 512 * k:512 * k + 512] for k in range(6)])
            free = [pe.now(), dve.now(), act.now(), pool.now()]
            for sl in (AR, PB):
                for n in range(len(sl.aps)):
                    sl.give(n, *free)
            mx, nm, ss, rs = (SM[:, 496 + 4 * k:500 + 4 * k] for k in range(4))

            def scores2(h, blk, it):
                res = []
                for c in range(2):
                    b = bank.take(pe)
                    pe.wait(qk[h], qk[4 + h])
                    t = mm(bank.aps[b], qT[64 * c:64 * c + 64, h, blk * P:blk * P + P],
                           kT[64 * c:64 * c + 64, h, :], True, True, True)
                    q = 2 * (it % 2) + c
                    dve.wait(t)
                    rmax(mx[:, q:q + 1], bank.aps[b])
                    own(dve)
                    t = ts(dve, nm[:, q:q + 1], mx[:, q:q + 1], -0.125, None, ALU.mult)
                    p = PB.take(act)
                    act.wait(t)
                    t = fn(PB.aps[p], bank.aps[b], ACT.Exp, bias=nm[:, q:q + 1], scale=0.125, acc=ss[:, q:q + 1])
                    bank.give(b, t)
                    res.append((p, q, t))
                return res

            def mix2(res):
                (p0, q0, t0), (p1, q1, t1) = res
                dve.wait(t0, t1)
                rcp(rs[:, q0:q0 + 2], ss[:, q0:q0 + 2])
                own(dve)
                t = tt(dve, rs[:, q1:q1 + 1], rs[:, q1:q1 + 1], nlam, ALU.mult)
                pool.wait(t)
                t = ts(pool, PB.aps[p1], PB.aps[p1], rs[:, q1:q1 + 1], 1.0, ALU.mult, ALU.mult)
                a = AR.take(dve)
                dve.wait(t)
                t = stt(AR.aps[a], PB.aps[p0], rs[:, q0:q0 + 1], PB.aps[p1], ALU.mult, ALU.add)
                PB.give(p0, t)
                PB.give(p1, t)
                return a, t

            def values2(h, parts_):
                ob = bank.take(pe)
                prev = None
                for j in range(4):
                    b = bank.take(pe)
                    for q in range(4):
                        a, t = parts_[q]
                        pe.wait(t)
                        tx = tr(bank.aps[b][:, q * P:q * P + P], AR.aps[a][:, j * P:j * P + P], inc=q == 3)
                    e = act if j % 2 else dve
                    s = scr.take(e)
                    e.wait(tx)
                    t = cp(e, scr.aps[s], bank.aps[b])
                    bank.give(b, t)
                    if prev is not None:
                        pe.wait(prev[2])
                        t3 = mm(bank.aps[ob], vv[:, prev[0], h * P:h * P + P], scr.aps[prev[1]],
                                prev[0] == 0, False, True)
                        scr.give(prev[1], t3)
                    prev = (j, s, t)
                    fill(FILL2[1])
                for a, _ in parts_:
                    AR.give(a, tx)
                pe.wait(prev[2], *[vtk[(h // 2, z)] for z in range(4)])
                t3 = mm(bank.aps[ob], vv[:, 3, h * P:h * P + P], scr.aps[prev[1]], False, True, True)
                scr.give(prev[1], t3)
                s = scr.take(act)
                act.wait(t3)
                t = cp(act, scr.aps[s], bank.aps[ob])
                bank.give(ob, t)
                s2, r = mean_square(128, [scr.aps[s]], S, EPS5, [t])
                dve.wait(r)
                t = stt(scr.aps[s], scr.aps[s], subg, scr.aps[s2], ALU.mult, ALU.mult)
                scr.give(s2, t)
                put(2 + h, s, t)

            FILL2 = (2, 4)
            work = [(h, b) for h in range(4) for b in range(4)]
            pend, got = [], []
            for it in range(len(work) + 2):
                if it < len(work):
                    h, _ = work[it]
                    if it % 4 == 0:
                        fill(10**9)
                        if h < 3:
                            filler.append(qk_steps(h + 1))
                    pend.append(scores2(*work[it], it))
                    fill(FILL2[0])
                if 1 <= it <= len(work):
                    got.append(mix2(pend[it - 1]))
                if it >= 2 and (it - 2) % 4 == 3:
                    h = (it - 2) // 4
                    values2(h, got[4 * h:4 * h + 4])
            hfree = [pe.now()]

            xt = {}
            LTB = BF[:, 12072:12072 + 128 + 15 * NBLK]
            tcm = constants("c_m", 12072, everyone())
            gather(XO, False)
            for m, r in enumerate(outputs(8, [(S, lambda k: of(YP, k))], lambda k, i_: yt[k], OUT_ORDER)):
                (b, t), = r
                dve.wait(t, *(everyone() if m == 0 else ()))
                xt[(m, 0)] = plus_alpha_h(m, bank.aps[b], b)
                sums[0].feed(XS[0][:, m, :], xt[(m, 0)])
            hk = layer_norm(xt, pc("ln1g", 8 * i, 8), pc("ln1b", 8 * i, 8), [dve.now(), *hfree])

            b = bank.take(pe)
            pe.wait(*twg)
            for k in range(8):
                pe.wait(*hk[(k, 0)])
                t = split_mm(bank.aps[b][0:20, :], [WG[:, z, 20 * k:20 * k + 20] for z in range(2)],
                             of(HS[0], k), k == 0, k == 7, k == 7)
            s = scr.take(act)
            act.wait(t)
            t = cp(act, scr.aps[s][0:20, :], bank.aps[b][0:20, :])
            bank.give(b, t)
            b2 = bank.take(pe)
            pe.wait(t)
            for tl in range(4):
                t = tr(bank.aps[b2][:, 20 * tl:20 * tl + 20], scr.aps[s][0:20, tl * P:tl * P + P], 20)
            scr.give(s, t)
            PT = Pair(16384, 2, S)
            ptk = []
            for z in range(2):
                s = scr.take(act)
                tp = l_cst.start(act, scr.aps[s], io[f"pt{i}"][:, z, :])
                ptk.append(split(scr.aps[s], PT.hi[:, z, :], PT.hf[:, z, :], PT.lo[:, z, :], tp))
                scr.give(s, ptk[-1][1])

            def embed(m):
                (b, t), = project(8, hparts(XO), hready(hk, XO))
                sg = scr.take(act)
                act.wait(t)
                ta = fn(scr.aps[sg], bank.aps[b], ACT.Sigmoid, bias=pc("pleb", 8 * i + m))
                bank.give(b, ta)
                (b, t), = project(2, [(S, lambda k: of(PT, k))], lambda k, i_: ptk[k])
                dve.wait(t, ta)
                t = tt(dve, scr.aps[sg], bank.aps[b], scr.aps[sg], ALU.mult)
                bank.give(b, t)
                own(dve)
                dve.wait(*hk[(m, 0)])
                xt[(m, 0)] = plus_alpha_h(m, scr.aps[sg], None)
                scr.give(sg, xt[(m, 0)])

            LGT = SM[:, 512:592].rearrange("p (a c) -> p a c", a=4)
            dve.wait(t)
            lgp = bank.aps[b2][:, 0:80].rearrange("p (a c) -> p a c", a=4)
            for tl in range(4):
                t = tt(dve, LGT[:, tl, :], lgp[:, tl, :], pc("mb", 20 * i, 20), ALU.add)
            bank.give(b2, t)
            own(dve)

            def region(a, n):
                return SM[:, a + 128:a + 128 + n]

            gmx, oh, gw = region(464, 4), region(468, 16), region(484, 4)
            fs, e16, tmp = region(488, 16), region(504, 16), region(520, 64)
            m1, m2, a1, a2 = region(584, 4), region(588, 4), region(592, 16), region(608, 16)
            GT, w1_, w2_ = region(624, 64), region(688, 4), region(692, 4)
            nf = region(696, 4)
            v4 = lambda z: z.rearrange("p (a c) -> p a c", a=4)

            def first_max(dst, src, mxv):
                rmax(mxv, src)
                own(dve)
                tt(dve, v4(dst), src, mxv.unsqueeze(2).to_broadcast([P, 4, 4]), ALU.is_equal)
                own(dve)
                ts(dve, nf, v4(dst)[:, :, 0], -1.0, 1.0, ALU.mult, ALU.add)
                own(dve)
                for c in range(1, 4):
                    tt(dve, v4(dst)[:, :, c], v4(dst)[:, :, c], nf, ALU.mult)
                    own(dve)
                    if c < 3:
                        tt(dve, nf, nf, v4(dst)[:, :, c], ALU.subtract)
                        own(dve)

            first_max(oh, LGT[:, :, 0:4], gmx)
            tt(dve, v4(e16), LGT[:, :, 0:4], gmx.unsqueeze(2).to_broadcast([P, 4, 4]), ALU.subtract)
            own(dve)
            act.wait(dve.now())
            t = fn(e16, e16, ACT.Exp)
            dve.wait(t)
            rsum(gw, v4(e16))
            own(dve)
            rcp(gw, gw)
            own(dve)
            for g in range(4):
                sel = v4(oh)[:, :, g].unsqueeze(2).to_broadcast([P, 4, 4])
                dst = fs if g == 0 else e16
                tt(dve, v4(dst), LGT[:, :, 4 + 4 * g:8 + 4 * g], sel, ALU.mult)
                own(dve)
                if g:
                    tt(dve, fs, fs, e16, ALU.add)
                    own(dve)
            first_max(a1, v4(fs), m1)
            stt(fs, a1, -1e30, fs, ALU.mult, ALU.add)
            own(dve)
            first_max(a2, v4(fs), m2)
            tt(dve, w2_, m2, m1, ALU.subtract)
            own(dve)
            act.wait(dve.now())
            t = fn(w2_, w2_, ACT.Exp)
            dve.wait(t)
            ts(dve, w1_, w2_, 1.0, None, ALU.add)
            own(dve)
            rcp(w1_, w1_)
            own(dve)
            tt(dve, w1_, w1_, gw, ALU.mult)
            own(dve)
            tt(dve, w2_, w2_, w1_, ALU.mult)
            own(dve)
            M1, M2, CM, Q = (SM[:, c:c + 64] for c in (832, 896, 960, 1024))
            NBL, TOT, Z = SM[:, 512:528], SM[:, 576:592], [SM[:, 528:552], SM[:, 552:576]]
            tl4 = lambda z: z.rearrange("p (a e) -> p a e", a=4)
            for src, dst in ((a1, M1), (a2, M2)):
                for g in range(4):
                    sel = v4(oh)[:, :, g].unsqueeze(2).to_broadcast([P, 4, 4])
                    tt(dve, dst.rearrange("p (a g c) -> p a g c", a=4, g=4)[:, :, g, :], v4(src), sel, ALU.mult)
            own(dve)
            tt(dve, Q, M1, M2, ALU.add)
            ms(dve, CM[:, 0:16], 0.0)
            own(dve)
            for z in range(1, 5):
                dst = CM[:, 16 * z:16 * z + 16] if z < 4 else TOT
                t = tt(dve, dst, CM[:, 16 * z - 16:16 * z], Q[:, 16 * z - 16:16 * z], ALU.add)
                own(dve)
            for m in range(4):
                embed(m)
            b = bank.take(pe)
            pe.wait(t, tcm)
            mm(bank.aps[b][:, 0:64], LTB[:, 0:128], Q, True, False, False)
            mm(bank.aps[b][:, 0:64], MEAN[128][:, :], CM, False, True, False)
            t = mm(bank.aps[b][:, 64:80], MEAN[128][:, :], TOT, True, True, True)
            dve.wait(t, tcm)
            for z in Z:
                ms(dve, z[:, 0:8], 0.0)
            ts(dve, NBL, bank.aps[b][:, 64:80], 0.49609375, MAGIC, ALU.add, ALU.add)
            own(dve)
            ts(dve, Z[0][:, 8:24], NBL, -MAGIC, None, ALU.add)
            own(dve)
            for n, z in enumerate((1, 2, 4, 8)):
                x, y = Z[n % 2], Z[1 - n % 2]
                tt(dve, y[:, 8:24], x[:, 8:24], x[:, 8 - z:24 - z], ALU.add)
                own(dve)
            t = tt(dve, tl4(Q), tl4(bank.aps[b][:, 0:64]), Z[0][:, 7:23].unsqueeze(1).to_broadcast([P, 4, 16]),
                   ALU.add)
            bank.give(b, t)
            own(dve)
            pos = SM[:, 512:520]
            for z, M in enumerate((M1, M2)):
                tt(dve, M, M, Q, ALU.mult)
                own(dve)
                rsum(pos[:, 4 * z:4 * z + 4], tl4(M))
            s = scr.take(dve)
            eq = scr.aps[s][0:1, 0:15 * NBLK].rearrange("p (b e) -> p b e", e=15)
            tt(dve, eq, Z[0][0:1, 8:23].unsqueeze(1).to_broadcast([1, NBLK, 15]),
               LTB[0:1, 128:128 + 15 * NBLK].rearrange("p (b e) -> p b e", e=15), ALU.is_le)
            own(dve)
            tpos = ts(dve, PLACE[:, :], pos, float(P), None, ALU.mult)
            rsum(scr.aps[s][0:1, 400:400 + NBLK], eq)
            own(dve)
            t = ts(dve, EXI[0:1, :], scr.aps[s][0:1, 400:400 + NBLK], float(EU), None, ALU.mult)
            scr.give(s, t)
            W.routing(f"moe{i}", t)

            TOK = BF[:, 2728:6824].rearrange("p (a f) -> p a f", a=4)
            pool.wait(tpos, tzero)
            for tl in range(4):
                for z in range(2):
                    b = bank.take(pe)
                    for q in range(4):
                        k = 4 * z + q
                        o = bank.aps[b][:, q * P:q * P + P]
                        mm(o, HS[0].hi[:, k, tl * P:tl * P + P], IDR[:, :], True, False, False)
                        t = mm(o, HS[0].lo[:, k, tl * P:tl * P + P], IDR[:, :], False, True, q == 3)
                    e = act if z else dve
                    e.wait(t)
                    t = cp(e, TOK[:, tl, 512 * z:512 * z + 512], bank.aps[b])
                    bank.give(b, t)
                    pool.wait(t)
                for z in range(2):
                    tsc = scatter(HD, PLACE[:, 4 * z + tl:4 * z + tl + 1], TOK[:, tl, :])

            XB = Slots([BF[:, 10024 + 1024 * z:11048 + 1024 * z] for z in range(2)])
            XT = Slots([Pair(8192 + 2048 * z, 8, P) for z in range(2)])
            AT = Slots([Pair(12288 + 512 * z, 2, P) for z in range(2)])
            OB = Slots([TOK[:, z, :] for z in range(2)])
            for z in range(2):
                for sl in (XB, XT, AT, OB):
                    sl.give(z, tsc, *everyone())
            loaded, turned_, acted, outs_ = {}, {}, {}, []

            def load_block(n, XB=XB, loaded=loaded, tsc=tsc):
                if n < NBLK:
                    z = XB.take(act)
                    act.wait(tsc)
                    loaded[n] = z, l_xb[z].start(act, XB.aps[z], HD[n * P:n * P + P, :])

            def turn(src, n, pair, need):
                for z in range(0, n, 4):
                    b = bank.take(pe)
                    c = min(n, 4)
                    pe.wait(need)
                    for q in range(c):
                        t = tr(bank.aps[b][:, q * P:q * P + P], src[:, (z + q) * P:(z + q + 1) * P], inc=q == c - 1)
                    v = bank.aps[b][:, 0:c * P].rearrange("p (k t) -> p k t", k=c)
                    act.wait(t)
                    ta = fn(pair.hi[:, z:z + c, :], v, ACT.Copy)
                    dve.wait(ta)
                    td = tt(dve, pair.lo[:, z:z + c, :], v, pair.hf[:, z:z + c, :], ALU.subtract)
                    bank.give(b, td)
                return t, td

            def turn_block(n):
                z, t = loaded[n]
                x = XT.take(act, dve)
                t, td = turn(XB.aps[z], 8, XT.aps[x], t)
                XB.give(z, t)
                turned_[n] = x, td
                load_block(n + 2)

            def way_in(n):
                x, t = turned_[n]
                pe.wait(t)
                b = bank.take(pe)
                for u in range(4):
                    w = W.unit()
                    for z in range(2):
                        k = 2 * u + z
                        t = split_mm(bank.aps[b], of(XT.aps[x], k), [y[:, 512 * z:512 * z + 512] for y in w],
                                     k == 0, k == 7, z == 1)
                    W.release(t)
                XT.give(x, t)
                s = scr.take(act)
                v = scr.aps[s][:, 0:256]
                act.wait(t)
                ta = fn(v, bank.aps[b][:, 0:256], ACT.Silu)
                dve.wait(ta)
                t = tt(dve, v, bank.aps[b][:, 256:512], v, ALU.mult)
                bank.give(b, t)
                acted[n] = s, v, t

            def way_out(n):
                s, v, t = acted[n]
                a = AT.take(act, dve)
                t, td = turn(v, 2, AT.aps[a], t)
                scr.give(s, t)
                if n + 2 < NBLK:
                    turn_block(n + 2)
                bs = [bank.take(pe) for _ in range(2)]
                pe.wait(td)
                for f in range(2):
                    w = W.unit()
                    for z in range(2):
                        t = split_mm(bank.aps[bs[z]], of(AT.aps[a], f), [y[:, 512 * z:512 * z + 512] for y in w],
                                     f == 0, f == 1, z == 1)
                    W.release(t)
                AT.give(a, t)
                o = OB.take(act, dve)
                for z, e in enumerate((act, dve)):
                    e.wait(t)
                    te = cp(e, OB.aps[o][:, 512 * z:512 * z + 512], bank.aps[bs[z]])
                    bank.give(bs[z], te)
                act.wait(te)
                own(act)
                to = l_ob[o].start(act, OD[n * P:n * P + P, :], OB.aps[o])
                OB.give(o, to)
                outs_.append(to)

            embed(4)
            embed(5)
            load_block(0)
            load_block(1)
            embed(6)
            turn_block(0)
            embed(7)
            hfree = [pe.now()]
            turn_block(1)
            if i == 0:
                tok = [constants("c_21", 0, ())]
            way_in(0)
            for n in range(NBLK):
                if n + 1 < NBLK:
                    way_in(n + 1)
                way_out(n)

            bm = bank.take(pe)
            pool.wait(*outs_[-2:], pe.now(), dve.now(), act.now())
            got = []
            for tl in range(4):
                if tl >= 2:
                    pool.wait(*got[tl - 2])
                for z in range(2):
                    g = 2 * (tl % 2) + z
                    t = fetch_rows(g, TOK[:, g, :], PLACE[:, 4 * z + tl:4 * z + tl + 1])
                    e = dve if z else act
                    e.wait(t)
                g1, g2 = TOK[:, 2 * (tl % 2), :], TOK[:, 2 * (tl % 2) + 1, :]
                ta = fn(g1, g1, ACT.Copy, scale=w1_[:, tl:tl + 1])
                dve.wait(ta)
                t = stt(g1, g2, w2_[:, tl:tl + 1], g1, ALU.mult, ALU.add)
                pe.wait(t)
                for z in range(2):
                    b = bank.take(pe)
                    for q in range(4):
                        t = tr(bank.aps[b][:, q * P:q * P + P], g1[:, (4 * z + q) * P:(4 * z + q + 1) * P],
                               inc=q == 3)
                    dve.wait(t, *[xt[(k, 0)] for k in range(8)])
                    x = XS[0][:, 4 * z:4 * z + 4, tl * P:tl * P + P]
                    tx = tt(dve, x, x, bank.aps[b].rearrange("p (k t) -> p k t", k=4), ALU.add)
                    bank.give(b, tx)
                got.append((t, tx))
                if tl:
                    feature_mean(bm, tl - 1, got[tl - 1][1])
            tm = feature_mean(bm, 3, tx)
            sums[0] = Known(bm, tm)
            for k in range(8):
                xt[(k, 0)] = tx
            if i == 0:
                tok.append(constants("c_f1", 6824, everyone()))
            hk = layer_norm(xt, pc("ln2g", 8 * i, 8), pc("ln2b", 8 * i, 8), [dve.now(), *hfree])

        for k in range(8):
            dve.wait(*hk[(k, 0)])
            t = tt(dve, XS[0][:, k, :], HS[0].hf[:, k, :], HS[0].lf[:, k, :], ALU.add)
        act.wait(t)
        finish(XS[0])


def shape_constants():
    f = np.float32
    p = np.arange(P)
    t = np.arange(S)
    c = {"ident": np.eye(P, dtype=f)}
    pos = (t // 64, t % 64)

    def inv(n):
        return (f(10000.0) ** (-np.arange(0, n, 2, dtype=f) / f(n))).astype(f)

    r = p % 64
    i32 = inv(32)
    ang = np.where((r // 32 == 0)[:, None], pos[0][None].astype(f), pos[1][None].astype(f)) * i32[r % 16][:, None]
    sgn = np.where(r % 32 < 16, -1, 1)[:, None]
    q, n = p[:, None], p[None, :]
    left = np.where(n >= q, 0.0, -1e30)
    right = np.where(n <= q, 0.0, -1e30)
    c["c_l0"] = np.concatenate([np.cos(ang), np.sin(ang) * sgn, left, right], 1).astype(f)
    i128 = inv(128)
    a = [pos[m][None].astype(f) * i128[p % 64][:, None] for m in range(2)]
    sg = np.where(p < 64, 1, -1)[:, None]
    w = np.arange(896)[None] - 384 - p[:, None]
    c["c_l1"] = np.concatenate(
        [np.cos(a[0]), np.cos(a[1]), np.sin(a[0]) * sg, np.sin(a[1]) * sg,
         w], 1).astype(f)
    j = r
    iv = np.power(f(500000.0), -np.arange(0, 16, 2, dtype=f) / f(16)).astype(f)
    ang = t[None].astype(f) * np.where(j < 16, iv[j % 8], 0)[:, None].astype(f)
    sgn = np.where(j < 8, -1, 1)[:, None]
    cos = np.where((j < 16)[:, None], np.cos(ang), 1.0)
    sin = np.where((j < 16)[:, None], np.sin(ang) * sgn, 0.0)
    tl = np.linspace(0.0, 1.0, S, dtype=f)[:, None]
    dmax, dmin = math.log(1e-2) / 0.3, math.log(1e-2) / 1.5
    deltas = np.linspace(dmin, dmax, 256, dtype=f)[None]
    win = np.exp(-tl * np.abs(deltas))
    wb = win.copy()
    wb[0] = 0.0
    win2 = np.concatenate([win, wb], 1).reshape(4, P, 512).transpose(1, 0, 2).reshape(P, 2048)
    icn = []
    for m in range(2):
        rows = []
        for g in range(2):
            wn = (2, 4, 8, 16)[2 * m + g]
            lo = np.clip(t - wn // 2, 0, S - 1)
            hi = np.clip(t + wn // 2 - 1, 0, S - 1)
            rows.append(np.repeat((1.0 / (hi - lo + 1))[None], 64, 0))
        icn.append(np.concatenate(rows, 0))
    wpos = (f(2.0 * math.pi) * t[:, None].astype(f) / f(S)).astype(f)
    bands = np.linspace(1e-4, 15, 16, dtype=f)[None]
    z = np.zeros((P, S))
    z[0:33] = np.concatenate([tl, np.cos(wpos * bands), -np.sin(wpos * bands)], 1).T
    alt = np.where(p % 2 == 0, 1.0, -1.0)[:, None]
    c["c_2"] = np.concatenate([cos, sin, *icn, alt, np.zeros((P, 7))], 1).astype(f)
    c["c_f"] = np.concatenate([win2, z], 1).astype(f)
    th = 2 * np.pi * ((np.arange(S)[:, None] * t[None]) % 1024) / 1024
    C, Sn = np.cos(th), np.sin(th)
    blocks = []
    for m in range(4):
        for M in (C, Sn):
            for k in range(4):
                blocks.append(M[k * P:(k + 1) * P, m * P:(m + 1) * P])
    c["dft"] = np.stack(blocks).reshape(4, 8, P, P).transpose(0, 2, 1, 3).reshape(4, P, 1024).astype(f)
    IC, IS = C * (2 / 1024), Sn * (2 / 1024)
    IC[0] = 1 / 1024
    IS[0] = np.where(t % 2 == 0, 1, -1) / 1024
    c["idft"] = np.stack([IC, IS]).reshape(4, 2, P, S).transpose(0, 2, 1, 3).reshape(4, P, 1024).astype(f)
    lower = np.where(p[:, None] < p[None], 1.0 / P, 0.0)
    c["c_m"] = np.concatenate([lower, np.repeat(np.arange(NBLK), 15)[None] + np.zeros((P, 1))], 1).astype(f)
    return {k: np.ascontiguousarray(x) for k, x in c.items()}


def _units(blocks):
    return blocks.reshape(-1, UB, P, P).transpose(0, 2, 1, 3).reshape(-1, P, UB * P)


def _mk(w):
    k, m = w.shape
    return w.reshape(k // P, P, m // P, P).transpose(2, 0, 1, 3).reshape(-1, P, P)


def _out(w, order=None):
    b = _mk(w).reshape(8, -1, P, P)
    if order:
        b = b[:, list(order)]
    return np.concatenate([b[0, :-1], b[1, :-1], b[0, -1:], b[1, -1:], b[2:].reshape(-1, P, P)], 0)


def _km(w):
    k, m = w.shape
    return w.reshape(k // P, P, m // 256, 2, P).transpose(2, 0, 3, 1, 4).reshape(-1, P, P)


def _cols(v):
    return v.reshape(-1, P).T


def _rows(v):
    return np.broadcast_to(v.reshape(1, -1), (P, v.size))


def _top(v):
    o = np.zeros((P, v.shape[1]), v.dtype)
    o[:v.shape[0]] = v
    return o


def layouts(a):
    g = {}
    cat = np.concatenate
    g["xt"] = cat([a[n][0].T.reshape(8, P, -1).transpose(1, 0, 2).reshape(P, -1) for n in ("x", "ctx")], 1)
    cols = {
        "cc": np.stack([_cols(a["c"][0]), _cols(a["c_ctx"])], 2).reshape(P, 16),
        "ada_b": cat([_cols(a["ada_b"][i]) for i in range(2)], 1),
        "n1": _cols(a["norm1_g"]), "n2": _cols(a["norm2_g"]),
        "qn": np.tile(a["attn_q_norm"][0], 2)[:, None], "kn": np.tile(a["attn_k_norm"][0], 2)[:, None],
        "sink": _rows(a["attn_sink"][0]), "dl": _rows(a["ret_decay_logit"][0]),
        "gn": _cols(a["ret_gn_g"][0]),
        "ln0g": _cols(a["ln0_g_2"]), "ln0b": _cols(a["ln0_b_2"]),
        "ln1g": _cols(a["ln1_g_2"]), "ln1b": _cols(a["ln1_b_2"]),
        "ln2g": _cols(a["ln2_g_2"]), "ln2b": _cols(a["ln2_b_2"]),
        "cw": _cols(a["hy_conv_w_2"]), "cb": _cols(a["hy_conv_b_2"]), "hb": _cols(a["hy_bias_2"]),
        "fr1": _top(a["hy_freq1_2"].T), "fb1": _top(a["hy_fb1_2"].T),
        "fr2": _top(a["hy_freq2_2"].T), "fb2": _top(a["hy_fb2_2"].T),
        "sub": a["att_subln_g_2"].T,
        "pb": _cols(a["pool_b_2"]), "psc": _cols(a["pool_scale_2"]), "pleb": _cols(a["ple_bg_2"]),
        "mb": cat([_rows(a[n][i]) for i in range(2) for n in ("moe_bgc_2", "moe_bgf_2")], 1),
    }
    prm = np.zeros((P, NPRM), np.float32)
    for n, (at, w) in PCOLS.items():
        prm[:, at:at + w] = cols[n]
    g["prm"] = prm
    qkv = a["attn_w_qkv"][0]
    wo = a["attn_w_o"][0]
    g["att"] = _units(cat([_mk(qkv[:, 1024:1280]), _km(qkv[:, 1280:1536]), _mk(qkv[:, 0:768]), _mk(wo[0:256]),
                           _mk(qkv[:, 768:1024]), *[_mk(wo[256 * g_:256 * g_ + 256]) for g_ in (1, 2, 3)]], 0))
    r, wo = a["ret_w_qkvg"][0], a["ret_w_o"][0]
    g["ret"] = _units(cat([b for h in range(4) for b in (
        _mk(r[:, 256 * h:256 * h + 256]), _mk(r[:, 1024 + 256 * h:1280 + 256 * h]),
        _km(r[:, 2048 + 512 * h:2560 + 512 * h]), _mk(r[:, 4096 + 512 * h:4608 + 512 * h]),
        _out(wo[512 * h:512 * h + 512]))], 0))
    wgs = [cat([a["moe_wgc_2"][i], a["moe_wgf_2"][i]], 1).reshape(8, P, 20) for i in range(2)]
    pws = np.zeros((2, 2, 2, 64, 2, 64), np.float32)
    for h in range(2):
        pws[:, :, h, :, h, :] = a["pool_w_2"].reshape(2, 2, 2, 64, 64)[:, :, h]
    c2 = shape_constants()
    for i in range(2):
        g[f"ada{i}"] = a["ada_w"][i].reshape(4, 2, P, 12, 512).transpose(3, 0, 2, 1, 4).reshape(48, P, 1024)
        w = a["ffn_w_in"][i].reshape(D, 2, NF, P).transpose(0, 2, 1, 3).reshape(D, 2 * DFF)
        f0, blocks = 0, []
        for nf in CHUNKS:
            blocks += [_mk(w[:, 2 * P * f0:2 * P * (f0 + nf)]), _out(a["ffn_w_out"][i][P * f0:P * (f0 + nf)])]
            f0 += nf
        g[f"ff{i}"] = _units(cat(blocks, 0))
        w = a["w_in_2"][i]
        qk = [w[:, a_ + P * h:a_ + P * h + P] for h in range(4) for a_ in (768, 1280)]
        g[f"win{i}"] = _units(cat([_mk(w[:, 0:768]), *[_mk(z) for z in qk[0:2]], _km(w[:, 1792:2304]),
                                   _mk(w[:, 2304:2560])], 0))
        g[f"wqk{i}"] = _units(cat([_mk(z) for z in qk[2:]], 0))
        g[f"wout{i}"] = _units(_out(a["w_out_2"][i], OUT_ORDER))
        wg_, wp = _mk(a["ple_wg_2"][i]).reshape(8, 8, P, P), _mk(a["ple_wp_2"][i]).reshape(8, 2, P, P)
        g[f"ple{i}"] = _units(cat([wg_, wp], 1).reshape(-1, P, P))
        w = cat([a["moe_w1_2"][i], a["moe_w3_2"][i]], 2).reshape(16, 4, 2, P, 512).transpose(0, 1, 3, 2, 4)
        g[f"moe{i}"] = cat([w.reshape(16, 4, P, 1024), a["moe_w2_2"][i].reshape(16, 2, P, 1024)], 1).reshape(
            16 * EU, P, 1024)
        g[f"pt{i}"] = a["p_2"][i, 0].T.reshape(2, P, S).transpose(1, 0, 2)
        g[f"c_2{i}"] = cat([c2["c_2"], pws[i].reshape(2, P, P).transpose(1, 0, 2).reshape(P, 256),
                            *[_rows(a[n][i]) for n in ("att_lq1_2", "att_lk1_2", "att_lq2_2", "att_lk2_2")],
                            wgs[i].transpose(1, 0, 2).reshape(P, 160)], 1)
        g[f"c_f{i}"] = cat([c2["c_f"], _top(a["hy_fw1_2"][i]), _top(a["hy_fw2_2"][i]), _top(a["hy_fw3_2"][i])], 1)
    g.update({k: v for k, v in c2.items() if k not in ("c_2", "c_f")})
    return {k: np.ascontiguousarray(v) for k, v in g.items()}


def kernel(**inputs):
    import numpy as _np
    import concourse.bacc as _bacc
    from concourse.bass_utils import run_bass_kernel_spmd as _run

    a = {k: _np.asarray(v) for k, v in inputs.items()}
    nc = _bacc.Bacc("TRN2", target_bir_lowering=False, num_devices=1)
    arrays, io = {}, {}
    for name, v in layouts(a).items():
        arrays[f"in_{name}"] = v
        io[name] = nc.dram_tensor(f"in_{name}", v.shape, mybir.dt.from_np(v.dtype), kind="ExternalInput").ap()
    out = nc.dram_tensor("out_0", (P, 8, S), F32, kind="ExternalOutput").ap()
    build(nc, io, out)
    r = _run(nc, [arrays], core_ids=[0])
    got = r.results[0]["out_0"]
    return got.transpose(2, 1, 0).reshape(1, S, D)
```
